# Optimizing a Trainium2 kernel written in Bass

```python
import math
import jax, jax.numpy as jnp
from jax import lax
import numpy as np

D_MODEL = 2048
BATCH = 1
SEQ = 256
DEPTH = 1

CHUNK = 64
D_MIX = D_MODEL
NORM_EPS = 1e-6
DSA_WIDTH = D_MIX // 2
DSA_HEAD_DIM = 128
DSA_HEADS = DSA_WIDTH // DSA_HEAD_DIM
IDX_HEADS = 16
IDX_DIM = 64
TOPK_MAX = 256
ROPE_THETA = 10000.0
RWKV_WIDTH = D_MIX - DSA_WIDTH
RWKV_HEAD_DIM = 64
RWKV_HEADS = RWKV_WIDTH // RWKV_HEAD_DIM
DECAY_LORA = 64
AICL_LORA = 64
GATE_LORA = 160
GN_EPS = 64e-5
N_GROUPS = 4
EXPERTS_PER_GROUP = 4
N_EXPERTS = N_GROUPS * EXPERTS_PER_GROUP
TOP_K_IN_GROUP = 2
D_EXPERT = 512
DSA_SPLITS = (DSA_WIDTH, DSA_WIDTH, DSA_WIDTH, IDX_HEADS * IDX_DIM, IDX_DIM, IDX_HEADS)
RWKV_SPLITS = (RWKV_WIDTH, DECAY_LORA, RWKV_WIDTH, RWKV_WIDTH, AICL_LORA, GATE_LORA)
DSA_COLS = sum(DSA_SPLITS)
RWKV_COLS = sum(RWKV_SPLITS)
IN_COLS = DSA_COLS + RWKV_COLS


def split_cols(p, sizes):
    cuts = np.cumsum(sizes)[:-1].tolist()
    return jnp.split(p, cuts, axis=-1)

def rms_norm(x, g, eps=NORM_EPS):
    xf = x.astype(jnp.float32)
    y = xf * lax.rsqrt(jnp.mean(xf * xf, axis=-1, keepdims=True) + eps)
    return (y * g.astype(jnp.float32)).astype(x.dtype)

def rope(x, pos):
    d = x.shape[-1]
    half = d // 2
    inv = ROPE_THETA ** (-jnp.arange(half, dtype=jnp.float32) * (2.0 / d))
    ang = pos.astype(jnp.float32)[:, None] * inv[None, :]
    cos = jnp.cos(ang)[None, :, None, :]
    sin = jnp.sin(ang)[None, :, None, :]
    xf = x.astype(jnp.float32)
    x1, x2 = xf[..., :half], xf[..., half:]
    out = jnp.concatenate([x1 * cos - x2 * sin, x2 * cos + x1 * sin], axis=-1)
    return out.astype(x.dtype)

def token_shift_mix(p, mu):
    prev = jnp.pad(p, ((0, 0), (1, 0), (0, 0)))[:, :-1]
    return p + (prev - p) * mu

def dsa_mixer(q, k, v, q_idx, k_idx, w_idx, q_gain, k_gain):
    B, S = q.shape[0], q.shape[1]
    f32 = jnp.float32
    pos = jnp.arange(S)
    q = rope(rms_norm(q.reshape(B, S, DSA_HEADS, DSA_HEAD_DIM), q_gain), pos)
    k = rope(rms_norm(k.reshape(B, S, DSA_HEADS, DSA_HEAD_DIM), k_gain), pos)
    v = v.reshape(B, S, DSA_HEADS, DSA_HEAD_DIM)
    q_idx = rope(q_idx.reshape(B, S, IDX_HEADS, IDX_DIM), pos)
    k_idx = rope(k_idx[:, :, None, :], pos)[:, :, 0]
    w_idx = w_idx.astype(f32) * (IDX_HEADS ** -0.5 * IDX_DIM ** -0.5)
    top_k = min(TOPK_MAX, S // 4)
    n_blocks = S // CHUNK
    key_pos = jnp.arange(S)
    scale = DSA_HEAD_DIM ** -0.5

    def block(i):
        start = i * CHUNK
        qi_idx = lax.dynamic_slice_in_dim(q_idx, start, CHUNK, axis=1)
        wi = lax.dynamic_slice_in_dim(w_idx, start, CHUNK, axis=1)
        qi = lax.dynamic_slice_in_dim(q, start, CHUNK, axis=1)
        iscore = jnp.einsum('bqhd,bsd->bqhs', qi_idx, k_idx, preferred_element_type=f32)
        iscore = jnp.einsum('bqhs,bqh->bqs', jax.nn.relu(iscore), wi)
        admissible = key_pos < start + CHUNK
        iscore = jnp.where(admissible[None, None, :], iscore, -jnp.inf)
        sel_score, sel = lax.top_k(iscore, top_k)
        valid = jnp.isfinite(sel_score)
        k_sel = jax.vmap(lambda kb, ib: kb[ib])(k, sel)
        v_sel = jax.vmap(lambda vb, ib: vb[ib])(v, sel)
        logits = jnp.einsum('bqhd,bqkhd->bhqk', qi, k_sel, preferred_element_type=f32) * scale
        logits = jnp.where(valid[:, None, :, :], logits, -jnp.inf)
        probs = jax.nn.softmax(logits, axis=-1)
        return jnp.einsum('bhqk,bqkhd->bqhd', probs.astype(v.dtype), v_sel)

    out = lax.map(block, jnp.arange(n_blocks))
    return out.transpose(1, 0, 2, 3, 4).reshape(B, S, DSA_WIDTH)

def rwkv7_mixer(r, d_w, k, v, d_a, d_g, w0, w_decay_up, a0, w_aicl_up, w_gate_lora_up,
                k_k, k_a, r_k, ln_x_w, ln_x_b, out_dtype):
    B, S = r.shape[0], r.shape[1]
    H, N = RWKV_HEADS, RWKV_HEAD_DIM
    f32 = jnp.float32
    w = -jax.nn.softplus(-(w0 + jnp.tanh(d_w) @ w_decay_up)) - 0.5
    decay = jnp.exp(-jnp.exp(w.astype(f32)))
    a = jax.nn.sigmoid((a0 + d_a @ w_aicl_up).astype(f32))
    g = (jax.nn.sigmoid(d_g) @ w_gate_lora_up).astype(f32)
    heads = lambda t: t.astype(f32).reshape(B, S, H, N)
    kk = heads(k * k_k)
    kk = kk / jnp.maximum(jnp.sqrt(jnp.sum(kk * kk, axis=-1, keepdims=True)), 1e-12)
    k = k.astype(f32) * (1.0 + (a - 1.0) * k_a.astype(f32))
    r_h, k_h, v_h, w_h, a_h = heads(r), heads(k), heads(v), heads(decay), heads(a)
    b_h = kk * a_h

    def step(state, inp):
        r_t, w_t, k_t, v_t, kk_t, b_t = inp
        sa = jnp.einsum('bhvk,bhk->bhv', state, -kk_t)
        state = (state * w_t[:, :, None, :] + sa[..., None] * b_t[:, :, None, :]
                 + v_t[..., None] * k_t[:, :, None, :])
        return state, jnp.einsum('bhvk,bhk->bhv', state, r_t)

    xs = tuple(t.transpose(1, 0, 2, 3) for t in (r_h, w_h, k_h, v_h, kk, b_h))
    _, ys = lax.scan(step, jnp.zeros((B, H, N, N), f32), xs)
    y = ys.transpose(1, 0, 2, 3)
    mu = jnp.mean(y, axis=-1, keepdims=True)
    var = jnp.mean(jnp.square(y - mu), axis=-1, keepdims=True)
    y = ((y - mu) * lax.rsqrt(var + GN_EPS)).reshape(B, S, RWKV_WIDTH)
    y = y * ln_x_w.astype(f32) + ln_x_b.astype(f32)
    bonus = jnp.sum(r_h * k_h * r_k.astype(f32), axis=-1, keepdims=True) * v_h
    y = (y + bonus.reshape(B, S, RWKV_WIDTH)) * g
    return y.astype(out_dtype)

def hier_moe(h, w_route_group, b_route_group, w_route_expert, b_route_expert,
             w_e_gate, w_e_up, w_e_down):
    B, S, D = h.shape
    f32 = jnp.float32
    t = h.reshape(B * S, D)
    grp_prob = jax.nn.softmax((t @ w_route_group).astype(f32) + b_route_group.astype(f32), axis=-1)
    p_grp, g_sel = lax.top_k(grp_prob, 1)
    exp_logits = ((t @ w_route_expert).astype(f32) + b_route_expert.astype(f32))
    exp_logits = exp_logits.reshape(-1, N_GROUPS, EXPERTS_PER_GROUP)
    exp_logits = jnp.take_along_axis(exp_logits, g_sel[:, :, None], axis=1)[:, 0]
    p_exp, e_sel = lax.top_k(jax.nn.softmax(exp_logits, axis=-1), TOP_K_IN_GROUP)
    p_exp = p_exp / jnp.sum(p_exp, axis=-1, keepdims=True)
    gate_w = p_grp * p_exp
    expert_id = g_sel * EXPERTS_PER_GROUP + e_sel
    combine = jnp.sum(jax.nn.one_hot(expert_id, N_EXPERTS, dtype=f32) * gate_w[..., None], axis=1)
    y = jnp.zeros((B * S, D), f32)
    for e in range(N_EXPERTS):
        he = jax.nn.silu(t @ w_e_gate[e]) * (t @ w_e_up[e])
        y = y + combine[:, e:e + 1] * (he @ w_e_down[e]).astype(f32)
    return y.reshape(B, S, D).astype(h.dtype)

def first_inputs(seed: int = 0) -> dict:
    key = jax.random.key(seed)
    ks = jax.random.split(key, 32)
    f32 = jnp.float32
    nrm = lambda k, shape, s: jax.random.normal(k, shape, f32) * s
    L, D = DEPTH, D_MODEL
    return {
        'x': jax.random.normal(ks[0], (BATCH, SEQ, D), f32),
        'g_mix': 1.0 + nrm(ks[1], (L, D), 0.02),
        'w_in': nrm(ks[2], (L, D, IN_COLS), D ** -0.5),
        'rwkv_shift_mix': jax.random.uniform(ks[3], (L, RWKV_COLS), f32),
        'q_gain': 1.0 + nrm(ks[4], (L, DSA_HEAD_DIM), 0.02),
        'k_gain': 1.0 + nrm(ks[5], (L, DSA_HEAD_DIM), 0.02),
        'w0': jax.random.uniform(ks[6], (L, RWKV_WIDTH), f32, -6.0, -1.0),
        'w_decay_up': nrm(ks[7], (L, DECAY_LORA, RWKV_WIDTH), 0.1),
        'a0': nrm(ks[8], (L, RWKV_WIDTH), 0.1),
        'w_aicl_up': nrm(ks[9], (L, AICL_LORA, RWKV_WIDTH), 0.5 * AICL_LORA ** -0.5),
        'w_gate_lora_up': nrm(ks[10], (L, GATE_LORA, RWKV_WIDTH), GATE_LORA ** -0.5),
        'k_k': 0.85 + nrm(ks[11], (L, RWKV_WIDTH), 0.02),
        'k_a': 1.0 + nrm(ks[12], (L, RWKV_WIDTH), 0.02),
        'r_k': nrm(ks[13], (L, RWKV_HEADS, RWKV_HEAD_DIM), 0.1),
        'ln_x_w': 1.0 + nrm(ks[14], (L, RWKV_WIDTH), 0.02),
        'ln_x_b': nrm(ks[15], (L, RWKV_WIDTH), 0.01),
        'w_out': nrm(ks[16], (L, D_MIX, D), D_MIX ** -0.5),
        'g_ffn': 1.0 + nrm(ks[17], (L, D), 0.02),
        'w_route_group': nrm(ks[18], (L, D, N_GROUPS), D ** -0.5),
        'b_route_group': nrm(ks[19], (L, N_GROUPS), 0.01),
        'w_route_expert': nrm(ks[20], (L, D, N_EXPERTS), D ** -0.5),
        'b_route_expert': nrm(ks[21], (L, N_EXPERTS), 0.01),
        'w_e_gate': nrm(ks[22], (L, N_EXPERTS, D, D_EXPERT), D ** -0.5),
        'w_e_up': nrm(ks[23], (L, N_EXPERTS, D, D_EXPERT), D ** -0.5),
        'w_e_down': nrm(ks[24], (L, N_EXPERTS, D_EXPERT, D), D_EXPERT ** -0.5),
    }

def first_block(x, g_mix, w_in, rwkv_shift_mix, q_gain, k_gain, w0, w_decay_up, a0, w_aicl_up,
              w_gate_lora_up, k_k, k_a, r_k, ln_x_w, ln_x_b, w_out, g_ffn, w_route_group,
              b_route_group, w_route_expert, b_route_expert, w_e_gate, w_e_up, w_e_down):
    for l in range(DEPTH):
        h = rms_norm(x, g_mix[l])
        proj = h @ w_in[l]
        p_dsa, p_rwkv = proj[..., :DSA_COLS], proj[..., DSA_COLS:]
        q, k, v, q_idx, k_idx, w_idx = split_cols(p_dsa, DSA_SPLITS)
        y_dsa = dsa_mixer(q, k, v, q_idx, k_idx, w_idx, q_gain[l], k_gain[l])
        p_rwkv = token_shift_mix(p_rwkv, rwkv_shift_mix[l])
        r, d_w, kr, vr, d_a, d_g = split_cols(p_rwkv, RWKV_SPLITS)
        y_rwkv = rwkv7_mixer(r, d_w, kr, vr, d_a, d_g, w0[l], w_decay_up[l], a0[l], w_aicl_up[l],
                             w_gate_lora_up[l], k_k[l], k_a[l], r_k[l], ln_x_w[l], ln_x_b[l],
                             x.dtype)
        x = x + jnp.concatenate([y_dsa.astype(x.dtype), y_rwkv], axis=-1) @ w_out[l]
        x = x + hier_moe(rms_norm(x, g_ffn[l]), w_route_group[l], b_route_group[l],
                         w_route_expert[l], b_route_expert[l], w_e_gate[l], w_e_up[l],
                         w_e_down[l])
    return x


MIX_WIDTH = D_MODEL // 2
N_BRANCHES = 3
EPS = 1e-6
CHUNK_2 = 128
GM_WIDTH = MIX_WIDTH
GM_GROUP_CH = 128
GM_GROUPS = GM_WIDTH // GM_GROUP_CH
S5_WIDTH = MIX_WIDTH
S5_GROUP_CH = 16
S5_GROUPS = S5_WIDTH // S5_GROUP_CH
S5_STATE = 64
DT_MIN = 1e-3
DT_MAX = 1e-1
SB_WIDTH = MIX_WIDTH
SB_HEAD_DIM = 128
SB_HEADS = SB_WIDTH // SB_HEAD_DIM
SB_BLOCK = 128
PROJ_COLS = 2 * GM_WIDTH + S5_WIDTH + 3 * SB_WIDTH + N_BRANCHES * D_MODEL
D_FF = 4 * D_MODEL


def rmsnorm(x, g):
    xf = x.astype(jnp.float32)
    y = xf * lax.rsqrt(jnp.mean(xf * xf, axis=-1, keepdims=True) + EPS)
    return (y * g.astype(jnp.float32)).astype(x.dtype)

def gmlp_mixer(uv, norm_g, w_s, b_s):
    bsz, seq, _ = uv.shape
    z = jax.nn.gelu(uv)
    u, v = jnp.split(z, 2, axis=-1)
    v = rmsnorm(v, norm_g)
    v = v.reshape(bsz, seq // CHUNK_2, CHUNK_2, GM_GROUPS, GM_GROUP_CH)
    w = jnp.tril(w_s)
    mixed = jnp.einsum('gts,bcsgh->bctgh', w, v) + jnp.transpose(b_s)[None, None, :, :, None]
    return u * mixed.reshape(bsz, seq, GM_WIDTH)

def s5_mixer(xin, lam_re, lam_im, log_dt, b_re, b_im, c_re, c_im, d, w_glu, b_glu):
    f32 = jnp.float32
    bsz, seq, _ = xin.shape
    u = xin.astype(f32).reshape(bsz, seq, S5_GROUPS, S5_GROUP_CH)
    lam_re = lam_re.astype(f32)
    lam_im = lam_im.astype(f32)
    b_re = b_re.astype(f32)
    b_im = b_im.astype(f32)
    dt = jnp.exp(log_dt.astype(f32))[:, None]
    mag = jnp.exp(lam_re * dt)
    ab_re = mag * jnp.cos(lam_im * dt)
    ab_im = mag * jnp.sin(lam_im * dt)
    den = lam_re * lam_re + lam_im * lam_im
    n_re = ab_re - 1.0
    n_im = ab_im
    k_re = (n_re * lam_re + n_im * lam_im) / den
    k_im = (n_im * lam_re - n_re * lam_im) / den
    bb_re = k_re[..., None] * b_re - k_im[..., None] * b_im
    bb_im = k_re[..., None] * b_im + k_im[..., None] * b_re
    bu_re = jnp.einsum('blgh,gph->blgp', u, bb_re)
    bu_im = jnp.einsum('blgh,gph->blgp', u, bb_im)
    a_re = jnp.broadcast_to(ab_re, bu_re.shape)
    a_im = jnp.broadcast_to(ab_im, bu_im.shape)

    def combine(e_i, e_j):
        ar_i, ai_i, br_i, bi_i = e_i
        ar_j, ai_j, br_j, bi_j = e_j
        return (ar_j * ar_i - ai_j * ai_i,
                ar_j * ai_i + ai_j * ar_i,
                ar_j * br_i - ai_j * bi_i + br_j,
                ar_j * bi_i + ai_j * br_i + bi_j)

    _, _, s_re, s_im = lax.associative_scan(combine, (a_re, a_im, bu_re, bu_im), axis=1)
    y = (jnp.einsum('blgp,ghp->blgh', s_re, c_re.astype(f32))
         - jnp.einsum('blgp,ghp->blgh', s_im, c_im.astype(f32)))
    y = y.reshape(bsz, seq, S5_WIDTH) + d.astype(f32) * xin.astype(f32)
    g = jax.nn.gelu(y)
    out = g * jax.nn.sigmoid(g @ w_glu.astype(f32) + b_glu.astype(f32))
    return out.astype(xin.dtype)

def stick_breaking_attention(q, k, v):
    f32 = jnp.float32
    seq = q.shape[2]
    scale = SB_HEAD_DIM ** -0.5
    outs = []
    for blk in range(seq // SB_BLOCK):
        t0 = blk * SB_BLOCK
        t1 = t0 + SB_BLOCK
        qb = q[:, :, t0:t1].astype(f32)
        kb = k[:, :, :t1].astype(f32)
        vb = v[:, :, :t1].astype(f32)
        z = jnp.einsum('bhtd,bhsd->bhts', qb, kb) * scale
        mask = jnp.arange(t1)[None, :] < jnp.arange(t0, t1)[:, None]
        log_1m = jnp.where(mask, jax.nn.log_sigmoid(-z), 0.0)
        after = lax.cumsum(log_1m, axis=3, reverse=True) - log_1m
        w = jnp.where(mask, jnp.exp(jax.nn.log_sigmoid(z) + after), 0.0)
        outs.append(jnp.einsum('bhts,bhsd->bhtd', w, vb))
    return jnp.concatenate(outs, axis=2).astype(q.dtype)

def second_inputs(seed: int = 0) -> dict:
    key = jax.random.key(seed)
    ks = jax.random.split(key, 32)

    def nrm(k, shape, scale):
        return jax.random.normal(k, shape, jnp.float32) * scale

    x = nrm(ks[0], (BATCH, SEQ, D_MODEL), 1.0)
    norm1_g = 1.0 + nrm(ks[1], (DEPTH, D_MODEL), 0.05)
    w_in = nrm(ks[2], (DEPTH, D_MODEL, PROJ_COLS), D_MODEL ** -0.5)
    b_gate = nrm(ks[3], (DEPTH, N_BRANCHES, D_MODEL), 0.1)
    gm_norm_g = 1.0 + nrm(ks[4], (DEPTH, GM_WIDTH), 0.05)
    gm_w_s = nrm(ks[5], (DEPTH, GM_GROUPS, CHUNK_2, CHUNK_2), CHUNK_2 ** -0.5)
    gm_b_s = 1.0 + nrm(ks[6], (DEPTH, GM_GROUPS, CHUNK_2), 0.1)
    s5_lambda_re = -0.5 + nrm(ks[7], (DEPTH, S5_GROUPS, S5_STATE), 0.01)
    s5_lambda_im = (math.pi * jnp.arange(S5_STATE, dtype=jnp.float32))[None, None, :] \
        + nrm(ks[8], (DEPTH, S5_GROUPS, S5_STATE), 0.01)
    s5_log_dt = jax.random.uniform(ks[9], (DEPTH, S5_GROUPS), jnp.float32,
                                   math.log(DT_MIN), math.log(DT_MAX))
    s5_b_re = nrm(ks[10], (DEPTH, S5_GROUPS, S5_STATE, S5_GROUP_CH), (2 * S5_GROUP_CH) ** -0.5)
    s5_b_im = nrm(ks[11], (DEPTH, S5_GROUPS, S5_STATE, S5_GROUP_CH), (2 * S5_GROUP_CH) ** -0.5)
    s5_c_re = nrm(ks[12], (DEPTH, S5_GROUPS, S5_GROUP_CH, S5_STATE), (2 * S5_STATE) ** -0.5)
    s5_c_im = nrm(ks[13], (DEPTH, S5_GROUPS, S5_GROUP_CH, S5_STATE), (2 * S5_STATE) ** -0.5)
    s5_d = nrm(ks[14], (DEPTH, S5_WIDTH), 1.0)
    s5_w_glu = nrm(ks[15], (DEPTH, S5_WIDTH, S5_WIDTH), S5_WIDTH ** -0.5)
    s5_b_glu = nrm(ks[16], (DEPTH, S5_WIDTH), 0.02)
    w_branch = nrm(ks[17], (DEPTH, N_BRANCHES, MIX_WIDTH, D_MODEL), MIX_WIDTH ** -0.5)
    w_out = nrm(ks[18], (DEPTH, D_MODEL, D_MODEL), D_MODEL ** -0.5)
    norm2_g = 1.0 + nrm(ks[19], (DEPTH, D_MODEL), 0.05)
    w_mlp_in = nrm(ks[20], (DEPTH, D_MODEL, D_FF), D_MODEL ** -0.5)
    w_mlp_out = nrm(ks[21], (DEPTH, D_FF, D_MODEL), D_FF ** -0.5)
    final_g = 1.0 + nrm(ks[22], (D_MODEL,), 0.05)
    return {"x": x, "norm1_g": norm1_g, "w_in": w_in, "b_gate": b_gate,
            "gm_norm_g": gm_norm_g, "gm_w_s": gm_w_s, "gm_b_s": gm_b_s,
            "s5_lambda_re": s5_lambda_re, "s5_lambda_im": s5_lambda_im, "s5_log_dt": s5_log_dt,
            "s5_b_re": s5_b_re, "s5_b_im": s5_b_im, "s5_c_re": s5_c_re, "s5_c_im": s5_c_im,
            "s5_d": s5_d, "s5_w_glu": s5_w_glu, "s5_b_glu": s5_b_glu,
            "w_branch": w_branch, "w_out": w_out, "norm2_g": norm2_g,
            "w_mlp_in": w_mlp_in, "w_mlp_out": w_mlp_out, "final_g": final_g}

def second_block(x, norm1_g, w_in, b_gate, gm_norm_g, gm_w_s, gm_b_s,
              s5_lambda_re, s5_lambda_im, s5_log_dt, s5_b_re, s5_b_im, s5_c_re, s5_c_im,
              s5_d, s5_w_glu, s5_b_glu, w_branch, w_out, norm2_g,
              w_mlp_in, w_mlp_out, final_g):
    bsz, seq, _ = x.shape
    o_a = 2 * GM_WIDTH
    o_b = o_a + S5_WIDTH
    o_c = o_b + 3 * SB_WIDTH
    for l in range(DEPTH):
        h = rmsnorm(x, norm1_g[l])
        proj = h @ w_in[l]
        uv = proj[..., :o_a]
        s5_in = proj[..., o_a:o_b]
        qkv = proj[..., o_b:o_c].reshape(bsz, seq, 3, SB_HEADS, SB_HEAD_DIM)
        qkv = jnp.transpose(qkv, (2, 0, 3, 1, 4))
        gates = jax.nn.sigmoid(proj[..., o_c:].reshape(bsz, seq, N_BRANCHES, D_MODEL) + b_gate[l])

        y_a = gmlp_mixer(uv, gm_norm_g[l], gm_w_s[l], gm_b_s[l])
        y_b = s5_mixer(s5_in, s5_lambda_re[l], s5_lambda_im[l], s5_log_dt[l],
                       s5_b_re[l], s5_b_im[l], s5_c_re[l], s5_c_im[l],
                       s5_d[l], s5_w_glu[l], s5_b_glu[l])
        y_c = stick_breaking_attention(qkv[0], qkv[1], qkv[2])
        y_c = jnp.transpose(y_c, (0, 2, 1, 3)).reshape(bsz, seq, SB_WIDTH)

        ys = jnp.stack([y_a, y_b, y_c], axis=2)
        br = jnp.einsum('blnw,nwd->blnd', ys, w_branch[l])
        merged = jnp.sum(gates * br, axis=2)
        x = x + merged @ w_out[l]
        h2 = rmsnorm(x, norm2_g[l])
        x = x + jnp.square(jax.nn.relu(h2 @ w_mlp_in[l])) @ w_mlp_out[l]
    return rmsnorm(x, final_g)


def setup_inputs(seed=0):
    out = dict(first_inputs(seed))
    for name, value in second_inputs(seed + 1).items():
        if name != "x":
            out[name + "_2"] = value
    return out


def reference(
    x, g_mix, w_in, rwkv_shift_mix, q_gain, k_gain, w0, w_decay_up, a0, w_aicl_up,
    w_gate_lora_up, k_k, k_a, r_k, ln_x_w, ln_x_b, w_out, g_ffn, w_route_group, b_route_group,
    w_route_expert, b_route_expert, w_e_gate, w_e_up, w_e_down, norm1_g_2, w_in_2, b_gate_2,
    gm_norm_g_2, gm_w_s_2, gm_b_s_2, s5_lambda_re_2, s5_lambda_im_2, s5_log_dt_2, s5_b_re_2,
    s5_b_im_2, s5_c_re_2, s5_c_im_2, s5_d_2, s5_w_glu_2, s5_b_glu_2, w_branch_2, w_out_2,
    norm2_g_2, w_mlp_in_2, w_mlp_out_2, final_g_2,
):
    x = first_block(
        x, g_mix, w_in, rwkv_shift_mix, q_gain, k_gain, w0, w_decay_up, a0, w_aicl_up,
        w_gate_lora_up, k_k, k_a, r_k, ln_x_w, ln_x_b, w_out, g_ffn, w_route_group,
        b_route_group, w_route_expert, b_route_expert, w_e_gate, w_e_up, w_e_down,
    )
    return second_block(
        x, norm1_g_2, w_in_2, b_gate_2, gm_norm_g_2, gm_w_s_2, gm_b_s_2, s5_lambda_re_2,
        s5_lambda_im_2, s5_log_dt_2, s5_b_re_2, s5_b_im_2, s5_c_re_2, s5_c_im_2, s5_d_2,
        s5_w_glu_2, s5_b_glu_2, w_branch_2, w_out_2, norm2_g_2, w_mlp_in_2, w_mlp_out_2,
        final_g_2,
    )


_drawn_inputs = setup_inputs


def setup_inputs(seed=0):
    import zlib

    import numpy as np

    out = dict(_drawn_inputs(seed))
    spreads = {}
    factors = {'q_gain': 6.494,
     'k_gain': 8.0,
     'k_k': 24.227,
     'ln_x_w': 16.124,
     'ln_x_b': 24.054,
     'b_route_group': 8.0,
     'b_route_expert': 29.539,
     'b_gate_2': 7.335,
     'gm_norm_g_2': 43.128,
     's5_lambda_re_2': 64.0,
     's5_lambda_im_2': 50.304,
     's5_log_dt_2': 51.856,
     's5_b_re_2': 64.0,
     's5_b_im_2': 64.0,
     's5_c_re_2': 64.0,
     's5_c_im_2': 64.0,
     's5_b_glu_2': 200.0,
     'g_ffn': 4.439,
     'gm_b_s_2': 19.545,
     's5_w_glu_2': 17.887,
     'norm1_g_2': 4.545,
     's5_d_2': 3.271,
     'norm2_g_2': 8.0}
    for name, (base, spread) in spreads.items():
        noise = np.random.default_rng([zlib.crc32(name.encode()), seed]).standard_normal(out[name].shape)
        drawn = base * np.exp(spread * noise) if base else spread * noise
        out[name] = __import__('jax').numpy.asarray(drawn.astype(out[name].dtype))
    for name, factor in factors.items():
        out[name] = (out[name] * factor).astype(out[name].dtype)
    return out
```

```python
from contextlib import ExitStack

import numpy as np
import concourse.bass as bass
from concourse import mybir

F32 = mybir.dt.float32
ALU = mybir.AluOpType
ACT = mybir.ActivationFunctionType
AX_X = mybir.AxisListType.X

P = 128
T = 256
D = 2048
KT = D // P
MIX = D // 2
MT = MIX // P
CH = 64
NCH = T // CH
TT = T // P
IDX_HEADS = 16
TOP_K = 64
NE, NG, EPG = 16, 4, 4
DE = 512
DFF = 4 * D
UNIT = 2048
RING = 4
BANKS = 4
S5_TILES = 32
NEG = -1.0e30
DECAY = float(np.exp(-0.5))

SECTIONS = [("p1", 60, 1), ("wo", 16, 1), ("moe", 192, 0), ("p2", 96, 1), ("glu", 4, 1),
            ("br", 24, 1), ("wo2", 16, 1), ("mlp", 128, 1)]
MOE_UNITS, MOE_USES = 12, 16


def offsets():
    u = use = 0
    first, uses = {}, {}
    for name, n, per in SECTIONS:
        first[name], uses[name] = u, use
        u += n
        use += NE * MOE_USES if name == "moe" else n * per
    return first, uses, u


U0, B0, UNITS = offsets()
R_DONE = 33

VEC = {}
_n = 0
for _name, _cols in [("g_mix", 16), ("mu", 27), ("w0", 8), ("a0", 8), ("k_k", 8), ("k_a", 8), ("r_k", 8),
                     ("ln_w", 8), ("ln_b", 8), ("q_gain", 1), ("k_gain", 1), ("g_ffn", 16),
                     ("norm1", 16), ("b_gate", 48), ("gm_norm", 8), ("s5_d", 8), ("b_glu", 8),
                     ("norm2", 16), ("final", 16), ("lam_re", 32), ("lam_im", 32), ("log_dt", 32),
                     ("b_route", 20)]:
    VEC[_name] = (_n, _n + _cols)
    _n += _cols
NV = _n

CON = {}
_n = 0
for _name, _cols in [("ident", 128), ("ones", 128), ("head64", 128), ("perm128", 128), ("perm64", 128),
                     ("up_strict64", 128), ("up_incl64", 128), ("lo_diag16", 128), ("up_diag16", 128),
                     ("lo_in32", 128), ("lo_in64", 128), ("cum_after", 128), ("up_strict", 128),
                     ("up_incl", 128), ("reset", 256), ("cos128", 256), ("sin128", 256),
                     ("cos64", 256), ("sin64", 256), ("rank", 16)]:
    CON[_name] = (_n, _n + _cols)
    _n += _cols
NC = _n


def constants():
    c = np.zeros((P, NC), np.float32)

    def put(name, a):
        c[:, CON[name][0]:CON[name][1]] = a

    i, j = np.arange(P)[:, None], np.arange(P)[None, :]
    put("ident", i == j)
    put("ones", 1.0)
    put("head64", i // 64 == j // 64)
    for name, half in (("perm128", 64), ("perm64", 32)):
        low = j % (2 * half) < half
        put(name, np.where(low & (i == j + half), -1.0, 0.0) + np.where(~low & (i == j - half), 1.0, 0.0))
    same = lambda n: i // n == j // n
    put("up_strict64", same(64) & (i < j))
    put("up_incl64", same(64) & (i <= j))
    put("lo_diag16", same(16) & (i > j))
    put("up_diag16", same(16) & (i < j))
    put("lo_in32", same(32) & ~same(16) & (i > j))
    put("lo_in64", same(64) & ~same(32) & (i > j))
    put("cum_after", i >= j)
    put("up_strict", i < j)
    put("up_incl", i <= j)
    t = np.arange(T)
    put("reset", (t % CH != 0)[None, :])
    for n, half in ((128, 64), (64, 32)):
        inv = np.float32(10000.0) ** (-np.arange(half, dtype=np.float32) * np.float32(2.0 / n))
        ang = (t.astype(np.float32)[None, :] * inv[:, None].astype(np.float32)).astype(np.float64)
        put(f"cos{n}", np.tile(np.cos(ang), (P // half, 1)))
        put(f"sin{n}", np.tile(np.sin(ang), (P // half, 1)))
    put("rank", np.broadcast_to(16.0 - np.arange(16), (P, 16)))
    return c


class Steps:

    def __init__(self, sem, names):
        self.sem, self.names, self.taken = sem, names, 0

    def at(self, rnd, name):
        return rnd * len(self.names) + self.names.index(name) + 1

    def step(self, rnd, name):
        self.taken += 1
        assert self.taken == self.at(rnd, name), (rnd, name)
        return 1


DSA_TILES = 33
DSA_PER_PAIR = [5] + [4] * 7
P1_ORDER = [("misc", 0), ("misc", 1), ("misc", 2)]
for _p in range(MT):
    P1_ORDER += [("r", _p), ("k", _p), ("v", _p)]
    P1_ORDER += [("dsa", sum(DSA_PER_PAIR[:_p]) + _q) for _q in range(DSA_PER_PAIR[_p])]
P1_AT = {what: n for n, what in enumerate(P1_ORDER)}
MIX_ORDER = [what for what in P1_ORDER if what[0] != "dsa"]
MU_COL = {what: (what[1] if what[0] == "misc" else 3 + 8 * "rkv".index(what[0]) + what[1]) for what in MIX_ORDER}

PE_RW = ["lora", "kks", "tok", "sco", "ksco", "sq2", "sq4", "sq8", "inv16", "t16", "inv32", "t32", "inv64"] \
    + [f"{s}{c}" for c in range(NCH) for s in "WUZ"] + ["gn1", "gn2"]
ACT_RW = ["lora", "kk2", "rn", "exps", "tok", "mab", "d2", "d4", "d8", "t16", "t32"] \
    + [f"{s}{c}" for c in range(NCH) for s in "WU"] + ["y", "ysq", "grs"]
DVE_RW = ["k", "cum", "kmax", "rk", "tilde", "bon", "mb", "dq", "mk", "d2t", "q1", "q2", "q16", "g16", "q32",
          "g32", "q64"] + [f"z{c}" for c in range(NCH)] + ["yc", "var", "out"]


def filler_ends(p):
    total = 16 * DSA_PER_PAIR[p]
    points = len(PE_RW)
    upto = [total * (f + 1) // points for f in range(points)]
    return upto, [next(f for f in range(points) if upto[f] >= 16 * (q + 1)) for q in range(DSA_PER_PAIR[p])]


def build(nc, A, out, upto="all", dump=None):
    ctx = ExitStack()
    with ctx:
        def sb(name, shape):
            return ctx.enter_context(nc.sbuf_tensor(name, shape, F32))

        def sem(name):
            return ctx.enter_context(nc.semaphore(name))

        ORDER = ["p1", "dsa", "wo", "moe", "p2", "mix2", "br", "mlp"]
        on = lambda s: upto == "all" or ORDER.index(s) <= ORDER.index(upto)

        ring = sb("ring", [P, RING, UNIT])
        XT = sb("XT", [P, KT, T])
        HT = sb("HT", [P, KT, T])
        YT = sb("YT", [P, KT, T])
        C = sb("C", [P, NC])
        V = sb("V", [P, NV])
        SQ = sb("SQ", [P, 4, T])
        RS = sb("RS", [P, T])
        NEGS = sb("NEGS", [P, 16])
        ONEMU = sb("ONEMU", [P, 27])
        ONEKA = sb("ONEKA", [P, 8])
        work = sb("work", [P, 27600])
        PG = ctx.enter_context(nc.psum_tensor("PG", [P, BANKS, 512], F32))
        PX = ctx.enter_context(nc.psum_tensor("PX", [P, 4, 512], F32))

        def con(name):
            return C[:, CON[name][0]:CON[name][1]]

        def vec(name, i=0):
            return V[:, VEC[name][0] + i:VEC[name][0] + i + 1]

        taken = [0]

        def area(n, at=None):
            if at is not None:
                taken[0] = at
            a = work[:, taken[0]:taken[0] + n]
            taken[0] += n
            assert taken[0] <= 27600, taken[0]
            return a

        def cube(a, n):
            return a.rearrange("p (a b) -> p a b", a=n)

        slot_full = [sem(f"slot_full{i}") for i in range(RING)]
        unit_done = sem("unit_done")
        bank_free = [sem(f"bank_free{i}") for i in range(BANKS)]
        s_x = [sem(f"x_in{i}") for i in range(4)]
        s_con, s_vec, s_lora, s_out = sem("constants_in"), sem("vectors_in"), sem("lora_in"), sem("out_stored")
        s_vprep = sem("vectors_prepared")
        s_sq, s_squsd, s_ms, s_rt, s_h = sem("squares_ready"), sem("squares_summed"), sem("mean_square"), \
            sem("root_ready"), sem("normed_tiles")
        s_mixed = sem("prev_scaled")
        s_lo_dve, s_lo_act = sem("low_rank_mixed"), sem("low_rank_act")
        s_zero = sem("zeros_set")
        s_xt = sem("residual_tiles")
        dve_chain, act_chain = sem("dve_chain"), sem("act_chain")
        PR = Steps(sem("rwkv_pe"), PE_RW)
        AR_ = Steps(sem("rwkv_act"), ACT_RW)
        DR = Steps(sem("rwkv_dve"), DVE_RW)
        a_sq, a_sum, a_ms, a_rs, a_nrm, a_rot, a_cos, a_rope = (sem("qk_" + n) for n in (
            "squared", "summed", "mean_square", "inverse_root", "normed", "rotated", "cos_part", "roped"))
        a_vt, a_v, a_is, a_relu, a_acc, a_bias = (sem("idx_" + n) for n in (
            "turned", "turned_taken", "products", "relu", "added", "bias"))
        a_lg, a_l, a_ex, a_p, a_t, a_pt, a_pv, a_y = (sem("att_" + n) for n in (
            "logits", "maximum", "exp", "probs", "turned", "turned_taken", "values", "out"))
        s_route_in, s_lgt, s_router, s_rexp, s_cbt, s_cbb, s_comb = (sem("route_" + n) for n in (
            "in", "logits", "vector", "exp", "turned", "spread", "weights"))
        s_he = sem("expert_hidden")
        c_act, c_dve, c_par, c_turn, c_lb, c_cd, c_tab, c_bu, c_x, c_s, c_y, c_yd, c_g = (sem("s5_" + n) for n in (
            "act", "vector", "in", "turned", "turned_taken", "out_matrix", "table", "inputs", "rotated", "states",
            "outputs", "outputs_taken", "gelu"))
        pool_chain = sem("pool_chain")
        c_pow = sem("s5_powers")
        g_in, g_sq, g_sum, g_ms, g_rt, g_vn, g_t, g_tt, g_mix, g_y = (sem("gmlp_" + n) for n in (
            "in", "squared", "summed", "mean_square", "root", "normed", "turned", "turned_taken", "mixed", "out"))
        b_z, b_l, b_sp, b_r, b_w, b_e, b_pv, b_y = (sem("stick_" + n) for n in (
            "products", "log", "softplus", "sums", "exponent", "weights", "values", "out"))
        s_relu, s_tile_out = sem("mlp_relu"), sem("tiles_out")
        c_zero, s_yb = sem("s5_zeroed"), sem("glu_out")
        s_end = sem("result_ready")

        DQ = cube(area(DSA_TILES * T, 0), DSA_TILES)
        LORA = area(MIX)
        GUP = area(2 * MIX).rearrange("p (a n) -> p a n", a=2)
        MBF = cube(area(3 * (T + 1)), 3)
        LO = cube(area(3 * T), 3)
        LO_END = taken[0]
        R_, K_, V_ = (area(T) for _ in range(3))
        EW, EA, G_, CS, CP, KK2, RN, PIN, PINV, PPREV, AM, KM, BON = (area(T) for _ in range(13))
        AR = area(2 * T).rearrange("p (tt a n) -> p tt a n", tt=TT, a=2)
        BT_, KT_ = area(T), area(T)
        TOK = cube(area(6 * P), 6)
        MBK = area(4 * T).rearrange("p (h tt a n) -> p h tt a n", h=2, tt=TT, a=2)
        MKK = area(4 * T).rearrange("p (h tt a n) -> p h tt a n", h=2, tt=TT, a=2)
        MAB, DA, EE, FF, DT, D2, D2T, Q_ = (cube(area(4 * P), 4) for _ in range(8))
        TM, GM = D2T, DT
        ZB = cube(area(2 * P), 2)
        ZP, ZT = area(P), area(P)
        W_, U_ = area(P), area(P)
        Y_, YC = area(T), area(T)
        YSQ = KK2
        GRS = RN

        area(0, LO_END)
        MSB = cube(area(16 * T), 16)
        VTOK = cube(area(TT * MIX), TT)
        ISC = cube(area(TT * T), TT)
        BIAS = cube(area(TT * T), TT)
        RL = cube(area(4 * T), 4)
        ROPE_C, ROPE_S = cube(area(4 * T), 4), cube(area(2 * T), 2)
        WX = cube(area(TT * IDX_HEADS), TT)
        TOP8 = area(8)
        LG, PR_, PT_ = cube(area(2 * T), 2), cube(area(2 * T), 2), cube(area(2 * T), 2)
        MX, NMX, SUM, RSUM = (area(16) for _ in range(4))

        COMB = cube(area(NE * T, 0), NE)
        HE = area(2 * 4 * T).rearrange("p (e j t) -> p e j t", e=2, j=4)
        SG, UP = cube(area(2 * T), 2), cube(area(2 * T), 2)
        ROUTE = cube(area(KT * 20), KT)
        LGT = cube(area(TT * 20), TT)
        G1, G2, G3, GO = (cube(area(TT * NG), TT) for _ in range(4))
        E1, E2, E3, O0, O1 = (cube(area(TT * NE), TT) for _ in range(5))
        m1, m2, m3, pg, v0, v1, vs = (area(TT) for _ in range(7))
        CB = cube(area(TT * P), TT)
        CT = area(T)

        S5IN = cube(area(MT * T, 0), MT)
        UV = cube(area(2 * MT * T), 2 * MT)
        QKV = cube(area(3 * MT * T), 3 * MT)
        gates_at = taken[0]
        GT = cube(area(3 * KT * T), 3 * KT)
        SPAT = cube(area(MT * P), MT)
        SPAT_B = area(MT * P)
        (S_DT, S_TH, S_LR, S_N, S_R, S_MAG, S_SIN, S_COS, S_ABR, S_ABI, S_DEN, S_KR, S_KI, S_A, S_B) = (
            area(S5_TILES) for _ in range(15))
        PW = [area(S5_TILES) for _ in range(5)]
        NEGM = area(P)
        area(0, gates_at)
        LB = area(2 * MT * P).rearrange("p (c b n) -> p c b n", c=2, b=MT)
        CD = area(2 * S5_TILES * 32).rearrange("p (c i n) -> p c i n", c=2, i=S5_TILES)
        ROT = area(4 * 4 * T).rearrange("p (b c n) -> p b c n", b=2, c=2)
        XR = area(2 * 4 * T).rearrange("p (c n) -> p c n", c=2)
        BBD = XR[:, :, :].rearrange("p c n -> p (c n)").rearrange("p (c i n) -> p c i n", c=2, i=S5_TILES)
        TR = area(2 * 4 * T).rearrange("p (c n) -> p c n", c=2)
        S5B = TR[:, 0, :].rearrange("p (c i n) -> p c i n", c=2, i=S5_TILES)
        S5C = TR[:, 1, :].rearrange("p (c i n) -> p c i n", c=2, i=S5_TILES)
        yt = YT[:, :, :].rearrange("p a t -> p (a t)")
        POW = yt[:, 0:2048].rearrange("p (f c i n) -> p f c i n", f=2, c=2, i=S5_TILES)
        PT2 = yt[:, 2048:4096].rearrange("p (c n) -> p c n", c=2)
        PB = PT2[:, :, :].rearrange("p c n -> p (c n)").rearrange("p (c n) -> p c n", c=4)
        GVT = yt[:, 0:2048].rearrange("p (tt n) -> p tt n", tt=TT)
        AVT = yt[:, 2048:4096].rearrange("p (tt n) -> p tt n", tt=TT)
        area(0, gates_at + 36 * T)
        ZS, LN_, SP_, WW = (cube(area(2 * 384), 2) for _ in range(4))
        HID = cube(area(KT * T, gates_at), KT)
        YB = YT[:, 0:MT, :]
        SQF = SQ[:, :, :].rearrange("p a t -> p (a t)")

        block = ctx.enter_context(nc.Block())

        def free_bank(use):
            return bank_free[use % BANKS]

        def wait_bank(eng, use, more=0):
            if use >= BANKS:
                eng.wait_ge(free_bank(use), use // BANKS + more)

        def wait_taken(eng, use, more=0):
            eng.wait_ge(free_bank(use), use // BANKS + 1 + more)

        def dump_or_end(sp):
            src = {"XT": XT, "YT": YT, "HT": HT}[dump or "XT"]
            lo = 8 if upto == 'p1' else 0
            sp.dma_start(out[:, lo:, :], src[:, lo:, :]).then_inc(s_out, 16)
            sp.wait_ge(s_out, 16)

        total_units = UNITS if upto == "all" else {"p1": 60, "dsa": 60, "wo": 76, "moe": 268, "p2": 364, "mix2": 368,
                                                   "br": 408, "mlp": 536}[upto]

        @block.sync
        def _(sp):
            for q in range(4):
                sp.dma_start(XT[:, 4 * q:4 * q + 4, :], A["xT"][:, 4 * q:4 * q + 4, :]).then_inc(s_x[q], 16)
            for s in range(RING):
                sp.dma_start(ring[:, s, :], A["weights"][s]).then_inc(slot_full[s], 16)
            with sp.Fori(1, total_units // RING) as i:
                for s in range(RING):
                    sp.wait_ge(unit_done, i * RING + (s + 1 - RING))
                    sp.dma_start(ring[:, s, :], A["weights"][bass.ds(i * RING + s, 1), :, :]
                                 .rearrange("o p n -> p (o n)")).then_inc(slot_full[s], 16)
            if upto in ("p1", "dsa"):
                sp.wait_ge(DR.sem, DR.at(MT - 1, "out"))
                if upto == "dsa":
                    sp.wait_ge(a_y, 16)
                dump_or_end(sp)
            else:
                if upto in ("all", "mlp"):
                    for q in range(4):
                        sp.wait_ge(s_h, 4 * KT + 4 * q + 4)
                        sp.dma_start(out[:, 4 * q:4 * q + 4, :], YT[:, 4 * q:4 * q + 4, :]).then_inc(s_out, 16)
                    sp.wait_ge(s_out, 64)
                else:
                    sp.wait_ge(s_end, 1)
                    if upto == "mix2":
                        lo = dict(ya=UV[:, 0:8, :], yb=YB, yc=QKV[:, 0:8, :])[dump]
                        sp.dma_start(out[:, 0:8, :], lo).then_inc(s_out, 16)
                        sp.dma_start(out[:, 8:16, :], lo).then_inc(s_out, 16)
                        sp.wait_ge(s_out, 32)
                    else:
                        dump_or_end(sp)

        @block.tensor
        def _(pe):
            def unit(u, use, x, kts=KT, tiles=1, first=None, full=0, free=0):
                pe.wait_ge(slot_full[u % RING], 16 * (u // RING + 1) + full)
                for t in range(tiles):
                    if t % 2 == 0:
                        wait_bank(pe, use + t // 2, free)
                    for k in range(kts):
                        if first is not None and t == 0:
                            pe.wait_ge(s_h, first + k + 1)
                        last = pe.matmul(PG[:, (use + t // 2) % BANKS, (t % 2) * T:(t % 2) * T + T],
                                         ring[:, u % RING, (k * tiles + t) * P:(k * tiles + t) * P + P],
                                         x[:, k, :], start=(k == 0), stop=(k == kts - 1))
                last.then_inc(unit_done, 1)

            def norm(n):
                for k in range(KT):
                    pe.wait_ge(s_sq, KT * n + k + 1)
                    pe.matmul(PX[:, 0, 0:T], con("ones"), SQ[:, k % 4, :], start=(k == 0),
                              stop=(k == KT - 1)).then_inc(s_squsd, 1)

            pe.wait_ge(s_con, 16)
            norm(0)
            for u in range(3):
                unit(u, u, HT, first=0 if u == 0 else None)

            def fill(p, f):
                upto_, ends = filler_ends(p)
                for m in range(upto_[f - 1] if f else 0, upto_[f]):
                    u = P1_AT[("dsa", sum(DSA_PER_PAIR[:p]) + m // 16)]
                    k = m % 16
                    if k == 0:
                        pe.wait_ge(slot_full[u % RING], 16 * (u // RING + 1))
                        wait_bank(pe, u)
                    mm = pe.matmul(PG[:, u % BANKS, 0:T], ring[:, u % RING, k * P:k * P + P], HT[:, k, :],
                                   start=(k == 0), stop=(k == KT - 1))
                    if k == KT - 1:
                        mm.then_inc(unit_done, 1)

            def pair(p):
                for w in "rkv":
                    unit(P1_AT[(w, p)], P1_AT[(w, p)], HT)
                step = iter(range(len(PE_RW)))
                act = lambda name: pe.wait_ge(AR_.sem, AR_.at(p, name))
                dve = lambda name: pe.wait_ge(DR.sem, DR.at(p, name))

                def done(mm, name):
                    mm.then_inc(PR.sem, PR.step(p, name))
                    fill(p, next(step))

                if p == 0:
                    pe.wait_ge(s_lora, 32)
                    pe.wait_ge(s_lo_dve, 2)
                    pe.wait_ge(s_lo_act, 3)
                else:
                    pe.wait_ge(DR.sem, DR.at(p - 1, "out"))
                cols = slice(p * P, p * P + P)
                pe.matmul(PX[:, 0, 0:T], LORA[0:64, cols], LO[0:64, 0, :], start=True, stop=True)
                pe.matmul(PX[:, 1, 0:T], LORA[64:128, cols], LO[64:128, 0, :], start=True, stop=True)
                pe.matmul(PX[:, 2, 0:T], GUP[:, 0, cols], LO[:, 1, :], start=True, stop=False)
                done(pe.matmul(PX[:, 2, 0:T], GUP[0:32, 1, cols], LO[0:32, 2, :], start=False, stop=True), "lora")
                act("kk2")
                done(pe.matmul(PX[:, 3, 0:T], con("head64"), KK2, start=True, stop=True), "kks")
                dve("tilde")
                act("lora")
                pe.matmul(PX[:, 3, T:2 * T], con("head64"), AM, start=True, stop=True)
                for n in range(6):
                    src = (V_, BT_, KT_)[n // 2]
                    mm = pe.transpose(PX[:, n // 4, (n % 4) * P:(n % 4) * P + P], src[:, (n % 2) * P:(n % 2) * P + P],
                                      con("ident"))
                done(mm, "tok")
                act("tok")
                dve("bon")
                for h in range(2):
                    hs = slice(64 * h, 64 * h + 64)
                    for tt in range(TT):
                        ts = slice(tt * P, tt * P + P)
                        pe.matmul(PX[:, 2 + h, 2 * P * tt:2 * P * tt + 2 * P], BT_[hs, ts],
                                  AR[hs, tt, :, :].rearrange("p a n -> p (a n)"), start=True, stop=True)
                        mm = pe.matmul(PX[:, h, P * tt:P * tt + P], AR[hs, tt, 0, :], BT_[hs, ts],
                                       start=True, stop=True)
                done(mm, "sco")
                dve("mb")
                for h in range(2):
                    hs = slice(64 * h, 64 * h + 64)
                    for tt in range(TT):
                        mm = pe.matmul(PX[:, 2 + h, 2 * P * tt:2 * P * tt + 2 * P], KT_[hs, tt * P:tt * P + P],
                                       AR[hs, tt, :, :].rearrange("p a n -> p (a n)"), start=True, stop=True)
                done(mm, "ksco")

                def four(bank, left, right, transpose=False):
                    for n in range(4):
                        o = PX[:, bank, n * P:n * P + P]
                        if transpose:
                            mm = pe.transpose(o, right[:, n, :], con("ident"))
                        else:
                            mm = pe.matmul(o, left[:, n, :], right[:, n, :], start=True, stop=True)
                    return mm

                act("mab")
                dve("dq")
                four(0, DT, DA)
                done(four(1, DA, DT), "sq2")
                act("d2")
                dve("d2t")
                four(0, D2T, D2)
                four(1, D2, D2T)
                dve("mk")
                done(four(2, D2, Q_), "sq4")
                act("d4")
                dve("q1")
                four(0, DT, DA)
                done(four(3, DA, Q_), "sq8")
                act("d8")
                dve("q2")
                done(four(2, D2, Q_), "inv16")
                for t, left in (("16", EE), ("32", FF)):
                    dve("q" + t)
                    four(0, None, Q_, transpose=True)
                    done(four(1, left, Q_), "t" + t)
                    act("t" + t)
                    dve("g" + t)
                    done(four(3 if t == "16" else 2, TM, GM), "inv32" if t == "16" else "inv64")
                for c in range(NCH):
                    tt, j = c // 2, c % 2
                    rows, cs = slice(64 * j, 64 * j + 64), slice(64 * j, 64 * j + 64)
                    z = ZB[:, c % 2, :]
                    if c == 0:
                        dve("q64")
                    else:
                        dve(f"z{c - 1}")
                    pe.matmul(PX[rows, 0, 0:P], AR[:, tt, 0, cs], z, start=True, stop=False, skip_group_check=True)
                    for h in range(2):
                        mm = pe.matmul(PX[rows, 0, 64 * h:64 * h + 64], MKK[:, h, tt, 0, cs],
                                       TOK[:, tt, 64 * h:64 * h + 64], start=False, stop=(h == 1),
                                       skip_group_check=True)
                    done(mm, f"W{c}")
                    act(f"W{c}")
                    for h in range(2):
                        mm = pe.matmul(PX[rows, 1, 64 * h:64 * h + 64], Q_[:, 2 * h + tt, cs],
                                       W_[:, 64 * h:64 * h + 64], start=True, stop=True)
                    done(mm, f"U{c}")
                    act(f"U{c}")
                    y = PX[:, 3, c * CH:c * CH + CH]
                    pe.matmul(y, z, AR[:, tt, 1, cs], start=True, stop=False, skip_group_check=True)
                    for h in range(2):
                        hs = slice(64 * h, 64 * h + 64)
                        yh = PX[hs, 3, c * CH:c * CH + CH]
                        pe.matmul(yh, U_[:, hs], MBK[:, h, tt, 1, cs], start=False, stop=False,
                                  skip_group_check=True)
                        pe.matmul(yh, TOK[:, tt, hs], MKK[:, h, tt, 1, cs], start=False, stop=(h == 1),
                                  skip_group_check=True)
                    pe.matmul(PX[:, 2, 0:P], TOK[rows, 2 + tt, :], U_[rows, :], start=True, stop=False)
                    done(pe.matmul(PX[:, 2, 0:P], TOK[rows, 4 + tt, :], TOK[rows, tt, :], start=False, stop=True),
                         f"Z{c}")
                act("y")
                done(pe.matmul(PX[:, 0, 0:T], con("head64"), Y_, start=True, stop=True), "gn1")
                act("ysq")
                done(pe.matmul(PX[:, 1, 0:T], con("head64"), YSQ, start=True, stop=True), "gn2")

            for p in range(MT):
                pair(p)

            def attention():
                pe.wait_ge(DR.sem, DR.at(MT - 1, "out"))
                for n in range(16):
                    pe.wait_ge(a_sq, n + 1)
                    if n >= 2:
                        pe.wait_ge(a_ms, n - 1)
                    pe.matmul(PX[:, n % 2, 0:T], con("ones"), SQ[:, n % 4, :], start=True, stop=True).then_inc(a_sum, 1)
                for r in range(25):
                    if r >= 9:
                        pe.wait_ge(a_nrm, r - 8)
                    if r >= 2:
                        pe.wait_ge(a_rope, r - 1)
                    pe.matmul(PX[:, 2 + r % 2, 0:T], con("perm64" if r < 9 else "perm128"), DQ[:, r, :],
                              start=True, stop=True).then_inc(a_rot, 1)
                pe.wait_ge(a_rope, 25)
                pe.wait_ge(a_ms, 16)
                for g in range(4):
                    if g >= 2:
                        pe.wait_ge(a_v, g - 1)
                    for n in range(4):
                        mm = pe.transpose(PX[:, g % 2, n * P:n * P + P],
                                          DQ[:, 25 + 4 * (g % 2) + n, (g // 2) * P:(g // 2) * P + P], con("ident"))
                    mm.then_inc(a_vt, 1)
                for tt in range(TT):
                    mm = pe.transpose(PX[:, 2, tt * P:tt * P + P], LO[:, 2, tt * P:tt * P + P], con("ident"))
                mm.then_inc(a_vt, 1)
                pe.wait_ge(a_v, 5)
                for n in range(TT * IDX_HEADS):
                    tt, h = n // IDX_HEADS, n % IDX_HEADS
                    rows = slice(64 * (h % 2), 64 * (h % 2) + 64)
                    if n >= 4:
                        pe.wait_ge(a_relu, n - 3)
                    pe.matmul(PX[:, h % 4, 0:(tt + 1) * P], DQ[rows, 1 + h // 2, tt * P:tt * P + P],
                              DQ[rows, 0, 0:(tt + 1) * P], start=True, stop=True).then_inc(a_is, 1)
                pe.wait_ge(a_relu, TT * IDX_HEADS)
                for n in range(18):
                    if n < 16:
                        tt, h = n // MT, n % MT
                        if n >= 2:
                            pe.wait_ge(a_l, n - 1)
                        pe.matmul(PX[:, n % 2, 0:(tt + 1) * P], DQ[:, 9 + h, tt * P:tt * P + P],
                                  DQ[:, 17 + h, 0:(tt + 1) * P], start=True, stop=True).then_inc(a_lg, 1)
                    if 1 <= n < 17:
                        m = n - 1
                        pe.wait_ge(a_p, m + 1)
                        if m:
                            pe.wait_ge(a_pt, m)
                        for s in range(m // MT + 1):
                            mm = pe.transpose(PX[:, 2, s * P:s * P + P], PR_[:, m % 2, s * P:s * P + P], con("ident"))
                        mm.then_inc(a_t, 1)
                    if n >= 2:
                        m = n - 2
                        tt, h = m // MT, m % MT
                        pe.wait_ge(a_pt, m + 1)
                        if m:
                            pe.wait_ge(a_y, m)
                        for s in range(tt + 1):
                            mm = pe.matmul(PX[:, 3, 0:P], VTOK[:, s, h * P:h * P + P], PT_[:, m % 2, s * P:s * P + P],
                                           start=(s == 0), stop=(s == tt))
                        mm.then_inc(a_pv, 1)

            if on("dsa"):
                attention()
            if on("wo"):
                pe.wait_ge(a_y, 16)
                for t in range(KT):
                    unit(U0["wo"] + t, B0["wo"] + t, YT)
            if on("moe"):
                norm(1)
                pe.wait_ge(s_h, 2 * KT)
                pe.wait_ge(s_route_in, 16)
                for tt in range(TT):
                    for k in range(KT):
                        mm = pe.matmul(PX[:, 1, 32 * tt:32 * tt + 20], HT[:, k, tt * P:tt * P + P], ROUTE[:, k, :],
                                       start=(k == 0), stop=(k == KT - 1))
                mm.then_inc(s_lgt, 1)
                pe.wait_ge(s_router, R_DONE)
                for tt in range(TT):
                    mm = pe.transpose(PX[:, 2, tt * P:tt * P + P], CB[:, tt, :], con("ident"))
                mm.then_inc(s_cbt, 1)
                pe.wait_ge(s_cbb, 1)
                for e in range(NE):
                    if e >= 4:
                        pe.wait_ge(s_comb, e - 3)
                    pe.matmul(PX[:, e % 4, 0:T], C[0:32, e:e + 1].to_broadcast([32, P]), CT[0:32, :],
                              start=True, stop=True).then_inc(s_cbt, 1)
                with pe.Fori(0, NE // 2) as i:
                    for e in range(2):
                        full, free = i * 96, i * 8
                        u, use = U0["moe"] + e * MOE_UNITS, B0["moe"] + e * MOE_USES
                        for j in range(8):
                            unit(u + j, use + j, HT, full=full, free=free)
                        for d in range(4):
                            if d == 0:
                                pe.wait_ge(s_he, i * 8 + (4 * e + 6))
                            unit(u + 8 + d, use + 8 + 2 * d, HE[:, e, :, :], kts=4, tiles=4, full=full, free=free)

            def s5_inputs(b):
                if b:
                    pe.wait_ge(c_yd, b)
                else:
                    pe.wait_ge(c_lb, 4)
                    wait_taken(pe, B0["p2"] + 7)
                for i in range(4):
                    rows = slice(32 * i, 32 * i + 32)
                    for c in range(2):
                        mm = pe.matmul(PX[:, i, c * T:c * T + T], LB[rows, c, b, :], S5IN[rows, b, :],
                                       start=True, stop=True)
                mm.then_inc(c_bu, 1)

            def s5_outputs(b):
                if b == 0:
                    pe.wait_ge(c_cd, 4)
                pe.wait_ge(c_s, b + 1)
                for i in range(4):
                    for c in range(2):
                        s = (TR[:, 0, :], XR[:, 1, :])[c]
                        mm = pe.matmul(PX[32 * i:32 * i + 32, 0, 0:T], CD[:, c, 4 * b + i, :], s[:, i * T:i * T + T],
                                       start=(c == 0), stop=(c == 1))
                mm.then_inc(c_y, 1)

            if on("p2"):
                norm(2)
                for n in range(48):
                    unit(U0["p2"] + n, B0["p2"] + n, HT, first=2 * KT if n == 0 else None)
                    if n == 22:
                        pe.wait_ge(c_dve, 2)
                        for q in range(4):
                            for m in range(4):
                                b = 4 * (q % 2) + m
                                mm = pe.transpose(PX[:, q, m * P:m * P + P],
                                                  BBD[:, q // 2, 4 * b:4 * b + 4, :].rearrange("p i n -> p (i n)"),
                                                  con("ident"))
                        mm.then_inc(c_turn, 1)
                    if n == 23:
                        s5_inputs(0)
                    if n >= 24 and n % 3 == 2:
                        b = (n - 24) // 3
                        s5_outputs(b)
                        if b + 1 < MT:
                            s5_inputs(b + 1)

            def gate_event(g):
                if g == 0:
                    pe.wait_ge(c_yd, MT)
                    for k in range(MT):
                        pe.wait_ge(g_sq, k + 1)
                        pe.matmul(PX[:, 0, 0:T], con("ones"), SQ[:, k % 4, :], start=(k == 0),
                                  stop=(k == MT - 1)).then_inc(g_sum, 1)
                elif g in (2, 3):
                    if g == 2:
                        pe.wait_ge(g_vn, MT)
                        pe.wait_ge(c_g, MT)
                    for q in range(4):
                        t = 4 * (g - 2) + q
                        if t >= 4:
                            pe.wait_ge(g_tt, t - 3)
                        for m in range(4):
                            src = (UV[:, MT + 4 * (q % 2) + m, :], QKV[:, 2 * MT + 4 * (q % 2) + m, :])[g - 2]
                            mm = pe.transpose(PX[:, q, m * P:m * P + P], src[:, (q // 2) * P:(q // 2) * P + P],
                                              con("ident"))
                        mm.then_inc(g_t, 1)
                elif g == 4:
                    pe.wait_ge(g_tt, 8)
                    pe.wait_ge(g_in, 32)
                    for m in range(MT):
                        for tt in range(TT):
                            o = PX[:, m // 2, (m % 2) * T + tt * P:(m % 2) * T + tt * P + P]
                            pe.matmul(o, GVT[:, tt, m * P:m * P + P], SPAT[:, m, :], start=True, stop=False)
                            mm = pe.matmul(o, con("ones")[0:1, :], SPAT_B[0:1, m * P:m * P + P], start=False, stop=True)
                    mm.then_inc(g_mix, 1)
                for h in range(MT):
                    q, k = QKV[:, h, :], QKV[:, MT + h, :]
                    if g == 6 + 2 * h:
                        if h == 0:
                            pe.wait_ge(g_y, 4)
                        else:
                            pe.wait_ge(b_l, h)
                        pe.matmul(PX[:, 0, 0:T], k[:, 0:P], q, start=True, stop=True)
                        pe.matmul(PX[:, 0, T:384], k[:, P:T], q[:, P:T], start=True, stop=True).then_inc(b_z, 1)
                    if g == 7 + 2 * h:
                        pe.wait_ge(b_sp, h + 1)
                        if h:
                            pe.wait_ge(b_w, h)
                        sp = SP_[:, h % 2, :]
                        pe.matmul(PX[:, 1, 0:T], con("cum_after"), sp[:, 0:T], start=True, stop=False)
                        pe.matmul(PX[:, 1, P:T], con("ones"), sp[:, T:384], start=False, stop=True)
                        pe.matmul(PX[:, 1, T:384], con("cum_after"), sp[:, T:384], start=True,
                                  stop=True).then_inc(b_r, 1)
                    if g == 8 + 2 * h:
                        pe.wait_ge(b_e, h + 1)
                        if h:
                            pe.wait_ge(b_y, h)
                        w = WW[:, h % 2, :]
                        pe.matmul(PX[:, 2, 0:T], AVT[:, 0, h * P:h * P + P], w[:, 0:T], start=True, stop=False)
                        pe.matmul(PX[:, 2, P:T], AVT[:, 1, h * P:h * P + P], w[:, T:384], start=False,
                                  stop=True).then_inc(b_pv, 1)

            if on("mix2"):
                for g in range(48):
                    unit(U0["p2"] + 48 + g, B0["p2"] + 48 + g, HT)
                    gate_event(g)
                for j in range(4):
                    unit(U0["glu"] + j, B0["glu"] + j, S5IN, kts=MT, tiles=2)
            if on("br"):
                for n in range(3):
                    x = (UV, YB, QKV)[n]
                    for j in range(8):
                        if n == 1 and j == 0:
                            pe.wait_ge(s_yb, 4)
                        unit(U0["br"] + 8 * n + j, B0["br"] + 8 * n + j, x, kts=MT, tiles=2)
                for j in range(4):
                    wait_taken(pe, B0["br"] + 20 + j)
                for t in range(KT):
                    unit(U0["wo2"] + t, B0["wo2"] + t, HT)
            if on("mlp"):
                norm(3)
                pe.wait_ge(s_h, 4 * KT)
                with pe.Fori(0, 4) as i:
                    u, use = U0["mlp"], B0["mlp"]
                    for t in range(KT):
                        unit(u + t, use + t, HT, full=i * 128, free=i * 8)
                    for t in range(KT):
                        if t == 0:
                            for b in range(BANKS):
                                wait_taken(pe, use + 12 + b, i * 8)
                        unit(u + KT + t, use + KT + t, HID, full=i * 128, free=i * 8)
                norm(4)

        @block.scalar
        def _(act):
            n_chain = [0]

            def link(ins):
                n_chain[0] += 1
                ins.then_inc(act_chain, 1)
                act.wait_ge(act_chain, n_chain[0])

            act.dma_start(C[:, :], A["constants"]).then_inc(s_con, 16)
            act.dma_start(V[:, :], A["vectors"]).then_inc(s_vec, 16)
            act.dma_start(LORA, A["lora"]).then_inc(s_lora, 16)
            act.dma_start(GUP, A["gate_up"]).then_inc(s_lora, 16)

            def norm(n, ready):
                for k in range(KT):
                    ready(k)
                    if KT * n + k >= 4:
                        act.wait_ge(s_squsd, KT * n + k - 3)
                    act.activation(SQ[:, k % 4, :], XT[:, k, :], ACT.Square).then_inc(s_sq, 1)
                act.wait_ge(s_ms, n + 1)
                act.activation(RS[:, :], RS[:, :], ACT.Sqrt).then_inc(s_rt, 1)

            norm(0, lambda k: act.wait_ge(s_x[k // 4], 16))

            def mix(what):
                m, u = MIX_ORDER.index(what), P1_AT[what]
                if m >= 3:
                    before = P1_AT[MIX_ORDER[m - 3]]
                    act.wait_ge(free_bank(before), before // BANKS + 1)
                act.wait_ge(unit_done, u + 1)
                act.activation(MBF[:, m % 3, 1:T + 1], PG[:, u % BANKS, 0:T], ACT.Copy,
                               scale=vec("mu", MU_COL[what])).then_inc(s_mixed, 1)

            act.wait_ge(s_vec, 16)
            act.wait_ge(s_zero, 1)
            for m in range(3):
                mix(("misc", m))
            act.wait_ge(free_bank(0), 1)
            act.activation(LO[0:64, 0, :], LO[0:64, 0, :], ACT.Tanh).then_inc(s_lo_act, 1)
            act.wait_ge(free_bank(1), 1)
            act.wait_ge(free_bank(2), 1)
            act.activation(LO[:, 1, :], LO[:, 1, :], ACT.Tanh, scale=0.5).then_inc(s_lo_act, 1)
            act.activation(LO[0:32, 2, :], LO[0:32, 2, :], ACT.Tanh, scale=0.5).then_inc(s_lo_act, 1)

            def pair(p):
                pe = lambda name: act.wait_ge(PR.sem, PR.at(p, name))
                dve = lambda name: act.wait_ge(DR.sem, DR.at(p, name))
                taken_ = [0]
                _, ends = filler_ends(p)

                def take_dsa(before):
                    while taken_[0] < len(ends) and ends[taken_[0]] < PE_RW.index(before):
                        d = sum(DSA_PER_PAIR[:p]) + taken_[0]
                        u = P1_AT[("dsa", d)]
                        act.wait_ge(unit_done, u + 1)
                        act.activation(DQ[:, d, :], PG[:, u % BANKS, 0:T], ACT.Copy).then_inc(free_bank(u), 1)
                        taken_[0] += 1

                def done(ins, name):
                    ins.then_inc(AR_.sem, AR_.step(p, name))

                def me(name):
                    act.wait_ge(AR_.sem, AR_.at(p, name))

                for w in "rkv":
                    mix((w, p))
                if p == 0:
                    act.wait_ge(s_vprep, 4)
                pe("lora")
                act.activation(EW, PX[:, 0, 0:T], ACT.Exp, scale=-1.0, bias=NEGS[:, p:p + 1])
                act.activation(EA, PX[:, 1, 0:T], ACT.Exp, scale=-1.0, bias=NEGS[:, 8 + p:9 + p])
                done(act.activation(G_, PX[:, 2, 0:T], ACT.Copy), "lora")
                dve("k")
                done(act.activation(KK2, K_, ACT.Square, scale=vec("k_k", p)), "kk2")
                dve("kmax")
                link(act.activation(RN, RN, ACT.Ln))
                done(act.activation(RN, RN, ACT.Exp, scale=-0.5), "rn")
                act.activation(PIN, CS, ACT.Exp, scale=-DECAY)
                act.activation(PINV, CS, ACT.Exp, scale=DECAY)
                done(act.activation(PPREV, CP, ACT.Exp, scale=-DECAY), "exps")
                take_dsa("tok")
                pe("tok")
                act.activation(TOK[:, 0:4, :], PX[:, 0, :].rearrange("p (n a) -> p n a", n=4), ACT.Copy)
                done(act.activation(TOK[:, 4:6, :], PX[:, 1, 0:T].rearrange("p (n a) -> p n a", n=2), ACT.Copy), "tok")
                take_dsa("sco")
                pe("sco")
                act.activation(MAB[:, 0:2, :], PX[:, 0, 0:T].rearrange("p (n a) -> p n a", n=2), ACT.Copy)
                done(act.activation(MAB[:, 2:4, :], PX[:, 1, 0:T].rearrange("p (n a) -> p n a", n=2), ACT.Copy), "mab")

                def four(dst, bank):
                    return act.activation(dst, PX[:, bank, :].rearrange("p (n a) -> p n a", n=4), ACT.Copy)

                take_dsa("sq2")
                pe("sq2")
                done(four(D2, 0), "d2")
                take_dsa("sq4")
                pe("sq4")
                four(DA, 0)
                done(four(DT, 1), "d4")
                take_dsa("sq8")
                pe("sq8")
                done(four(D2, 0), "d8")
                for t in ("16", "32"):
                    take_dsa("t" + t)
                    pe("t" + t)
                    done(four(TM, 0), "t" + t)
                for c in range(NCH):
                    rows = slice(64 * (c % 2), 64 * (c % 2) + 64)
                    take_dsa(f"W{c}")
                    pe(f"W{c}")
                    done(act.activation(W_[rows, :], PX[rows, 0, 0:P], ACT.Copy), f"W{c}")
                    take_dsa(f"U{c}")
                    pe(f"U{c}")
                    done(act.activation(U_[rows, :], PX[rows, 1, 0:P], ACT.Copy), f"U{c}")
                take_dsa("Z3")
                pe("Z3")
                done(act.activation(Y_, PX[:, 3, 0:T], ACT.Copy), "y")
                dve("yc")
                done(act.activation(YSQ, YC, ACT.Square), "ysq")
                take_dsa("gn2")
                dve("var")
                link(act.activation(GRS, GRS, ACT.Ln))
                done(act.activation(GRS, GRS, ACT.Exp, scale=-0.5), "grs")
                while taken_[0] < len(ends):
                    d = sum(DSA_PER_PAIR[:p]) + taken_[0]
                    u = P1_AT[("dsa", d)]
                    act.wait_ge(unit_done, u + 1)
                    act.activation(DQ[:, d, :], PG[:, u % BANKS, 0:T], ACT.Copy).then_inc(free_bank(u), 1)
                    taken_[0] += 1

            for p in range(MT):
                pair(p)

            def attention():
                act.wait_ge(DR.sem, DR.at(MT - 1, "out"))
                for n in range(16):
                    if n >= 4:
                        act.wait_ge(a_sum, n - 3)
                    act.activation(SQ[:, n % 4, :], DQ[:, 9 + n, :], ACT.Square).then_inc(a_sq, 1)
                for g in range(4):
                    act.wait_ge(a_ms, 4 * g + 4)
                    link(act.activation(MSB[:, 4 * g:4 * g + 4, :], MSB[:, 4 * g:4 * g + 4, :], ACT.Ln))
                    act.activation(MSB[:, 4 * g:4 * g + 4, :], MSB[:, 4 * g:4 * g + 4, :], ACT.Exp,
                                   scale=-0.5).then_inc(a_rs, 1)
                for g in range(4):
                    act.wait_ge(a_vt, g + 1)
                    c = 4 * (g % 2) * P
                    act.activation(VTOK[:, g // 2, c:c + 4 * P], PX[:, g % 2, :], ACT.Copy).then_inc(a_v, 1)
                act.wait_ge(a_vt, 5)
                act.activation(WX, PX[:, 2, 0:T].rearrange("p (tt n) -> p tt n", tt=TT)[:, :, 32:32 + IDX_HEADS],
                               ACT.Copy, scale=IDX_HEADS ** -0.5 * 64 ** -0.5).then_inc(a_v, 1)
                for n in range(TT * IDX_HEADS):
                    keys = (n // IDX_HEADS + 1) * P
                    act.wait_ge(a_is, n + 1)
                    if n >= 4:
                        act.wait_ge(a_acc, n - 3)
                    act.activation(RL[:, n % 4, 0:keys], PX[:, n % 4, 0:keys], ACT.Relu).then_inc(a_relu, 1)
                for n in range(17):
                    if n < 16:
                        keys = (n // MT + 1) * P
                        act.wait_ge(a_l, n + 1)
                        if n >= 2:
                            act.wait_ge(a_t, n - 1)
                        act.activation(PR_[:, n % 2, 0:keys], LG[:, n % 2, 0:keys], ACT.Exp, bias=NMX[:, n:n + 1],
                                       accum_out=SUM[:, n:n + 1]).then_inc(a_ex, 1)
                    if n >= 1:
                        m = n - 1
                        keys = (m // MT + 1) * P
                        act.wait_ge(a_t, m + 1)
                        if m >= 2:
                            act.wait_ge(a_pv, m - 1)
                        act.activation(PT_[:, m % 2, 0:keys], PX[:, 2, 0:keys], ACT.Copy).then_inc(a_pt, 1)

            if on("dsa"):
                attention()
            if on("moe"):
                act.dma_start(ROUTE, A["route"].rearrange("p (k n) -> p k n", k=KT)).then_inc(s_route_in, 16)
                norm(1, lambda k: wait_taken(act, B0["wo"] + k))
                act.wait_ge(s_router, 4)
                act.activation(G2, G1, ACT.Exp).then_inc(s_rexp, 1)
                act.wait_ge(s_router, 13)
                act.activation(E2, E1, ACT.Exp).then_inc(s_rexp, 1)
                act.wait_ge(s_cbt, 1)
                act.activation(CT[0:32, :], PX[0:32, 2, 0:T], ACT.Copy).then_inc(s_cbb, 1)
                for e in range(NE):
                    act.wait_ge(s_cbt, e + 2)
                    act.activation(COMB[:, e, :], PX[:, e % 4, 0:T], ACT.Copy).then_inc(s_comb, 1)
                with act.Fori(0, NE // 2) as i:
                    for e in range(2):
                        for j in range(4):
                            u, use = U0["moe"] + e * MOE_UNITS + 2 * j, B0["moe"] + e * MOE_USES + 2 * j
                            act.wait_ge(unit_done, i * 24 + (u + 1))
                            act.wait_ge(s_he, i * 8 + (4 * e + j + 1))
                            act.activation(SG[:, j % 2, :], PG[:, use % BANKS, 0:T], ACT.Silu) \
                               .then_inc(free_bank(use), 1)

            if on("p2"):
                act.wait_ge(free_bank(0), B0["p2"] // BANKS)
                act.wait_ge(s_he, 2 + 4 * NE)
                act.dma_start(S5B, A["s5_b"].rearrange("p (c i n) -> p c i n", c=2, i=S5_TILES)).then_inc(c_par, 16)
                act.dma_start(S5C, A["s5_c"].rearrange("p (c i n) -> p c i n", c=2, i=S5_TILES)).then_inc(c_par, 16)
                act.dma_start(SPAT, A["spatial"].rearrange("p (m n) -> p m n", m=MT)).then_inc(g_in, 16)
                act.dma_start(SPAT_B[0:1, :], A["spatial_b"]).then_inc(g_in, 16)
                norm(2, lambda k: wait_taken(act, B0["p2"] - 8 + k // 2))
                v = lambda name: V[:, VEC[name][0]:VEC[name][1]]
                act.activation(S_DT, v("log_dt"), ACT.Exp).then_inc(c_act, 1)
                act.wait_ge(c_dve, 1)
                act.activation(S_MAG, S_LR, ACT.Exp)
                act.activation(S_SIN, S_R, ACT.Sin)
                act.activation(S_COS, S_R, ACT.Sin, scale=0.5).then_inc(c_act, 1)
                act.wait_ge(c_par, 32)
                act.wait_ge(c_zero, 1)
                for c in range(2):
                    for h in range(2):
                        act.activation(CD[64 * h:64 * h + 64, c, :, 16 * h:16 * h + 16],
                                       S5C[64 * h:64 * h + 64, c, :, :], ACT.Copy,
                                       scale=(1.0, -1.0)[c]).then_inc(c_cd, 1)
                for n in range(48):
                    u, use = U0["p2"] + n, B0["p2"] + n
                    act.wait_ge(unit_done, u + 1)
                    dst = S5IN[:, n, :] if n < 8 else UV[:, n - 8, :] if n < 24 else QKV[:, n - 24, :]
                    act.activation(dst, PG[:, use % BANKS, 0:T], ACT.Gelu_apprx_tanh if 8 <= n < 24 else ACT.Copy) \
                       .then_inc(free_bank(use), 1)
                    if n == 22:
                        act.wait_ge(c_turn, 1)
                        for q in range(4):
                            act.activation(LB[:, q // 2, 4 * (q % 2):4 * (q % 2) + 4, :],
                                           PX[:, q, :].rearrange("p (m n) -> p m n", m=4), ACT.Copy).then_inc(c_lb, 1)
                    if n >= 24 and n % 3 == 2:
                        b = (n - 24) // 3
                        act.wait_ge(c_yd, b + 1)
                        act.activation(S5IN[:, b, :], S5IN[:, b, :], ACT.Gelu_apprx_tanh).then_inc(c_g, 1)

            def gate_event(g):
                if g == 0:
                    for k in range(MT):
                        if k >= 4:
                            act.wait_ge(g_sum, k - 3)
                        act.activation(SQ[:, k % 4, :], UV[:, MT + k, :], ACT.Square).then_inc(g_sq, 1)
                    act.wait_ge(g_ms, 1)
                    act.activation(RS[:, :], RS[:, :], ACT.Sqrt).then_inc(g_rt, 1)
                elif g in (2, 3):
                    for q in range(4):
                        act.wait_ge(g_t, 4 * (g - 2) + q + 1)
                        dst = (GVT, AVT)[g - 2]
                        act.activation(dst[:, q // 2, 4 * P * (q % 2):4 * P * (q % 2) + 4 * P], PX[:, q, :],
                                       ACT.Copy).then_inc(g_tt, 1)
                for h in range(MT):
                    if g == 6 + 2 * h:
                        z, l = ZS[:, h % 2, :], LN_[:, h % 2, :]
                        act.wait_ge(b_z, h + 1)
                        if h >= 2:
                            act.wait_ge(b_w, h - 1)
                        link(act.activation(z, PX[:, 0, 0:384], ACT.Copy, scale=P ** -0.5))
                        link(act.activation(l, z, ACT.Abs))
                        link(act.activation(l, l, ACT.Exp, scale=-1.0))
                        act.activation(l, l, ACT.Ln, bias=1.0).then_inc(b_l, 1)
                    if g == 7 + 2 * h:
                        act.wait_ge(b_w, h + 1)
                        act.activation(WW[:, h % 2, :], WW[:, h % 2, :], ACT.Exp).then_inc(b_e, 1)

            if on("mix2"):
                for g in range(48):
                    use = B0["p2"] + 48 + g
                    act.wait_ge(unit_done, U0["p2"] + 48 + g + 1)
                    if g == 0:
                        act.wait_ge(c_yd, MT)
                    if g == 36:
                        act.wait_ge(b_y, MT)
                    act.activation(GT[:, g, :], PG[:, use % BANKS, 0:T], ACT.Sigmoid, bias=vec("b_gate", g)) \
                       .then_inc(free_bank(use), 1)
                    gate_event(g)
                for j in range(4):
                    use = B0["glu"] + j
                    act.wait_ge(unit_done, U0["glu"] + j + 1)
                    if j >= 2:
                        act.wait_ge(s_yb, j - 1)
                    act.activation(SQ[:, 2 * (j % 2), :], PG[:, use % BANKS, 0:T], ACT.Sigmoid, bias=vec("b_glu", 2 * j))
                    act.activation(SQ[:, 2 * (j % 2) + 1, :], PG[:, use % BANKS, T:2 * T], ACT.Sigmoid,
                                   bias=vec("b_glu", 2 * j + 1)).then_inc(free_bank(use), 1)
            if on("mlp"):
                norm(3, lambda k: wait_taken(act, B0["wo2"] + k))
                with act.Fori(0, 4) as i:
                    for t in range(KT):
                        use = B0["mlp"] + t
                        act.wait_ge(unit_done, i * 32 + (U0["mlp"] + t + 1))
                        if t >= 2:
                            wait_taken(act, use - 2, i * 8)
                        act.activation(SQ[:, t % 2, :], PG[:, use % BANKS, 0:T], ACT.Relu).then_inc(s_relu, 1)
                norm(4, lambda k: wait_taken(act, B0["mlp"] + 112 + k))

        @block.vector
        def _(dve):
            n_chain = [0]

            def link(ins):
                n_chain[0] += 1
                ins.then_inc(dve_chain, 1)
                dve.wait_ge(dve_chain, n_chain[0])

            dve.memset(MBF[:, :, 0:1], 0.0)
            dve.memset(W_, 0.0)
            dve.memset(U_, 0.0).then_inc(s_zero, 1)
            dve.wait_ge(s_vec, 16)
            a, b = VEC["w0"][0], VEC["mu"][0]
            dve.tensor_scalar(NEGS[:, 0:8], V[:, a:a + 8], -1.0, None, ALU.mult).then_inc(s_vprep, 1)
            a = VEC["a0"][0]
            dve.tensor_scalar(NEGS[:, 8:16], V[:, a:a + 8], -1.0, None, ALU.mult).then_inc(s_vprep, 1)
            dve.tensor_scalar(ONEMU[:, :], V[:, b:b + 27], -1.0, 1.0, ALU.mult, ALU.add).then_inc(s_vprep, 1)
            a = VEC["k_a"][0]
            dve.tensor_scalar(ONEKA[:, :], V[:, a:a + 8], -1.0, 1.0, ALU.mult, ALU.add).then_inc(s_vprep, 1)
            dve.wait_ge(s_vprep, 4)

            def norm(n, gain, dst=HT):
                dve.wait_ge(s_squsd, KT * (n + 1))
                dve.tensor_scalar(RS[:, :], PX[:, 0, 0:T], 1.0 / D, 1e-6, ALU.mult, ALU.add).then_inc(s_ms, 1)
                dve.wait_ge(s_rt, n + 1)
                link(dve.reciprocal(RS[:, :], RS[:, :]))
                for k in range(KT):
                    dve.scalar_tensor_tensor(dst[:, k, :], XT[:, k, :], vec(gain, k), RS[:, :], ALU.mult,
                                             ALU.mult).then_inc(s_h, 1)

            norm(0, "g_mix")

            def mix(what, dst):
                m, u = MIX_ORDER.index(what), P1_AT[what]
                c = MU_COL[what]
                dve.wait_ge(s_mixed, m + 1)
                dve.scalar_tensor_tensor(dst, PG[:, u % BANKS, 0:T], ONEMU[:, c:c + 1], MBF[:, m % 3, 0:T],
                                         ALU.mult, ALU.add).then_inc(free_bank(u), 1)

            for m in range(3):
                mix(("misc", m), LO[:, m, :])
            dve.wait_ge(s_lo_act, 3)
            dve.tensor_scalar(LO[:, 1, :], LO[:, 1, :], 0.5, 0.5, ALU.mult, ALU.add).then_inc(s_lo_dve, 1)
            dve.tensor_scalar(LO[0:32, 2, :], LO[0:32, 2, :], 0.5, 0.5, ALU.mult, ALU.add).then_inc(s_lo_dve, 1)

            def pair(p):
                pe = lambda name: dve.wait_ge(PR.sem, PR.at(p, name))
                act = lambda name: dve.wait_ge(AR_.sem, AR_.at(p, name))

                def done(ins, name):
                    ins.then_inc(DR.sem, DR.step(p, name))

                def me(name):
                    dve.wait_ge(DR.sem, DR.at(p, name))

                mix(("r", p), R_)
                mix(("k", p), K_)
                mix(("v", p), V_)
                v = P1_AT[("v", p)]
                dve.wait_ge(free_bank(v), v // BANKS + 1)
                done(dve.memset(ZB[:, 0, :], 0.0), "k")
                act("lora")
                dve.tensor_scalar(EW, EW, 1.0, None, ALU.add)
                link(dve.tensor_scalar(EA, EA, 1.0, None, ALU.add))
                dve.reciprocal(EW, EW)
                link(dve.reciprocal(EA, EA))
                link(dve.tensor_tensor_scan(CS, con("reset"), EW, 0.0, ALU.mult, ALU.add))
                done(dve.tensor_tensor(CP, CS, EW, ALU.subtract), "cum")
                pe("kks")
                done(dve.tensor_scalar(RN, PX[:, 3, 0:T], 1e-24, None, ALU.max), "kmax")
                link(dve.tensor_scalar(AM, EA, vec("k_a", p), ONEKA[:, p:p + 1], ALU.mult, ALU.add))
                link(dve.tensor_tensor(KM, K_, AM, ALU.mult))
                done(dve.scalar_tensor_tensor(AM, R_, vec("r_k", p), KM, ALU.mult, ALU.mult), "rk")
                act("rn")
                link(dve.scalar_tensor_tensor(RN, K_, vec("k_k", p), RN, ALU.mult, ALU.mult))
                link(dve.tensor_tensor(EA, RN, EA, ALU.mult))
                act("exps")
                a3 = lambda a: a.rearrange("p (tt n) -> p tt n", tt=TT)
                dve.scalar_tensor_tensor(AR[:, :, 0, :], a3(RN), -1.0, a3(PPREV), ALU.mult, ALU.mult)
                dve.tensor_tensor(AR[:, :, 1, :], a3(R_), a3(PIN), ALU.mult)
                dve.tensor_tensor(BT_, EA, PINV, ALU.mult)
                done(dve.tensor_tensor(KT_, KM, PINV, ALU.mult), "tilde")
                pe("tok")
                done(dve.tensor_tensor(BON, PX[:, 3, T:2 * T], V_, ALU.mult), "bon")
                pe("sco")
                c0 = CON["up_strict64"][0]
                m4 = C[:, c0:c0 + 2 * P].rearrange("p (o n) -> p o n", o=1).to_broadcast([P, TT, 2 * P])
                for h in range(2):
                    ins = dve.tensor_tensor(MBK[:, h, :, :, :].rearrange("p tt a n -> p tt (a n)"),
                                            PX[:, 2 + h, :].rearrange("p (tt n) -> p tt n", tt=TT), m4, ALU.mult)
                done(ins, "mb")
                me("mb")
                bc = lambda name: con(name).rearrange("p (o n) -> p o n", o=1).to_broadcast([P, 4, P])
                mbt = MBK[:, :, :, 0, :].rearrange("p h tt n -> p (h tt) n")
                link(dve.tensor_tensor(DT, mbt, bc("up_diag16"), ALU.mult))
                dve.tensor_tensor(Q_, DT, bc("ident"), ALU.add)
                act("mab")
                dve.tensor_tensor(EE, MAB, bc("lo_in32"), ALU.mult)
                dve.tensor_tensor(FF, MAB, bc("lo_in64"), ALU.mult)
                done(dve.tensor_tensor(DA, MAB, bc("lo_diag16"), ALU.mult), "dq")
                pe("ksco")
                for h in range(2):
                    ins = dve.tensor_tensor(MKK[:, h, :, :, :].rearrange("p tt a n -> p tt (a n)"),
                                            PX[:, 2 + h, :].rearrange("p (tt n) -> p tt n", tt=TT), m4, ALU.mult)
                done(ins, "mk")
                bank = lambda b: PX[:, b, :].rearrange("p (n a) -> p n a", n=4)
                pe("sq2")
                done(dve.tensor_copy(D2T, bank(1)), "d2t")
                pe("sq4")
                done(dve.tensor_tensor(Q_, Q_, bank(2), ALU.add), "q1")
                pe("sq8")
                me("q1")
                done(dve.tensor_tensor(Q_, Q_, bank(3), ALU.add), "q2")
                pe("inv16")
                me("q2")
                done(dve.tensor_tensor(Q_, Q_, bank(2), ALU.add), "q16")
                for t, b in (("16", 3), ("32", 2)):
                    pe("t" + t)
                    done(dve.tensor_copy(GM, bank(1)), "g" + t)
                    nxt = "32" if t == "16" else "64"
                    pe("inv" + nxt)
                    done(dve.tensor_tensor(Q_, Q_, bank(b), ALU.add), "q" + nxt)
                for c in range(NCH):
                    end = c * CH + CH - 1
                    pc = PIN[:, end:end + 1]
                    if c:
                        me(f"z{c - 1}")
                    dve.tensor_scalar(ZP, ZB[:, c % 2, :], pc, None, ALU.mult)
                    pe(f"Z{c}")
                    link(dve.scalar_tensor_tensor(ZT, PX[:, 2, 0:P], pc, con("head64"), ALU.mult, ALU.mult))
                    done(dve.tensor_tensor(ZB[:, (c + 1) % 2, :], ZT, ZP, ALU.add), f"z{c}")
                pe("gn1")
                done(dve.scalar_tensor_tensor(YC, PX[:, 0, 0:T], -1.0 / 64, Y_, ALU.mult, ALU.add), "yc")
                pe("gn2")
                done(dve.tensor_scalar(GRS, PX[:, 1, 0:T], 1.0 / 64, 64e-5, ALU.mult, ALU.add), "var")
                act("grs")
                link(dve.scalar_tensor_tensor(YC, YC, vec("ln_w", p), GRS, ALU.mult, ALU.mult))
                link(dve.scalar_tensor_tensor(YC, YC, vec("ln_b", p), BON, ALU.add, ALU.add))
                done(dve.tensor_tensor(YT[:, MT + p, :], YC, G_, ALU.mult), "out")

            for p in range(MT):
                pair(p)

            def attention():
                for n in range(16):
                    dve.wait_ge(a_sum, n + 1)
                    dve.tensor_scalar(MSB[:, n, :], PX[:, n % 2, 0:T], 1.0 / P, 1e-6, ALU.mult,
                                      ALU.add).then_inc(a_ms, 1)

                def normed(r):
                    n = r - 9
                    if n % 4 == 0:
                        dve.wait_ge(a_rs, n // 4 + 1)
                    dve.scalar_tensor_tensor(DQ[:, r, :], DQ[:, r, :], vec("q_gain" if n < 8 else "k_gain"),
                                             MSB[:, n, :], ALU.mult, ALU.mult).then_inc(a_nrm, 1)

                for r in range(25):
                    if 9 <= r + 1 < 25:
                        normed(r + 1)
                    dve.wait_ge(a_rot, r + 1)
                    link(dve.tensor_tensor(ROPE_S[:, r % 2, :], PX[:, 2 + r % 2, 0:T],
                                           con("sin64" if r < 9 else "sin128"), ALU.mult))
                    dve.wait_ge(a_cos, r + 1)
                    dve.tensor_tensor(DQ[:, r, :], ROPE_S[:, r % 2, :], ROPE_C[:, r % 4, :], ALU.add) \
                       .then_inc(a_rope, 1)
                dve.wait_ge(a_v, 5)
                for tt in range(TT):
                    keys = (tt + 1) * P
                    sc = ISC[:, tt, 0:keys]
                    for h in range(IDX_HEADS):
                        n = tt * IDX_HEADS + h
                        dve.wait_ge(a_relu, n + 1)
                        w = WX[:, tt, h:h + 1]
                        if h == 0:
                            dve.tensor_scalar(sc, RL[:, n % 4, 0:keys], w, None, ALU.mult).then_inc(a_acc, 1)
                        else:
                            dve.scalar_tensor_tensor(sc, RL[:, n % 4, 0:keys], w, sc, ALU.mult, ALU.add) \
                               .then_inc(a_acc, 1)
                        dve.wait_ge(a_acc, n + 1)
                    link(dve.memset(ISC[0:CH, tt, keys - CH:keys], NEG))
                    for n in range(TOP_K // 8):
                        link(dve.max(TOP8, sc))
                        link(dve.match_replace(out=sc, in_to_replace=TOP8, in_values=sc, imm_value=-3.0e38))
                    dve.tensor_scalar(BIAS[:, tt, 0:keys], sc, -2.0e38, NEG, ALU.is_gt, ALU.mult).then_inc(a_bias, 1)
                dve.wait_ge(a_bias, 2)
                for n in range(18):
                    if n < 16:
                        tt = n // MT
                        keys = (tt + 1) * P
                        dve.wait_ge(a_lg, n + 1)
                        if n >= 2:
                            dve.wait_ge(a_ex, n - 1)
                        link(dve.tensor_tensor_reduce(LG[:, n % 2, 0:keys], PX[:, n % 2, 0:keys], BIAS[:, tt, 0:keys],
                                                      P ** -0.5, -3.0e38, ALU.add, ALU.max, MX[:, n:n + 1]))
                        dve.tensor_scalar(NMX[:, n:n + 1], MX[:, n:n + 1], -1.0, None, ALU.mult).then_inc(a_l, 1)
                    if 1 <= n < 17:
                        m = n - 1
                        keys = (m // MT + 1) * P
                        dve.wait_ge(a_ex, m + 1)
                        link(dve.reciprocal(RSUM[:, m:m + 1], SUM[:, m:m + 1]))
                        dve.tensor_scalar(PR_[:, m % 2, 0:keys], PR_[:, m % 2, 0:keys], RSUM[:, m:m + 1], None,
                                          ALU.mult).then_inc(a_p, 1)
                    if n >= 2:
                        m = n - 2
                        dve.wait_ge(a_pv, m + 1)
                        dve.tensor_copy(YT[:, m % MT, (m // MT) * P:(m // MT) * P + P], PX[:, 3, 0:P]).then_inc(a_y, 1)

            if on("dsa"):
                attention()

            def add_tile(u, use, t):
                dve.wait_ge(unit_done, u + 1)
                dve.tensor_tensor(XT[:, t, :], XT[:, t, :], PG[:, use % BANKS, 0:T], ALU.add).then_inc(free_bank(use), 1)

            if on("wo"):
                for t in range(KT):
                    add_tile(U0["wo"] + t, B0["wo"] + t, t)
                if upto == "wo":
                    wait_taken(dve, B0["wo"] + 15)
                    dve.memset(RS[:, :], 0.0).then_inc(s_end, 1)

            def router():
                n_done = [0]

                def do(ins):
                    n_done[0] += 1
                    ins.then_inc(s_router, 1)
                    dve.wait_ge(s_router, n_done[0])

                b = lambda a, n: a.rearrange("p (t o) -> p t o", o=1).to_broadcast([P, TT, n])
                br = V[:, VEC["b_route"][0]:VEC["b_route"][1]].rearrange("p (o n) -> p o n", o=1) \
                    .to_broadcast([P, TT, 20])
                rank = lambda n: con("rank")[:, 0:n].rearrange("p (o n) -> p o n", o=1).to_broadcast([P, TT, n])
                do(dve.memset(CB, 0.0))
                dve.wait_ge(s_lgt, 1)
                do(dve.tensor_tensor(LGT, PX[:, 1, 0:64].rearrange("p (t n) -> p t n", t=TT)[:, :, 0:20], br, ALU.add))
                grp = LGT[:, :, 0:NG]
                do(dve.tensor_reduce(m1, grp, AX_X, ALU.max))
                do(dve.tensor_tensor(G1, grp, b(m1, NG), ALU.subtract))
                do(dve.tensor_tensor(G3, grp, b(m1, NG), ALU.is_equal))
                do(dve.tensor_tensor(G3, G3, rank(NG), ALU.mult))
                do(dve.tensor_reduce(m2, G3, AX_X, ALU.max))
                do(dve.tensor_tensor(GO, G3, b(m2, NG), ALU.is_equal))
                do(dve.tensor_scalar(GO, GO, -NEG, NEG, ALU.mult, ALU.add))
                for t in range(TT):
                    ins = dve.tensor_tensor(E1[:, t, :].rearrange("p (g e) -> p g e", g=NG),
                                            LGT[:, t, NG:20].rearrange("p (g e) -> p g e", g=NG),
                                            GO[:, t, :].rearrange("p (g o) -> p g o", o=1)
                                            .to_broadcast([P, NG, EPG]), ALU.add)
                    do(ins)
                do(dve.tensor_reduce(m3, E1, AX_X, ALU.max))
                do(dve.tensor_tensor(E1, E1, b(m3, NE), ALU.subtract))
                assert n_done[0] == 13
                dve.wait_ge(s_rexp, 2)
                do(dve.tensor_reduce(pg, G2, AX_X, ALU.add))
                for v, o in ((v0, O0), (v1, O1)):
                    do(dve.tensor_reduce(v, E2, AX_X, ALU.max))
                    do(dve.tensor_tensor(E3, E2, b(v, NE), ALU.is_equal))
                    do(dve.tensor_tensor(E3, E3, rank(NE), ALU.mult))
                    do(dve.tensor_reduce(m2, E3, AX_X, ALU.max))
                    do(dve.tensor_tensor(o, E3, b(m2, NE), ALU.is_equal))
                    do(dve.scalar_tensor_tensor(E2, o, -4.0, E2, ALU.mult, ALU.add))
                    do(dve.tensor_tensor(o, o, b(v, NE), ALU.mult))
                do(dve.tensor_tensor(vs, v0, v1, ALU.add))
                do(dve.tensor_tensor(vs, vs, pg, ALU.mult))
                do(dve.reciprocal(vs, vs))
                do(dve.tensor_tensor(O0, O0, O1, ALU.add))
                do(dve.tensor_tensor(CB[:, :, 0:NE], O0, b(vs, NE), ALU.mult))
                assert n_done[0] == R_DONE, n_done[0]

            if on("moe"):
                norm(1, "g_ffn")
                router()
                dve.memset(UP[:, 0, :], 0.0).then_inc(s_he, 1)
                dve.memset(UP[:, 1, :], 0.0).then_inc(s_he, 1)
                dve.wait_ge(s_he, 2)
                with dve.Fori(0, NE // 2) as i:
                    for e in range(2):
                        u, use = U0["moe"] + e * MOE_UNITS, B0["moe"] + e * MOE_USES
                        for j in range(4):
                            dve.wait_ge(unit_done, i * 24 + (u + 2 * j + 2))
                            if e == 0 and j == 0:
                                dve.wait_ge(s_comb, NE)
                            dve.tensor_tensor(UP[:, j % 2, :], PG[:, (use + 2 * j + 1) % BANKS, 0:T],
                                              COMB[:, bass.ds(i * 2 + e, 1), :].rearrange("p o t -> p (o t)"),
                                              ALU.mult).then_inc(free_bank(use + 2 * j + 1), 1)
                            wait_taken(dve, use + 2 * j + 1, i * 8)
                            wait_taken(dve, use + 2 * j, i * 8)
                            dve.tensor_tensor(HE[:, e, j, :], UP[:, j % 2, :], SG[:, j % 2, :], ALU.mult) \
                               .then_inc(s_he, 1)
                        for d in range(4):
                            dve.wait_ge(unit_done, i * 24 + (u + 8 + d + 1))
                            for half in range(2):
                                x = XT[:, 4 * d + 2 * half:4 * d + 2 * half + 2, :].rearrange("p a t -> p (a t)")
                                b = use + 8 + 2 * d + half
                                dve.tensor_tensor(x, x, PG[:, b % BANKS, :], ALU.add).then_inc(free_bank(b), 1)
                if upto == "moe":
                    dve.wait_ge(free_bank(0), B0["p2"] // BANKS)
                    for b in range(1, 4):
                        dve.wait_ge(free_bank(b), B0["p2"] // BANKS)
                    dve.memset(RS[:, :], 0.0).then_inc(s_end, 1)

            def s5_parameters():
                v = lambda name: V[:, VEC[name][0]:VEC[name][1]]
                tt, ts = dve.tensor_tensor, dve.tensor_scalar
                dve.wait_ge(c_act, 1)
                tt(S_LR, v("lam_re"), S_DT, ALU.mult)
                link(tt(S_TH, v("lam_im"), S_DT, ALU.mult))
                link(ts(S_N, S_TH, float(np.float32(1 / (2 * np.pi))), 12582912.0, ALU.mult, ALU.add))
                link(ts(S_N, S_N, -12582912.0, None, ALU.add))
                src = S_TH
                for part in (6.28125, 0.0019350051879882812, 3.019915981956753e-07):
                    link(dve.scalar_tensor_tensor(S_R, S_N, -part, src, ALU.mult, ALU.add))
                    src = S_R
                ts(S_R, S_R, 3.1415925, -3.1415925, ALU.min, ALU.max).then_inc(c_dve, 1)
                dve.memset(CD, 0.0)
                dve.memset(BBD, 0.0).then_inc(c_zero, 1)
                dve.wait_ge(c_act, 2)
                link(tt(S_COS, S_COS, S_COS, ALU.mult))
                link(ts(S_COS, S_COS, -2.0, 1.0, ALU.mult, ALU.add))
                tt(S_ABR, S_MAG, S_COS, ALU.mult)
                link(tt(S_ABI, S_MAG, S_SIN, ALU.mult))
                ts(S_ABR, S_ABR, -1.0, None, ALU.add)
                tt(S_A, v("lam_re"), v("lam_re"), ALU.mult)
                link(tt(S_B, v("lam_im"), v("lam_im"), ALU.mult))
                link(tt(S_DEN, S_A, S_B, ALU.add))
                dve.reciprocal(S_DEN, S_DEN)
                tt(S_A, S_ABR, v("lam_re"), ALU.mult)
                link(tt(S_B, S_ABI, v("lam_im"), ALU.mult))
                link(tt(S_KR, S_A, S_B, ALU.add))
                tt(S_A, S_ABI, v("lam_re"), ALU.mult)
                link(tt(S_B, S_ABR, v("lam_im"), ALU.mult))
                link(tt(S_KI, S_A, S_B, ALU.subtract))
                tt(S_KR, S_KR, S_DEN, ALU.mult)
                link(tt(S_KI, S_KI, S_DEN, ALU.mult))
                dve.wait_ge(c_par, 32)
                dve.wait_ge(c_zero, 1)
                wide = lambda a: a.rearrange("p (i o) -> p i o", o=1).to_broadcast([P, S5_TILES, 16])
                a4 = lambda n: PB[:, n, :].rearrange("p (i n) -> p i n", i=S5_TILES)
                br, bi = S5B[:, 0, :, :], S5B[:, 1, :, :]
                tt(a4(0), br, wide(S_KR), ALU.mult)
                tt(a4(1), bi, wide(S_KI), ALU.mult)
                tt(a4(2), bi, wide(S_KR), ALU.mult)
                link(tt(a4(3), br, wide(S_KI), ALU.mult))
                for h in range(2):
                    hs, cs = slice(64 * h, 64 * h + 64), slice(16 * h, 16 * h + 16)
                    tt(BBD[hs, 0, :, cs], a4(0)[hs], a4(1)[hs], ALU.subtract)
                    ins = tt(BBD[hs, 1, :, cs], a4(2)[hs], a4(3)[hs], ALU.add)
                ins.then_inc(c_dve, 1)

            def s5_scan(b):
                tt = dve.tensor_tensor
                w = lambda a: a.rearrange("p (i t) -> p i t", i=4)
                bu = lambda c: PX[:, :, c * T:c * T + T]
                er, ei = w(ROT[:, b % 2, 0, :]), w(ROT[:, b % 2, 1, :])
                x0, x1, t0, t1 = w(XR[:, 0, :]), w(XR[:, 1, :]), w(TR[:, 0, :]), w(TR[:, 1, :])
                dve.wait_ge(c_bu, b + 1)
                dve.wait_ge(c_tab, b + 1)
                if b == 0:
                    dve.wait_ge(c_lb, 4)
                    dve.wait_ge(c_cd, 4)
                tt(x0, bu(0), er, ALU.mult)
                tt(t0, bu(1), ei, ALU.mult)
                tt(x1, bu(1), er, ALU.mult)
                link(tt(t1, bu(0), ei, ALU.mult))
                tt(x0, x0, t0, ALU.add)
                tt(x1, x1, t1, ALU.subtract).then_inc(c_x, 1)
                dve.wait_ge(c_x, b + 1)
                for i in range(4):
                    mag = S_MAG[:, 4 * b + i:4 * b + i + 1].to_broadcast([P, T])
                    for x in (x0, x1):
                        ins = dve.tensor_tensor_scan(x[:, i, :], mag, x[:, i, :], 0.0, ALU.mult, ALU.add)
                link(ins)
                tt(t0, x0, er, ALU.mult)
                link(tt(t1, x1, ei, ALU.mult))
                link(tt(t0, t0, t1, ALU.subtract))
                tt(t1, x0, ei, ALU.mult)
                link(tt(x1, x1, er, ALU.mult))
                tt(x1, x1, t1, ALU.add).then_inc(c_s, 1)
                dve.wait_ge(c_y, b + 1)
                dve.scalar_tensor_tensor(S5IN[:, b, :], S5IN[:, b, :], vec("s5_d", b), PX[:, 0, 0:T], ALU.mult,
                                         ALU.add).then_inc(c_yd, 1)

            if on("p2"):
                norm(2, "norm1")
                s5_parameters()
                for b in range(MT):
                    s5_scan(b)

            if on("mix2"):
                dve.wait_ge(g_in, 32)
                link(dve.tensor_scalar(NEGM, con("up_strict"), -NEG, NEG, ALU.mult, ALU.add))
                dve.tensor_tensor(SPAT, SPAT, con("up_incl").rearrange("p (o n) -> p o n", o=1)
                                  .to_broadcast([P, MT, P]), ALU.mult)
                dve.wait_ge(g_sum, MT)
                dve.tensor_scalar(RS[:, :], PX[:, 0, 0:T], 1.0 / MIX, 1e-6, ALU.mult, ALU.add).then_inc(g_ms, 1)
                dve.wait_ge(g_rt, 1)
                link(dve.reciprocal(RS[:, :], RS[:, :]))
                for k in range(MT):
                    dve.scalar_tensor_tensor(UV[:, MT + k, :], UV[:, MT + k, :], vec("gm_norm", k), RS[:, :], ALU.mult,
                                             ALU.mult).then_inc(g_vn, 1)
                dve.wait_ge(g_mix, 1)
                for q in range(4):
                    u = UV[:, 2 * q:2 * q + 2, :].rearrange("p a t -> p (a t)")
                    dve.tensor_tensor(u, u, PX[:, q, :], ALU.mult).then_inc(g_y, 1)
                diag = lambda a: a.rearrange("p (b n) -> p b n", b=3)[:, 0:3:2, :]
                two = lambda a: a.rearrange("p (o n) -> p o n", o=1).to_broadcast([P, 2, P])
                for h in range(MT):
                    z, l, sp, w = (a[:, h % 2, :] for a in (ZS, LN_, SP_, WW))
                    dve.wait_ge(b_l, h + 1)
                    link(dve.scalar_tensor_tensor(sp, z, 0.0, l, ALU.max, ALU.add))
                    dve.tensor_tensor(diag(sp), diag(sp), two(con("up_strict")), ALU.mult).then_inc(b_sp, 1)
                    dve.wait_ge(b_r, h + 1)
                    if h >= 2:
                        dve.wait_ge(b_pv, h - 1)
                    link(dve.tensor_tensor(w, z, PX[:, 1, 0:384], ALU.subtract))
                    dve.tensor_tensor(diag(w), diag(w), two(NEGM), ALU.add).then_inc(b_w, 1)
                    dve.wait_ge(b_pv, h + 1)
                    dve.tensor_copy(QKV[:, h, :], PX[:, 2, 0:T]).then_inc(b_y, 1)
                for j in range(4):
                    wait_taken(dve, B0["glu"] + j)
                    dve.tensor_tensor(YB[:, 2 * j:2 * j + 2, :], S5IN[:, 2 * j:2 * j + 2, :],
                                      SQ[:, 2 * (j % 2):2 * (j % 2) + 2, :], ALU.mult).then_inc(s_yb, 1)
                if upto == "mix2":
                    dve.wait_ge(s_yb, 4)
                    dve.memset(RS[:, :], 0.0).then_inc(s_end, 1)
            if on("br"):
                dve.wait_ge(s_yb, 4)
                for n in range(3):
                    for j in range(8):
                        use = B0["br"] + 8 * n + j
                        m = HT[:, 2 * j:2 * j + 2, :].rearrange("p a t -> p (a t)")
                        gate = GT[:, n * KT + 2 * j:n * KT + 2 * j + 2, :].rearrange("p a t -> p (a t)")
                        dve.wait_ge(unit_done, U0["br"] + 8 * n + j + 1)
                        if n == 0:
                            dve.tensor_tensor(m, PG[:, use % BANKS, :], gate, ALU.mult).then_inc(free_bank(use), 1)
                        else:
                            link(dve.tensor_tensor(SQF[:, 0:2 * T], PG[:, use % BANKS, :], gate, ALU.mult))
                            dve.tensor_tensor(m, m, SQF[:, 0:2 * T], ALU.add).then_inc(free_bank(use), 1)
                            wait_taken(dve, use)
                for t in range(KT):
                    add_tile(U0["wo2"] + t, B0["wo2"] + t, t)
                if upto == "br":
                    wait_taken(dve, B0["wo2"] + 15)
                    dve.memset(RS[:, :], 0.0).then_inc(s_end, 1)
            if on("mlp"):
                norm(3, "norm2")
                with dve.Fori(0, 4) as i:
                    for t in range(KT):
                        use = B0["mlp"] + t
                        dve.wait_ge(s_relu, i * KT + (t + 1))
                        dve.scalar_tensor_tensor(HID[:, t, :], PG[:, use % BANKS, 0:T], 0.0, SQ[:, t % 2, :], ALU.max,
                                                 ALU.mult).then_inc(free_bank(use), 1)
                    for t in range(KT):
                        use = B0["mlp"] + KT + t
                        dve.wait_ge(unit_done, i * 32 + (U0["mlp"] + KT + t + 1))
                        dve.tensor_tensor(XT[:, t, :], XT[:, t, :], PG[:, use % BANKS, 0:T], ALU.add) \
                           .then_inc(free_bank(use), 1)
                norm(4, "final", YT)

        @block.gpsimd
        def _(pool):
            if on("dsa"):
                for r in range(25):
                    pool.wait_ge(a_sq, 1) if r < 9 else pool.wait_ge(a_nrm, r - 8)
                    if r >= 4:
                        pool.wait_ge(a_rope, r - 3)
                    pool.tensor_tensor(ROPE_C[:, r % 4, :], DQ[:, r, :], con("cos64" if r < 9 else "cos128"),
                                       ALU.mult).then_inc(a_cos, 1)
            if on("p2"):
                n_chain = [0]

                def link(ins):
                    n_chain[0] += 1
                    ins.then_inc(pool_chain, 1)
                    pool.wait_ge(pool_chain, n_chain[0])

                tt = pool.tensor_tensor
                pool.wait_ge(c_dve, 2)
                ar, ai, sr, si, tmp = PW
                p2 = [POW[:, f, c, :, :] for f in range(2) for c in range(2)]
                wide = lambda a, n: a.rearrange("p (i o) -> p i o", o=1).to_broadcast([P, S5_TILES, n])

                def square():
                    tt(sr, ar, ar, ALU.mult)
                    tt(si, ai, ai, ALU.mult)
                    link(tt(tmp, ar, ai, ALU.mult))
                    tt(ar, sr, si, ALU.subtract)
                    link(tt(ai, tmp, tmp, ALU.add))

                link(pool.tensor_copy(ar, S_COS))
                link(pool.tensor_copy(ai, S_SIN))
                for f in range(2):
                    re, im = POW[:, f, 0, :, :], POW[:, f, 1, :, :]
                    pool.memset(re[:, :, 0:1], 1.0)
                    link(pool.memset(im[:, :, 0:1], 0.0))
                    pool.tensor_copy(re[:, :, 1:2], ar.rearrange("p (i o) -> p i o", o=1))
                    link(pool.tensor_copy(im[:, :, 1:2], ai.rearrange("p (i o) -> p i o", o=1)))
                    for m in (2, 4, 8):
                        square()
                        t0 = PT2[:, 0, 0:S5_TILES * m].rearrange("p (i n) -> p i n", i=S5_TILES)
                        t1 = PT2[:, 1, 0:S5_TILES * m].rearrange("p (i n) -> p i n", i=S5_TILES)
                        tt(t0, re[:, :, 0:m], wide(ar, m), ALU.mult)
                        link(tt(t1, im[:, :, 0:m], wide(ai, m), ALU.mult))
                        link(tt(re[:, :, m:2 * m], t0, t1, ALU.subtract))
                        tt(t0, re[:, :, 0:m], wide(ai, m), ALU.mult)
                        link(tt(t1, im[:, :, 0:m], wide(ar, m), ALU.mult))
                        link(tt(im[:, :, m:2 * m], t0, t1, ALU.add))
                    square()
                for b in range(MT):
                    if b:
                        pool.wait_ge(c_tab, b)
                    for c in range(2):
                        for i in range(4):
                            i_ = 4 * b + i
                            J = lambda k: POW[:, 0, k, i_, :].rearrange("p (o n) -> p o n", o=1).to_broadcast([P, 16, 16])
                            F = lambda k: POW[:, 1, k, i_, :].rearrange("p (n o) -> p n o", o=1).to_broadcast([P, 16, 16])
                            o = lambda a: a[:, i * T:i * T + T].rearrange("p (c j) -> p c j", c=16)
                            if b >= 2 and c == 0 and i == 0:
                                pool.wait_ge(c_s, b - 1)
                            tt(o(ROT[:, b % 2, c, :]), J(0), F(c), ALU.mult)
                            ins = tt(o(PT2[:, 0, :]), J(1), F(1 - c), ALU.mult)
                        link(ins)
                        r = ROT[:, b % 2, c, :]
                        ins = tt(r, r, PT2[:, 0, :], ALU.subtract if c == 0 else ALU.add)
                        if c == 0:
                            link(ins)
                        else:
                            ins.then_inc(c_tab, 1)


DSA_COLS = (MIX, MIX, MIX, IDX_HEADS * 64, 64, IDX_HEADS)
RWKV_COLS = (MIX, 64, MIX, MIX, 64, 160)


def units(w, cols):
    k, n = w.shape
    return w.reshape(k // P, P, n // cols, cols).transpose(2, 1, 0, 3).reshape(n // cols, P, k // P * cols)


def by_feature(v):
    return v.reshape(-1, P).T


def lay_out(x):
    f = {k: np.asarray(v) for k, v in x.items()}
    w_in = f["w_in"][0]
    edges = np.cumsum((0,) + DSA_COLS + RWKV_COLS)
    q, k, v, qi, ki, wi, r, dw, kr, vr, da, dg = (w_in[:, a:b] for a, b in zip(edges[:-1], edges[1:]))
    pad = np.zeros((D, P - 48), np.float32)
    p1 = {"misc": np.concatenate([dw, da, dg[:, :P], dg[:, P:], wi, pad], 1), "r": r, "k": kr, "v": vr,
          "dsa": np.concatenate([ki, ki, qi, q, k, v], 1)}
    parts = [units(np.concatenate([p1[a][:, n * P:n * P + P] for a, n in P1_ORDER], 1), P), units(f["w_out"][0], P)]
    for e in range(NE):
        g, up, dn = f["w_e_gate"][0, e], f["w_e_up"][0, e], f["w_e_down"][0, e]
        parts.append(np.stack([units(g, P), units(up, P)], 1).reshape(8, P, UNIT))
        parts.append(units(dn, 4 * P))
    w2 = f["w_in_2"][0]
    parts.append(units(np.concatenate([w2[:, 2 * MIX:3 * MIX], w2[:, :2 * MIX], w2[:, 3 * MIX:]], 1), P))
    parts.append(units(f["s5_w_glu_2"][0], 2 * P))
    parts += [units(f["w_branch_2"][0, n], 2 * P) for n in range(3)]
    parts.append(units(f["w_out_2"][0], P))
    for b in range(4):
        parts.append(units(f["w_mlp_in_2"][0][:, b * D:(b + 1) * D], P))
        parts.append(units(f["w_mlp_out_2"][0][b * D:(b + 1) * D], P))
    weights = np.concatenate(parts, 0)
    assert weights.shape == (UNITS, P, UNIT), weights.shape

    mu = f["rwkv_shift_mix"][0]
    e2 = np.cumsum((0,) + RWKV_COLS)
    mr, mdw, mk, mv, mda, mdg = (mu[a:b] for a, b in zip(e2[:-1], e2[1:]))
    mu_cols = np.concatenate([mdw, mda, mdg, np.zeros(P - 32, np.float32), mr, mk, mv])
    states = lambda a: a.reshape(S5_TILES, P).T
    vectors = {"g_mix": f["g_mix"], "mu": mu_cols, "w0": f["w0"], "a0": f["a0"], "k_k": f["k_k"], "k_a": f["k_a"],
               "r_k": f["r_k"], "ln_w": f["ln_x_w"], "ln_b": f["ln_x_b"], "q_gain": f["q_gain"],
               "k_gain": f["k_gain"], "g_ffn": f["g_ffn"], "norm1": f["norm1_g_2"], "b_gate": f["b_gate_2"],
               "gm_norm": f["gm_norm_g_2"], "s5_d": f["s5_d_2"], "b_glu": f["s5_b_glu_2"], "norm2": f["norm2_g_2"],
               "final": f["final_g_2"], "lam_re": f["s5_lambda_re_2"], "lam_im": f["s5_lambda_im_2"],
               "log_dt": np.repeat(f["s5_log_dt_2"].reshape(-1), 64)}
    V = np.zeros((P, NV), np.float32)
    for name, a in vectors.items():
        V[:, VEC[name][0]:VEC[name][1]] = by_feature(a.reshape(-1))
    V[:, VEC["b_route"][0]:VEC["b_route"][1]] = np.concatenate([f["b_route_group"][0], f["b_route_expert"][0]])[None]

    gate_up = np.zeros((P, 2, MIX), np.float32)
    gate_up[:, 0] = f["w_gate_lora_up"][0, :P]
    gate_up[:32, 1] = f["w_gate_lora_up"][0, P:]
    state_rows = lambda a: a.reshape(S5_TILES, P, 16).transpose(1, 0, 2)
    route = np.concatenate([f["w_route_group"][0], f["w_route_expert"][0]], 1)
    return {
        "xT": f["x"][0].T.reshape(KT, P, T).transpose(1, 0, 2),
        "weights": weights, "vectors": V, "constants": constants(),
        "lora": np.concatenate([f["w_decay_up"][0], f["w_aicl_up"][0]], 0),
        "gate_up": gate_up.reshape(P, 2 * MIX),
        "route": route.reshape(KT, P, 20).transpose(1, 0, 2).reshape(P, KT * 20),
        "spatial": f["gm_w_s_2"][0].transpose(2, 0, 1).reshape(P, MT * P),
        "spatial_b": f["gm_b_s_2"][0].reshape(1, MT * P),
        "s5_b": np.stack([state_rows(f["s5_b_re_2"][0]), state_rows(f["s5_b_im_2"][0])], 1).reshape(P, -1),
        "s5_c": np.stack([state_rows(f["s5_c_re_2"][0].transpose(0, 2, 1)),
                          state_rows(f["s5_c_im_2"][0].transpose(0, 2, 1))], 1).reshape(P, -1),
    }


def kernel(**inputs):
    import concourse.bacc as bacc
    from concourse.bass_utils import run_bass_kernel_spmd as run

    nc = bacc.Bacc("TRN2", target_bir_lowering=False, num_devices=1)
    arrays = {k: np.ascontiguousarray(v) for k, v in lay_out(inputs).items()}
    A = {k: nc.dram_tensor(k, v.shape, F32, kind="ExternalInput").ap() for k, v in arrays.items()}
    out = nc.dram_tensor("result", (P, KT, T), F32, kind="ExternalOutput").ap()
    build(nc, A, out)
    r = run(nc, [arrays], core_ids=[0])
    return r.results[0]["result"].transpose(1, 0, 2).reshape(D, T).T.reshape(1, T, D)
```

```python
from contextlib import ExitStack

import numpy as np
import concourse.bass as bass
from concourse import mybir

F32 = mybir.dt.float32
F32R = mybir.dt.float32r
ALU = mybir.AluOpType
ACT = mybir.ActivationFunctionType
AX_X = mybir.AxisListType.X

P = 128
T = 256
D = 2048
KT = D // P
MIX = D // 2
MT = MIX // P
CH = 64
NCH = T // CH
TT = T // P
IDX_HEADS = 16
TOP_K = 64
NE, NG, EPG = 16, 4, 4
UNIT = 2048
RING = 4
WORK = 27600
PIECE = 2 * UNIT
BANKS = 4
S5_TILES = 32
NEG = -1.0e30
DECAY = float(np.exp(-0.5))

SECTIONS = [("p1", 60, 1), ("wo", 16, 1), ("moe", 192, 0), ("p2", 96, 1), ("glu", 4, 1),
            ("br", 24, 1), ("wo2", 16, 1), ("mlp", 128, 1)]
MOE_UNITS, MOE_USES = 12, 16


def offsets():
    u = use = 0
    first, uses = {}, {}
    for name, n, per in SECTIONS:
        first[name], uses[name] = u, use
        u += n
        use += NE * MOE_USES if name == "moe" else n * per
    return first, uses, u


U0, B0, UNITS = offsets()
R_DONE = 33

VEC = {}
_n = 0
for _name, _cols in [("g_mix", 16), ("mu", 27), ("w0", 8), ("a0", 8), ("k_k", 8), ("k_a", 8), ("r_k", 8),
                     ("ln_w", 8), ("ln_b", 8), ("q_gain", 1), ("k_gain", 1), ("g_ffn", 16),
                     ("norm1", 16), ("b_gate", 48), ("gm_norm", 8), ("s5_d", 8), ("b_glu", 8),
                     ("norm2", 16), ("final", 16), ("lam_re", 32), ("lam_im", 32), ("log_dt", 32),
                     ("b_route", 20)]:
    VEC[_name] = (_n, _n + _cols)
    _n += _cols
NV = _n

CON = {}
_n = 0
for _name, _cols in [("head64", 128), ("perm128", 128), ("perm64", 128), ("up_strict64", 128), ("up_incl64", 128),
                     ("lo_diag16", 128), ("up_diag16", 128), ("lo_in32", 128), ("lo_in64", 128), ("reset", 256),
                     ("cos128", 256), ("sin128", 256), ("cos64", 256), ("sin64", 256), ("ident", 128), ("ones", 128),
                     ("cum_after", 128), ("up_strict", 128), ("up_incl", 128), ("rank", 16)]:
    CON[_name] = (_n, _n + _cols)
    _n += _cols
NC = _n


def constants():
    c = np.zeros((P, NC), np.float32)

    def put(name, a):
        c[:, CON[name][0]:CON[name][1]] = a

    i, j = np.arange(P)[:, None], np.arange(P)[None, :]
    put("ident", i == j)
    put("ones", 1.0)
    put("head64", i // 64 == j // 64)
    for name, half in (("perm128", 64), ("perm64", 32)):
        low = j % (2 * half) < half
        put(name, np.where(low & (i == j + half), -1.0, 0.0) + np.where(~low & (i == j - half), 1.0, 0.0))
    same = lambda n: i // n == j // n
    put("up_strict64", same(64) & (i < j))
    put("up_incl64", same(64) & (i <= j))
    put("lo_diag16", same(16) & (i > j))
    put("up_diag16", same(16) & (i < j))
    put("lo_in32", same(32) & ~same(16) & (i > j))
    put("lo_in64", same(64) & ~same(32) & (i > j))
    put("cum_after", i >= j)
    put("up_strict", i < j)
    put("up_incl", i <= j)
    t = np.arange(T)
    put("reset", (t % CH != 0)[None, :])
    for n, half in ((128, 64), (64, 32)):
        inv = np.float32(10000.0) ** (-np.arange(half, dtype=np.float32) * np.float32(2.0 / n))
        ang = (t.astype(np.float32)[None, :] * inv[:, None].astype(np.float32)).astype(np.float64)
        put(f"cos{n}", np.tile(np.cos(ang), (P // half, 1)))
        put(f"sin{n}", np.tile(np.sin(ang), (P // half, 1)))
    put("rank", np.broadcast_to(16.0 - np.arange(16), (P, 16)))
    return c


class Steps:

    def __init__(self, sem, names):
        self.sem, self.names, self.taken = sem, names, 0

    def at(self, rnd, name):
        return rnd * len(self.names) + self.names.index(name) + 1

    def step(self, rnd, name):
        self.taken += 1
        assert self.taken == self.at(rnd, name), (rnd, name)
        return 1


S5_FIRST, S5_END = 21, 21 + 3 * MT

HEAD_AT = [7 + 7 * _h // 2 for _h in range(MT)]

DSA_TILES = 33
LATE = 6
DSA_PER_PAIR = [3] * 7 + [6]
P1_ORDER = [("misc", 0), ("misc", 1), ("misc", 2)]
for _p in range(MT):
    P1_ORDER += [("r", _p), ("k", _p), ("v", _p)]
    P1_ORDER += [("dsa", sum(DSA_PER_PAIR[:_p]) + _q) for _q in range(DSA_PER_PAIR[_p])]
P1_ORDER += [("dsa", _q) for _q in range(sum(DSA_PER_PAIR), DSA_TILES)]
P1_AT = {what: n for n, what in enumerate(P1_ORDER)}
V_UNIT = P1_AT[("dsa", DSA_TILES - LATE)]
MIX_ORDER = [what for what in P1_ORDER if what[0] != "dsa"]
MU_COL = {what: (what[1] if what[0] == "misc" else 3 + 8 * "rkv".index(what[0]) + what[1]) for what in MIX_ORDER}

PE_RW = ["lora", "kks", "tok", "sco", "ksco", "sq2", "sq4", "sq8", "inv16", "t16", "inv32", "t32", "inv64"] \
    + [f"{s}{c}" for c in range(NCH) for s in "WUZ"] + ["gn1", "gn2"]
ACT_RW = ["lora", "kk2", "rn", "exps", "tok", "mab", "d2", "d4", "d8", "t16", "t32"] \
    + [f"{s}{c}" for c in range(NCH) for s in "WU"] + ["y", "ysq", "grs"]
DVE_RW = ["k", "cum", "kmax", "rk", "tilde", "bon", "mb", "dq", "mk", "d2t", "q1", "q2", "q16", "g16", "q32",
          "g32", "q64"] + [f"z{c}" for c in range(NCH)] + ["yc", "var", "out"]


FILL = {"lora": 4, "kks": 10, "tok": 2, "gn1": 3, "gn2": 3}


def filler_ends(p):
    total = KT * (DSA_PER_PAIR[p] + (3 if p + 1 < MT else 0))
    share = np.cumsum([FILL.get(name, 1) for name in PE_RW])
    upto = [int(total * n) // int(share[-1]) for n in share]
    return upto, [next(f for f in range(len(upto)) if upto[f] >= KT * (q + 1)) for q in range(DSA_PER_PAIR[p])]


def build(nc, A, out):
    ctx = ExitStack()
    with ctx:
        def sb(name, shape):
            return ctx.enter_context(nc.sbuf_tensor(name, shape, F32))

        def sem(name):
            return ctx.enter_context(nc.semaphore(name))


        V = sb("V", [P, NV])
        SQ = sb("SQ", [P, 4, T])
        RS = sb("RS", [P, T])
        NEGS = sb("NEGS", [P, 16])
        ONEMU = sb("ONEMU", [P, 27])
        ONEKA = sb("ONEKA", [P, 8])

        def split_memory(kind, suffix, pieces):
            shapes = [("ring", [P, RING, UNIT]), ("HT", [P, KT, T]), ("YT", [P, KT, T]), ("XT", [P, KT, T]),
                      ("C", [P, NC])]
            shapes += [(f"work{i}", [P, n]) for i, n in enumerate(pieces)]
            with ExitStack() as c:
                return [c.enter_context(nc.sbuf_tensor(n + suffix, shape, kind)) for n, shape in shapes]

        ring, HT, YT, XT, C, work = split_memory(F32, "", [WORK])
        ring_r, HT_r, YT_r, XT_r, C_r, *work_r = split_memory(F32R, "_r", [PIECE] * (WORK // PIECE) + [WORK % PIECE])
        PG = ctx.enter_context(nc.psum_tensor("PG", [P, BANKS, 512], F32))
        PX = ctx.enter_context(nc.psum_tensor("PX", [P, 4, 512], F32))

        def con(name):
            return C[:, CON[name][0]:CON[name][1]]

        def vec(name, i=0):
            return V[:, VEC[name][0] + i:VEC[name][0] + i + 1]

        taken = [0]

        def area(n, at=None):
            if at is not None:
                taken[0] = at
            a = work[:, taken[0]:taken[0] + n]
            taken[0] += n
            assert taken[0] <= WORK, taken[0]
            return a

        def cube(a, n):
            return a.rearrange("p (a b) -> p a b", a=n)

        def rounded_floats(at, n):
            assert at % PIECE + n <= PIECE
            return work_r[at // PIECE][:, at % PIECE:at % PIECE + n]

        def rounded(at, n):
            return cube(rounded_floats(at, n * T), n)

        slot_full = [sem(f"slot_full{i}") for i in range(RING)]
        unit_done = sem("unit_done")
        w_hi, w_lo = sem("weights_high"), sem("weights_low")
        late_lo = sem("late_inputs_low")
        s_spill, s_back = sem("residual_stored"), sem("residual_back")
        x_hi, x_lo = sem("inputs_high"), sem("inputs_low")
        he_hi, he_lo = sem("expert_hidden_high"), sem("expert_hidden_low")
        hid_hi, hid_lo = sem("mlp_hidden_high"), sem("mlp_hidden_low")
        bank_free = [sem(f"bank_free{i}") for i in range(BANKS)]
        s_x = [sem(f"x_in{i}") for i in range(4)]
        s_con, s_vec, s_lora, s_out = sem("constants_in"), sem("vectors_in"), sem("lora_in"), sem("out_stored")
        s_vprep = sem("vectors_prepared")
        s_sq, s_squsd, s_ms, s_rt, s_h = sem("squares_ready"), sem("squares_summed"), sem("mean_square"), \
            sem("root_ready"), sem("normed_tiles")
        s_sqsum = sem("squares_summed_over_partitions")
        s_mixed = sem("prev_scaled")
        s_lo_dve, s_lo_act = sem("low_rank_mixed"), sem("low_rank_act")
        s_zero = sem("zeros_set")
        dve_chain, act_chain = sem("dve_chain"), sem("act_chain")
        PR = Steps(sem("rwkv_pe"), PE_RW)
        AR_ = Steps(sem("rwkv_act"), ACT_RW)
        DR = Steps(sem("rwkv_dve"), DVE_RW)
        a_sq, a_sum, a_ms, a_rs, a_nrm, a_rot, a_cos, a_rope = (sem("qk_" + n) for n in (
            "squared", "summed", "mean_square", "inverse_root", "normed", "rotated", "cos_part", "roped"))
        a_vt, a_v, a_is, a_relu, a_acc, a_bias = (sem("idx_" + n) for n in (
            "turned", "turned_taken", "products", "relu", "added", "bias"))
        a_lg, a_l, a_ex, a_p, a_t, a_pt, a_pv, a_y = (sem("att_" + n) for n in (
            "logits", "maximum", "exp", "probs", "turned", "turned_taken", "values", "out"))
        s_route_in, s_lgt, s_router, s_rexp, s_cbt, s_cbb, s_comb = (sem("route_" + n) for n in (
            "in", "logits", "vector", "exp", "turned", "spread", "weights"))
        s_he = sem("expert_hidden")
        c_act, c_dve, c_par, c_turn, c_lb, c_cd, c_tab, c_bu, c_x, c_s, c_y, c_yd, c_g = (sem("s5_" + n) for n in (
            "act", "vector", "in", "turned", "turned_taken", "out_matrix", "table", "inputs", "rotated", "states",
            "outputs", "outputs_taken", "gelu"))
        pool_chain = sem("pool_chain")
        c_pow = sem("s5_powers")
        g_in, g_sq, g_sum, g_ms, g_rt, g_vn, g_t, g_tt, g_mix, g_y = (sem("gmlp_" + n) for n in (
            "in", "squared", "summed", "mean_square", "root", "normed", "turned", "turned_taken", "mixed", "out"))
        b_z, b_l, b_sp, b_r, b_w, b_e, b_pv, b_y = (sem("stick_" + n) for n in (
            "products", "log", "softplus", "sums", "exponent", "weights", "values", "out"))
        s_relu = sem("mlp_relu")
        c_zero, s_yb = sem("s5_zeroed"), sem("glu_out")

        DQ = cube(area(DSA_TILES * T, 0), DSA_TILES)
        LORA = area(MIX)
        GUP = area(2 * MIX).rearrange("p (a n) -> p a n", a=2)
        MBF = cube(area(3 * (T + 1)), 3)
        LO = cube(area(3 * T), 3)
        LO_END = taken[0]
        R_, K_, V_ = (area(T) for _ in range(3))
        EW, EA, G_, CS, CP, KK2, RN, PIN, PINV, PPREV, AM, KM, BON = (area(T) for _ in range(13))
        AR = area(2 * T).rearrange("p (tt a n) -> p tt a n", tt=TT, a=2)
        BT_, KT_ = area(T), area(T)
        TOK = cube(area(6 * P), 6)
        MBK = area(4 * T).rearrange("p (h tt a n) -> p h tt a n", h=2, tt=TT, a=2)
        MKK = area(4 * T).rearrange("p (h tt a n) -> p h tt a n", h=2, tt=TT, a=2)
        MAB, DA, EE, FF, DT, D2, D2T, Q_ = (cube(area(4 * P), 4) for _ in range(8))
        TM, GM = D2T, DT
        ZB = cube(area(2 * P), 2)
        ZP, ZT = area(P), area(P)
        W_, U_ = area(P), area(P)
        Y_, YC = area(T), area(T)
        YSQ = KK2
        GRS = RN

        area(0, LO_END)
        MSB = cube(area(16 * T), 16)
        VTOK = cube(area(TT * MIX), TT)
        ISC = cube(area(TT * T), TT)
        BIAS = cube(area(TT * T), TT)
        RL = cube(area(4 * T), 4)
        ROPE_C, ROPE_S = cube(area(4 * T), 4), cube(area(2 * T), 2)
        WX = cube(area(TT * IDX_HEADS), TT)
        TOP8 = area(8)
        LG, PR_, PT_ = cube(area(2 * T), 2), cube(area(2 * T), 2), cube(area(2 * T), 2)
        MX, NMX, SUM, RSUM = (area(16) for _ in range(4))

        H_HI = rounded(0, KT)
        HE_AT, HE_HI_AT = KT * T, (KT + 8) * T
        HE = area(2 * 4 * T, HE_AT).rearrange("p (e j t) -> p e j t", e=2, j=4)
        HE_LO = rounded(HE_AT, 8).rearrange("p (e j) t -> p e j t", e=2)
        HE_HI = rounded(HE_HI_AT, 8).rearrange("p (e j) t -> p e j t", e=2)
        W_HI_AT = 2 * KT * T
        COMB = cube(area(NE * T, W_HI_AT + 2 * UNIT), NE)
        SG, UP = cube(area(2 * T), 2), cube(area(2 * T), 2)
        ROUTE = cube(area(KT * 20), KT)
        LGT = cube(area(TT * 20), TT)
        G1, G2, G3, GO = (cube(area(TT * NG), TT) for _ in range(4))
        E1, E2, E3, O0, O1 = (cube(area(TT * NE), TT) for _ in range(5))
        m1, m2, m3, pg, v0, v1, vs = (area(TT) for _ in range(7))
        CB = cube(area(TT * P), TT)
        CT = area(T)

        S5IN = cube(area(MT * T, 0), MT)
        UV = cube(area(2 * MT * T), 2 * MT)
        QKV = cube(area(3 * MT * T), 3 * MT)
        gates_at = taken[0]
        GT = cube(area(3 * KT * T), 3 * KT)
        W_HI2_AT = taken[0]
        area(UNIT)
        (S_DT, S_TH, S_LR, S_N, S_R, S_MAG, S_SIN, S_COS, S_ABR, S_ABI, S_DEN, S_KR, S_KI, S_A, S_B) = (
            area(S5_TILES) for _ in range(15))
        PW = [area(S5_TILES) for _ in range(5)]
        NEGM = area(P)
        area(0, gates_at)
        LB = area(2 * MT * P).rearrange("p (c b n) -> p c b n", c=2, b=MT)
        CD = area(2 * S5_TILES * 32).rearrange("p (c i n) -> p c i n", c=2, i=S5_TILES)
        ROT = area(4 * 4 * T).rearrange("p (b c n) -> p b c n", b=2, c=2)
        XR = area(2 * 4 * T).rearrange("p (c n) -> p c n", c=2)
        BBD = XR[:, :, :].rearrange("p c n -> p (c n)").rearrange("p (c i n) -> p c i n", c=2, i=S5_TILES)
        TR = area(2 * 4 * T).rearrange("p (c n) -> p c n", c=2)
        S5B = TR[:, 0, :].rearrange("p (c i n) -> p c i n", c=2, i=S5_TILES)
        S5C = TR[:, 1, :].rearrange("p (c i n) -> p c i n", c=2, i=S5_TILES)
        yt = YT[:, :, :].rearrange("p a t -> p (a t)")
        POW = yt[:, 0:2048].rearrange("p (f c i n) -> p f c i n", f=2, c=2, i=S5_TILES)
        PT2 = yt[:, 2048:4096].rearrange("p (c n) -> p c n", c=2)
        PB = PT2[:, :, :].rearrange("p c n -> p (c n)").rearrange("p (c n) -> p c n", c=4)
        GVT = yt[:, 0:2048].rearrange("p (tt n) -> p tt n", tt=TT)
        AVT = yt[:, 2048:4096].rearrange("p (tt n) -> p tt n", tt=TT)
        SPAT = cube(area(MT * P, gates_at + 28 * T), MT)
        SPAT_B = area(MT * P)
        ZS, LN_, SP_, WW = (cube(area(2 * 384), 2) for _ in range(4))
        M_HI = rounded(gates_at, KT)
        HID = cube(area(KT * T, gates_at + KT * T), KT)
        HID_LO = rounded(gates_at + KT * T, KT)
        HID_HI = rounded(gates_at + 2 * KT * T, KT)
        S5_HI = rounded(4 * MT * T, MT)
        P2_LO = rounded(4 * MT * T, KT)
        YA_LO, YA_HI = rounded(MT * T, MT), rounded(2 * MT * T, MT)
        YC_LO, YC_HI = rounded(3 * MT * T, MT), rounded(0, MT)
        YB = YT[:, 0:MT, :]
        SQF = SQ[:, :, :].rearrange("p a t -> p (a t)")

        block = ctx.enter_context(nc.Block())

        spill = nc.dram_tensor("residual", (P, KT, T), F32, kind="Internal").ap()

        def free_bank(use):
            return bank_free[use % BANKS]

        def wait_bank(eng, use, more=0):
            if use >= BANKS:
                eng.wait_ge(free_bank(use), use // BANKS + more)

        def wait_taken(eng, use, more=0):
            eng.wait_ge(free_bank(use), use // BANKS + 1 + more)

        def split_count(u):
            return u - U0["wo"] if u < U0["p2"] + S5_FIRST else u - U0["wo"] - (S5_END - S5_FIRST)

        def w_high(u):
            if u < U0["p2"]:
                return rounded_floats(W_HI_AT + u % 2 * UNIT, UNIT)
            return rounded_floats(W_HI2_AT, UNIT) if u % 2 else C_r[:, 0:UNIT]

        def split_high(act, u, more=0, first=False):
            act.wait_ge(slot_full[u % RING], 16 * (u // RING + 1) + more * 4)
            if not first:
                act.wait_ge(unit_done, u - 1 + more)
            for h in range(2):
                c = slice(h * UNIT // 2, (h + 1) * UNIT // 2)
                act.activation(w_high(u)[:, c], ring[:, u % RING, c], ACT.Copy).then_inc(w_hi, 1)

        def split_low(dve, u, more=0):
            for h in range(2):
                c = slice(h * UNIT // 2, (h + 1) * UNIT // 2)
                dve.wait_ge(w_hi, 2 * split_count(u) + h + 1 + more * 2)
                dve.tensor_tensor(ring_r[:, u % RING, c], ring[:, u % RING, c], w_high(u)[:, c].bitcast(F32),
                                  ALU.subtract).then_inc(w_lo, 1)

        def four_high(act, dst, src, q):
            act.activation(dst[:, 4 * q:4 * q + 4, :], src[:, 4 * q:4 * q + 4, :], ACT.Copy).then_inc(x_hi, 1)

        def four_low(dve, dst, src, high, q, n):
            c = slice(4 * q, 4 * q + 4)
            dve.wait_ge(x_hi, n + 1)
            dve.tensor_tensor(dst[:, c, :], src[:, c, :], high[:, c, :].bitcast(F32), ALU.subtract).then_inc(x_lo, 1)

        X0, _n = {}, 0
        for _name, _fours in [("y", 4), ("h", 4), ("h1", 4), ("s5", 2), ("ya", 2), ("yb", 2), ("yc", 2), ("merged", 4),
                              ("h2", 4)]:
            X0[_name] = _n
            _n += _fours

        @block.sync
        def _(sp):
            for q in range(4):
                sp.dma_start(XT[:, 4 * q:4 * q + 4, :], A["xT"][:, 4 * q:4 * q + 4, :]).then_inc(s_x[q], 16)
            for s in range(RING):
                sp.dma_start(ring[:, s, :], A["weights"][s]).then_inc(slot_full[s], 16)
            with sp.Fori(1, UNITS // RING) as i:
                for s in range(RING):
                    sp.wait_ge(unit_done, i * RING + (s + 1 - RING))
                    sp.dma_start(ring[:, s, :], A["weights"][bass.ds(i * RING + s, 1), :, :]
                                 .rearrange("o p n -> p (o n)")).then_inc(slot_full[s], 16)
            for q in range(4):
                sp.wait_ge(s_h, 4 * KT + 4 * q + 4)
                sp.dma_start(out[:, 4 * q:4 * q + 4, :], YT[:, 4 * q:4 * q + 4, :]).then_inc(s_out, 16)
            sp.wait_ge(s_out, 64)

        @block.tensor
        def _(pe):
            def unit(u, use, x, kts=KT, tiles=1, first=None, full=0, free=0):
                pe.wait_ge(slot_full[u % RING], 16 * (u // RING + 1) + full)
                for t in range(tiles):
                    if t % 2 == 0:
                        wait_bank(pe, use + t // 2, free)
                    for k in range(kts):
                        if first is not None and t == 0:
                            pe.wait_ge(s_h, first + k + 1)
                        last = pe.matmul(PG[:, (use + t // 2) % BANKS, (t % 2) * T:(t % 2) * T + T],
                                         ring[:, u % RING, (k * tiles + t) * P:(k * tiles + t) * P + P],
                                         x[:, k, :], start=(k == 0), stop=(k == kts - 1))
                last.then_inc(unit_done, 1)

            def split_unit(u, use, high, low, kts=KT, tiles=1, more=0, free=0, before=None, order=None):
                s = 2 * split_count(u) + 2 * more
                order = order or range(kts)
                down = tiles == 4
                for t in range(1 if down else tiles):
                    if t % 2 == 0:
                        wait_bank(pe, use + t // 2, free)
                        if down:
                            wait_bank(pe, use + 1, free)
                    for n, k in enumerate(order):
                        if t == 0 and n == 0:
                            pe.wait_ge(w_lo, s + 1 if k == 0 else s + 2)
                        elif t == 0 and n == kts // 2:
                            pe.wait_ge(w_lo, s + 2)
                        if before and t == 0:
                            before(k)
                        for t_ in (range(tiles) if down else (t,)):
                            o = PG[:, (use + t_ // 2) % BANKS, (t_ % 2) * T:(t_ % 2) * T + T]
                            c = slice((k * tiles + t_) * P, (k * tiles + t_) * P + P)
                            wh, wl = w_high(u)[:, c], ring_r[:, u % RING, c]
                            pe.matmul(o, wh, high[:, k, :], start=(n == 0 and not (down and t_ % 2)), stop=False,
                                      skip_group_check=True)
                            pe.matmul(o, wh, low[:, k, :], start=False, stop=False, skip_group_check=True)
                            last = pe.matmul(o, wl, high[:, k, :], start=False, stop=(n == kts - 1),
                                             skip_group_check=True)
                last.then_inc(unit_done, 1)

            def fours(name, first):
                return (lambda k: pe.wait_ge(x_lo, X0[name] + k // 4 + 1) if k % 4 == 0 else None) if first else None

            def norm(n):
                pe.wait_ge(s_squsd, KT * (n + 1))
                pe.matmul(PX[:, 0, 0:T], con("ones"), RS[:, :], start=True, stop=True).then_inc(s_sqsum, 1)

            pe.wait_ge(s_con, 16)
            for k in range(KT):
                pe.wait_ge(s_sq, k + 1)
                pe.matmul(PX[:, 0, 0:T], con("ones"), SQ[:, k % 4, :], start=(k == 0),
                          stop=(k == KT - 1)).then_inc(s_squsd, 1)
            for u in range(3):
                unit(u, u, HT, first=0 if u == 0 else None)

            def product(u, k):
                if k == 0:
                    pe.wait_ge(slot_full[u % RING], 16 * (u // RING + 1))
                    wait_bank(pe, u)
                mm = pe.matmul(PG[:, u % BANKS, 0:T], ring[:, u % RING, k * P:k * P + P], HT[:, k, :],
                               start=(k == 0), stop=(k == KT - 1))
                if k == KT - 1:
                    mm.then_inc(unit_done, 1)

            def fill(p, f):
                upto_, ends = filler_ends(p)
                for m in range(upto_[f - 1] if f else 0, upto_[f]):
                    product(P1_AT[("v", p)] + 1 + m // KT, m % KT)

            def pair(p):
                for w in "rkv" if p == 0 else "":
                    unit(P1_AT[(w, p)], P1_AT[(w, p)], HT)
                step = iter(range(len(PE_RW)))
                act = lambda name: pe.wait_ge(AR_.sem, AR_.at(p, name))
                dve = lambda name: pe.wait_ge(DR.sem, DR.at(p, name))

                def done(mm, name):
                    mm.then_inc(PR.sem, PR.step(p, name))
                    fill(p, next(step))

                if p == 0:
                    pe.wait_ge(s_lora, 32)
                    pe.wait_ge(s_lo_dve, 2)
                    pe.wait_ge(s_lo_act, 3)
                else:
                    pe.wait_ge(DR.sem, DR.at(p - 1, "out"))
                cols = slice(p * P, p * P + P)
                pe.matmul(PX[:, 0, 0:T], LORA[0:64, cols], LO[0:64, 0, :], start=True, stop=True)
                pe.matmul(PX[:, 1, 0:T], LORA[64:128, cols], LO[64:128, 0, :], start=True, stop=True)
                pe.matmul(PX[:, 2, 0:T], GUP[:, 0, cols], LO[:, 1, :], start=True, stop=False)
                done(pe.matmul(PX[:, 2, 0:T], GUP[0:32, 1, cols], LO[0:32, 2, :], start=False, stop=True), "lora")
                act("kk2")
                done(pe.matmul(PX[:, 3, 0:T], con("head64"), KK2, start=True, stop=True), "kks")
                dve("tilde")
                act("lora")
                pe.matmul(PX[:, 3, T:2 * T], con("head64"), AM, start=True, stop=True)
                for n in range(6):
                    src = (V_, BT_, KT_)[n // 2]
                    mm = pe.transpose(PX[:, n // 4, (n % 4) * P:(n % 4) * P + P], src[:, (n % 2) * P:(n % 2) * P + P],
                                      con("ident"))
                done(mm, "tok")
                act("tok")
                dve("bon")
                for h in range(2):
                    hs = slice(64 * h, 64 * h + 64)
                    for tt in range(TT):
                        ts = slice(tt * P, tt * P + P)
                        pe.matmul(PX[:, 2 + h, 2 * P * tt:2 * P * tt + 2 * P], BT_[hs, ts],
                                  AR[hs, tt, :, :].rearrange("p a n -> p (a n)"), start=True, stop=True)
                        mm = pe.matmul(PX[:, h, P * tt:P * tt + P], AR[hs, tt, 0, :], BT_[hs, ts],
                                       start=True, stop=True)
                done(mm, "sco")
                dve("mb")
                for h in range(2):
                    hs = slice(64 * h, 64 * h + 64)
                    for tt in range(TT):
                        mm = pe.matmul(PX[:, 2 + h, 2 * P * tt:2 * P * tt + 2 * P], KT_[hs, tt * P:tt * P + P],
                                       AR[hs, tt, :, :].rearrange("p a n -> p (a n)"), start=True, stop=True)
                done(mm, "ksco")

                def four(bank, left, right, transpose=False):
                    for n in range(4):
                        o = PX[:, bank, n * P:n * P + P]
                        if transpose:
                            mm = pe.transpose(o, right[:, n, :], con("ident"))
                        else:
                            mm = pe.matmul(o, left[:, n, :], right[:, n, :], start=True, stop=True)
                    return mm

                act("mab")
                dve("dq")
                four(0, DT, DA)
                done(four(1, DA, DT), "sq2")
                act("d2")
                dve("d2t")
                four(0, D2T, D2)
                four(1, D2, D2T)
                dve("mk")
                done(four(2, D2, Q_), "sq4")
                act("d4")
                dve("q1")
                four(0, DT, DA)
                done(four(3, DA, Q_), "sq8")
                act("d8")
                dve("q2")
                done(four(2, D2, Q_), "inv16")
                for t, left in (("16", EE), ("32", FF)):
                    dve("q" + t)
                    four(0, None, Q_, transpose=True)
                    done(four(1, left, Q_), "t" + t)
                    act("t" + t)
                    dve("g" + t)
                    done(four(3 if t == "16" else 2, TM, GM), "inv32" if t == "16" else "inv64")
                for c in range(NCH):
                    tt, j = c // 2, c % 2
                    rows, cs = slice(64 * j, 64 * j + 64), slice(64 * j, 64 * j + 64)
                    z = ZB[:, c % 2, :]
                    if c == 0:
                        dve("q64")
                    else:
                        dve(f"z{c - 1}")
                    pe.matmul(PX[rows, 0, 0:P], AR[:, tt, 0, cs], z, start=True, stop=False, skip_group_check=True)
                    for h in range(2):
                        mm = pe.matmul(PX[rows, 0, 64 * h:64 * h + 64], MKK[:, h, tt, 0, cs],
                                       TOK[:, tt, 64 * h:64 * h + 64], start=False, stop=(h == 1),
                                       skip_group_check=True)
                    done(mm, f"W{c}")
                    act(f"W{c}")
                    for h in range(2):
                        mm = pe.matmul(PX[rows, 1, 64 * h:64 * h + 64], Q_[:, 2 * h + tt, cs],
                                       W_[:, 64 * h:64 * h + 64], start=True, stop=True)
                    done(mm, f"U{c}")
                    act(f"U{c}")
                    y = PX[:, 3, c * CH:c * CH + CH]
                    pe.matmul(y, z, AR[:, tt, 1, cs], start=True, stop=False, skip_group_check=True)
                    for h in range(2):
                        hs = slice(64 * h, 64 * h + 64)
                        yh = PX[hs, 3, c * CH:c * CH + CH]
                        pe.matmul(yh, U_[:, hs], MBK[:, h, tt, 1, cs], start=False, stop=False,
                                  skip_group_check=True)
                        pe.matmul(yh, TOK[:, tt, hs], MKK[:, h, tt, 1, cs], start=False, stop=(h == 1),
                                  skip_group_check=True)
                    pe.matmul(PX[:, 2, 0:P], TOK[rows, 2 + tt, :], U_[rows, :], start=True, stop=False)
                    done(pe.matmul(PX[:, 2, 0:P], TOK[rows, 4 + tt, :], TOK[rows, tt, :], start=False, stop=True),
                         f"Z{c}")
                act("y")
                done(pe.matmul(PX[:, 0, 0:T], con("head64"), Y_, start=True, stop=True), "gn1")
                act("ysq")
                done(pe.matmul(PX[:, 1, 0:T], con("head64"), YSQ, start=True, stop=True), "gn2")

            for p in range(MT):
                pair(p)

            def values(lo, hi):
                for m in range(lo, hi):
                    product(V_UNIT + m // KT, m % KT)

            def attention():
                pe.wait_ge(DR.sem, DR.at(MT - 1, "out"))
                for n in range(16):
                    pe.wait_ge(a_sq, n + 1)
                    if n >= 2:
                        pe.wait_ge(a_ms, n - 1)
                    pe.matmul(PX[:, n % 2, 0:T], con("ones"), SQ[:, n % 4, :], start=True, stop=True).then_inc(a_sum, 1)
                for r in range(25):
                    if r >= 9:
                        pe.wait_ge(a_nrm, r - 8)
                    if r >= 2:
                        pe.wait_ge(a_rope, r - 1)
                    pe.matmul(PX[:, 2 + r % 2, 0:T], con("perm64" if r < 9 else "perm128"), DQ[:, r, :],
                              start=True, stop=True).then_inc(a_rot, 1)
                    values(2 * r, 2 * r + 2)
                pe.wait_ge(a_rope, 25)
                for tt in range(TT):
                    mm = pe.transpose(PX[:, 2, tt * P:tt * P + P], LO[:, 2, tt * P:tt * P + P], con("ident"))
                mm.then_inc(a_vt, 1)
                pe.wait_ge(a_v, 1)
                for n in range(TT * IDX_HEADS):
                    tt, h = n // IDX_HEADS, n % IDX_HEADS
                    rows = slice(64 * (h % 2), 64 * (h % 2) + 64)
                    if n >= 4:
                        pe.wait_ge(a_relu, n - 3)
                    pe.matmul(PX[:, h % 4, 0:(tt + 1) * P], DQ[rows, 1 + h // 2, tt * P:tt * P + P],
                              DQ[rows, 0, 0:(tt + 1) * P], start=True, stop=True).then_inc(a_is, 1)
                    values(50 + n, 51 + n)
                values(82, LATE * KT)
                pe.wait_ge(a_relu, TT * IDX_HEADS)
                wait_taken(pe, V_UNIT + LATE - 1)
                for g in range(4):
                    if g >= 2:
                        pe.wait_ge(a_v, g)
                    for n in range(4):
                        mm = pe.transpose(PX[:, g % 2, n * P:n * P + P],
                                          DQ[:, 25 + 4 * (g % 2) + n, (g // 2) * P:(g // 2) * P + P], con("ident"))
                    mm.then_inc(a_vt, 1)
                pe.wait_ge(a_v, 5)
                def logits(n):
                    tt, h = n // MT, n % MT
                    if n >= 2:
                        pe.wait_ge(a_l, n - 1)
                    pe.matmul(PX[:, n % 2, 0:(tt + 1) * P], DQ[:, 9 + h, tt * P:tt * P + P],
                              DQ[:, 17 + h, 0:(tt + 1) * P], start=True, stop=True).then_inc(a_lg, 1)

                logits(0)
                for n in range(18):
                    if n + 1 < 16:
                        logits(n + 1)
                    if n >= 2:
                        m = n - 2
                        tt, h = m // MT, m % MT
                        pe.wait_ge(a_pt, m + 1)
                        if m:
                            pe.wait_ge(a_y, m)
                        for s in range(tt + 1):
                            mm = pe.matmul(PX[:, 3, 0:P], VTOK[:, s, h * P:h * P + P], PT_[:, m % 2, s * P:s * P + P],
                                           start=(s == 0), stop=(s == tt))
                        mm.then_inc(a_pv, 1)
                    if 1 <= n < 17:
                        m = n - 1
                        pe.wait_ge(a_p, m + 1)
                        if m:
                            pe.wait_ge(a_pt, m)
                        for s in range(m // MT + 1):
                            mm = pe.transpose(PX[:, 2, s * P:s * P + P], PR_[:, m % 2, s * P:s * P + P], con("ident"))
                        mm.then_inc(a_t, 1)

            attention()
            order = list(range(MT, KT)) + list(range(MT))
            for t in range(KT):
                split_unit(U0["wo"] + t, B0["wo"] + t, HT_r, YT_r, order=order, before=None if t else
                           lambda k: pe.wait_ge(x_lo, X0["y"] + (k // 4 + 2) % 4 + 1) if k % 4 == 0 else None)
            norm(1)

            def routing():
                pe.wait_ge(s_h, 2 * KT)
                pe.wait_ge(s_route_in, 16)
                for tt in range(TT):
                    for k in range(KT):
                        mm = pe.matmul(PX[:, 1, 32 * tt:32 * tt + 20], HT[:, k, tt * P:tt * P + P], ROUTE[:, k, :],
                                       start=(k == 0), stop=(k == KT - 1))
                mm.then_inc(s_lgt, 1)

            def weights_of_experts():
                pe.wait_ge(s_router, R_DONE)
                for tt in range(TT):
                    mm = pe.transpose(PX[:, 2, tt * P:tt * P + P], CB[:, tt, :], con("ident"))
                mm.then_inc(s_cbt, 1)
                pe.wait_ge(s_cbb, 1)
                for e in range(NE):
                    if e >= 4:
                        pe.wait_ge(s_comb, e - 3)
                    pe.matmul(PX[:, e % 4, 0:T], con("ident")[0:32, e:e + 1].to_broadcast([32, P]), CT[0:32, :],
                              start=True, stop=True).then_inc(s_cbt, 1)

            def two_experts(i, first=False):
                for e in range(2):
                    more, free = i * 24, i * 8
                    u, use = U0["moe"] + e * MOE_UNITS, B0["moe"] + e * MOE_USES
                    for j in range(8):
                        split_unit(u + j, use + j, H_HI, YT_r, more=more, free=free,
                                   before=fours("h", first and e == 0 and j == 0))
                        if first and e == 0 and j == 1:
                            routing()
                        if first and e == 0 and j == 3:
                            weights_of_experts()
                    for d in range(4):
                        split_unit(u + 8 + d, use + 8 + 2 * d, HE_HI[:, e, :, :], HE_LO[:, e, :, :], kts=4, tiles=4,
                                   more=more, free=free, before=None if d else
                                   lambda k: pe.wait_ge(he_lo, i * 8 + (4 * e + k + 1)))

            two_experts(0, first=True)
            with pe.Fori(1, NE // 2 - 1) as i:
                two_experts(i)
            two_experts(NE // 2 - 1)

            def s5_inputs(b):
                if b:
                    pe.wait_ge(c_yd, b)
                else:
                    pe.wait_ge(c_lb, 4)
                    wait_taken(pe, B0["p2"] + 7)
                for i in range(4):
                    rows = slice(32 * i, 32 * i + 32)
                    for c in range(2):
                        mm = pe.matmul(PX[:, i, c * T:c * T + T], LB[rows, c, b, :], S5IN[rows, b, :],
                                       start=True, stop=True)
                mm.then_inc(c_bu, 1)

            def s5_outputs(b):
                if b == 0:
                    pe.wait_ge(c_cd, 4)
                pe.wait_ge(c_s, b + 1)
                for i in range(4):
                    for c in range(2):
                        s = (TR[:, 0, :], XR[:, 1, :])[c]
                        mm = pe.matmul(PX[32 * i:32 * i + 32, 0, 0:T], CD[:, c, 4 * b + i, :], s[:, i * T:i * T + T],
                                       start=(c == 0), stop=(c == 1))
                mm.then_inc(c_y, 1)

            norm(2)
            for n in range(48):
                if n < S5_FIRST:
                    split_unit(U0["p2"] + n, B0["p2"] + n, XT_r, P2_LO, before=fours("h1", n == 0))
                elif n >= S5_END:
                    split_unit(U0["p2"] + n, B0["p2"] + n, XT_r, HT_r, before=None if n > S5_END else
                               lambda k: pe.wait_ge(late_lo, k // 4 + 1) if k % 4 == 0 else None)
                else:
                    unit(U0["p2"] + n, B0["p2"] + n, HT)
                if n == S5_FIRST - 2:
                    pe.wait_ge(c_dve, 2)
                    for q in range(4):
                        for m in range(4):
                            b = 4 * (q % 2) + m
                            mm = pe.transpose(PX[:, q, m * P:m * P + P],
                                              BBD[:, q // 2, 4 * b:4 * b + 4, :].rearrange("p i n -> p (i n)"),
                                              con("ident"))
                    mm.then_inc(c_turn, 1)
                if n == S5_FIRST - 1:
                    s5_inputs(0)
                if S5_FIRST <= n < S5_END and (n - S5_FIRST) % 3 == 2:
                    b = (n - S5_FIRST) // 3
                    s5_outputs(b)
                    if b + 1 < MT:
                        s5_inputs(b + 1)

            def gate_event(g):
                if g == 1:
                    pe.wait_ge(c_yd, MT)
                    for k in range(MT):
                        pe.wait_ge(g_sq, k + 1)
                        pe.matmul(PX[:, 0, 0:T], con("ones"), SQ[:, k % 4, :], start=(k == 0),
                                  stop=(k == MT - 1)).then_inc(g_sum, 1)
                elif g in (3, 4):
                    if g == 3:
                        pe.wait_ge(g_vn, MT)
                        pe.wait_ge(c_g, MT)
                    for q in range(4):
                        t = 4 * (g - 3) + q
                        if t >= 4:
                            pe.wait_ge(g_tt, t - 3)
                        for m in range(4):
                            src = (UV[:, MT + 4 * (q % 2) + m, :], QKV[:, 2 * MT + 4 * (q % 2) + m, :])[g - 3]
                            mm = pe.transpose(PX[:, q, m * P:m * P + P], src[:, (q // 2) * P:(q // 2) * P + P],
                                              con("ident"))
                        mm.then_inc(g_t, 1)
                elif g == 5:
                    pe.wait_ge(g_tt, 8)
                    pe.wait_ge(g_in, 33)
                    for m in range(MT):
                        for tt in range(TT):
                            o = PX[:, m // 2, (m % 2) * T + tt * P:(m % 2) * T + tt * P + P]
                            pe.matmul(o, GVT[:, tt, m * P:m * P + P], SPAT[:, m, :], start=True, stop=False)
                            mm = pe.matmul(o, con("ones")[0:1, :], SPAT_B[0:1, m * P:m * P + P], start=False, stop=True)
                    mm.then_inc(g_mix, 1)
                for h in range(MT):
                    q, k = QKV[:, h, :], QKV[:, MT + h, :]
                    if g == HEAD_AT[h]:
                        if h == 0:
                            pe.wait_ge(g_y, 4)
                        else:
                            pe.wait_ge(b_l, h)
                        pe.matmul(PX[:, 0, 0:T], k[:, 0:P], q, start=True, stop=True)
                        pe.matmul(PX[:, 0, T:384], k[:, P:T], q[:, P:T], start=True, stop=True).then_inc(b_z, 1)
                    if g == HEAD_AT[h] + 2:
                        pe.wait_ge(b_sp, h + 1)
                        if h:
                            pe.wait_ge(b_w, h)
                        sp = SP_[:, h % 2, :]
                        pe.matmul(PX[:, 1, 0:T], con("cum_after"), sp[:, 0:T], start=True, stop=False)
                        pe.matmul(PX[:, 1, P:T], con("ones"), sp[:, T:384], start=False, stop=True)
                        pe.matmul(PX[:, 1, T:384], con("cum_after"), sp[:, T:384], start=True,
                                  stop=True).then_inc(b_r, 1)
                    if g == HEAD_AT[h] + 4:
                        pe.wait_ge(b_e, h + 1)
                        if h:
                            pe.wait_ge(b_y, h)
                        w = WW[:, h % 2, :]
                        pe.matmul(PX[:, 2, 0:T], AVT[:, 0, h * P:h * P + P], w[:, 0:T], start=True, stop=False)
                        pe.matmul(PX[:, 2, P:T], AVT[:, 1, h * P:h * P + P], w[:, T:384], start=False,
                                  stop=True).then_inc(b_pv, 1)

            for g in range(48):
                split_unit(U0["p2"] + 48 + g, B0["p2"] + 48 + g, XT_r, HT_r)
                gate_event(g)
            for j in range(4):
                split_unit(U0["glu"] + j, B0["glu"] + j, S5_HI, YT_r[:, MT:KT, :], kts=MT, tiles=2,
                           before=fours("s5", j == 0))
            for n in range(3):
                high, low = ((YA_HI, YA_LO), (YT_r[:, MT:KT, :], YT_r[:, 0:MT, :]), (YC_HI, YC_LO))[n]
                for j in range(8):
                    split_unit(U0["br"] + 8 * n + j, B0["br"] + 8 * n + j, high, low, kts=MT, tiles=2,
                               before=fours(("ya", "yb", "yc")[n], j == 0))
            for t in range(KT):
                split_unit(U0["wo2"] + t, B0["wo2"] + t, M_HI, HT_r, before=fours("merged", t == 0))
            norm(3)

            def block_of_hidden(i):
                u, use = U0["mlp"], B0["mlp"]
                for t in range(KT):
                    split_unit(u + t, use + t, M_HI, HT_r, more=i * 32, free=i * 8,
                               before=fours("h2", t == 0))
                for t in range(KT):
                    split_unit(u + KT + t, use + KT + t, HID_HI, HID_LO, more=i * 32, free=i * 8,
                               before=None if t else lambda k: pe.wait_ge(hid_lo, i * KT + (k + 1)))

            with pe.Fori(0, 3) as i:
                block_of_hidden(i)
            block_of_hidden(3)
            norm(4)

        @block.scalar
        def _(act):
            n_chain = [0]

            def link(ins):
                n_chain[0] += 1
                ins.then_inc(act_chain, 1)
                act.wait_ge(act_chain, n_chain[0])

            act.dma_start(C[:, :], A["constants"]).then_inc(s_con, 16)
            act.dma_start(V[:, :], A["vectors"]).then_inc(s_vec, 16)
            act.dma_start(LORA, A["lora"]).then_inc(s_lora, 16)
            act.dma_start(GUP, A["gate_up"]).then_inc(s_lora, 16)

            def square(n, k):
                if KT * n + k >= 4:
                    act.wait_ge(s_squsd, KT * n + k - 3)
                act.activation(SQ[:, k % 4, :], XT[:, k, :], ACT.Square).then_inc(s_sq, 1)

            def root(n):
                act.wait_ge(s_ms, n + 1)
                act.activation(RS[:, :], RS[:, :], ACT.Sqrt).then_inc(s_rt, 1)

            for k in range(KT):
                act.wait_ge(s_x[k // 4], 16)
                square(0, k)
            root(0)

            def mix(what):
                m, u = MIX_ORDER.index(what), P1_AT[what]
                if m >= 3:
                    before = P1_AT[MIX_ORDER[m - 3]]
                    act.wait_ge(free_bank(before), before // BANKS + 1)
                act.wait_ge(unit_done, u + 1)
                act.activation(MBF[:, m % 3, 1:T + 1], PG[:, u % BANKS, 0:T], ACT.Copy,
                               scale=vec("mu", MU_COL[what])).then_inc(s_mixed, 1)

            act.wait_ge(s_vec, 16)
            act.wait_ge(s_zero, 1)
            for m in range(3):
                mix(("misc", m))
            act.wait_ge(free_bank(0), 1)
            act.activation(LO[0:64, 0, :], LO[0:64, 0, :], ACT.Tanh).then_inc(s_lo_act, 1)
            act.wait_ge(free_bank(1), 1)
            act.wait_ge(free_bank(2), 1)
            act.activation(LO[:, 1, :], LO[:, 1, :], ACT.Tanh, scale=0.5).then_inc(s_lo_act, 1)
            act.activation(LO[0:32, 2, :], LO[0:32, 2, :], ACT.Tanh, scale=0.5).then_inc(s_lo_act, 1)

            def pair(p):
                pe = lambda name: act.wait_ge(PR.sem, PR.at(p, name))
                dve = lambda name: act.wait_ge(DR.sem, DR.at(p, name))
                taken_ = [0]
                _, ends = filler_ends(p)

                def take_dsa(before):
                    while taken_[0] < len(ends) and ends[taken_[0]] < PE_RW.index(before):
                        d = sum(DSA_PER_PAIR[:p]) + taken_[0]
                        u = P1_AT[("dsa", d)]
                        act.wait_ge(unit_done, u + 1)
                        act.activation(DQ[:, d, :], PG[:, u % BANKS, 0:T], ACT.Copy).then_inc(free_bank(u), 1)
                        taken_[0] += 1

                def done(ins, name):
                    ins.then_inc(AR_.sem, AR_.step(p, name))

                for w in "rkv":
                    mix((w, p))
                if p == 0:
                    act.wait_ge(s_vprep, 4)
                pe("lora")
                act.activation(EW, PX[:, 0, 0:T], ACT.Exp, scale=-1.0, bias=NEGS[:, p:p + 1])
                act.activation(EA, PX[:, 1, 0:T], ACT.Exp, scale=-1.0, bias=NEGS[:, 8 + p:9 + p])
                done(act.activation(G_, PX[:, 2, 0:T], ACT.Copy), "lora")
                dve("k")
                done(act.activation(KK2, K_, ACT.Square, scale=vec("k_k", p)), "kk2")
                dve("kmax")
                link(act.activation(RN, RN, ACT.Ln))
                done(act.activation(RN, RN, ACT.Exp, scale=-0.5), "rn")
                act.activation(PIN, CS, ACT.Exp, scale=-DECAY)
                act.activation(PINV, CS, ACT.Exp, scale=DECAY)
                done(act.activation(PPREV, CP, ACT.Exp, scale=-DECAY), "exps")
                take_dsa("tok")
                pe("tok")
                act.activation(TOK[:, 0:4, :], PX[:, 0, :].rearrange("p (n a) -> p n a", n=4), ACT.Copy)
                done(act.activation(TOK[:, 4:6, :], PX[:, 1, 0:T].rearrange("p (n a) -> p n a", n=2), ACT.Copy), "tok")
                take_dsa("sco")
                pe("sco")
                act.activation(MAB[:, 0:2, :], PX[:, 0, 0:T].rearrange("p (n a) -> p n a", n=2), ACT.Copy)
                done(act.activation(MAB[:, 2:4, :], PX[:, 1, 0:T].rearrange("p (n a) -> p n a", n=2), ACT.Copy), "mab")

                def four(dst, bank):
                    return act.activation(dst, PX[:, bank, :].rearrange("p (n a) -> p n a", n=4), ACT.Copy)

                take_dsa("sq2")
                pe("sq2")
                done(four(D2, 0), "d2")
                take_dsa("sq4")
                pe("sq4")
                four(DA, 0)
                done(four(DT, 1), "d4")
                take_dsa("sq8")
                pe("sq8")
                done(four(D2, 0), "d8")
                for t in ("16", "32"):
                    take_dsa("t" + t)
                    pe("t" + t)
                    done(four(TM, 0), "t" + t)
                for c in range(NCH):
                    rows = slice(64 * (c % 2), 64 * (c % 2) + 64)
                    take_dsa(f"W{c}")
                    pe(f"W{c}")
                    done(act.activation(W_[rows, :], PX[rows, 0, 0:P], ACT.Copy), f"W{c}")
                    take_dsa(f"U{c}")
                    pe(f"U{c}")
                    done(act.activation(U_[rows, :], PX[rows, 1, 0:P], ACT.Copy), f"U{c}")
                take_dsa("Z3")
                pe("Z3")
                done(act.activation(Y_, PX[:, 3, 0:T], ACT.Copy), "y")
                dve("yc")
                done(act.activation(YSQ, YC, ACT.Square), "ysq")
                take_dsa("gn2")
                dve("var")
                link(act.activation(GRS, GRS, ACT.Ln))
                done(act.activation(GRS, GRS, ACT.Exp, scale=-0.5), "grs")
                while taken_[0] < len(ends):
                    d = sum(DSA_PER_PAIR[:p]) + taken_[0]
                    u = P1_AT[("dsa", d)]
                    act.wait_ge(unit_done, u + 1)
                    act.activation(DQ[:, d, :], PG[:, u % BANKS, 0:T], ACT.Copy).then_inc(free_bank(u), 1)
                    taken_[0] += 1

            for p in range(MT):
                pair(p)

            def attention():
                act.wait_ge(DR.sem, DR.at(MT - 1, "out"))
                for n in range(16):
                    if n >= 4:
                        act.wait_ge(a_sum, n - 3)
                    act.activation(SQ[:, n % 4, :], DQ[:, 9 + n, :], ACT.Square).then_inc(a_sq, 1)
                for g in range(4):
                    act.wait_ge(a_ms, 4 * g + 4)
                    link(act.activation(MSB[:, 4 * g:4 * g + 4, :], MSB[:, 4 * g:4 * g + 4, :], ACT.Ln))
                    act.activation(MSB[:, 4 * g:4 * g + 4, :], MSB[:, 4 * g:4 * g + 4, :], ACT.Exp,
                                   scale=-0.5).then_inc(a_rs, 1)
                def take_v(q):
                    u = V_UNIT + q
                    act.wait_ge(unit_done, u + 1)
                    act.activation(DQ[:, DSA_TILES - LATE + q, :], PG[:, u % BANKS, 0:T],
                                   ACT.Copy).then_inc(free_bank(u), 1)

                for q in range(3):
                    take_v(q)
                act.wait_ge(a_vt, 1)
                act.activation(WX, PX[:, 2, 0:T].rearrange("p (tt n) -> p tt n", tt=TT)[:, :, 32:32 + IDX_HEADS],
                               ACT.Copy, scale=IDX_HEADS ** -0.5 * 64 ** -0.5).then_inc(a_v, 1)
                for n in range(TT * IDX_HEADS):
                    keys = (n // IDX_HEADS + 1) * P
                    act.wait_ge(a_is, n + 1)
                    if n >= 4:
                        act.wait_ge(a_acc, n - 3)
                    act.activation(RL[:, n % 4, 0:keys], PX[:, n % 4, 0:keys], ACT.Relu).then_inc(a_relu, 1)
                    if n in (16, 31):
                        take_v(3 + n // 31)
                for q in range(5, LATE):
                    take_v(q)
                for g in range(4):
                    act.wait_ge(a_vt, g + 2)
                    c = 4 * (g % 2) * P
                    act.activation(VTOK[:, g // 2, c:c + 4 * P], PX[:, g % 2, :], ACT.Copy).then_inc(a_v, 1)
                for n in range(17):
                    if n < 16:
                        keys = (n // MT + 1) * P
                        act.wait_ge(a_l, n + 1)
                        if n >= 2:
                            act.wait_ge(a_t, n - 1)
                        act.activation(PR_[:, n % 2, 0:keys], LG[:, n % 2, 0:keys], ACT.Exp, bias=NMX[:, n:n + 1],
                                       accum_out=SUM[:, n:n + 1]).then_inc(a_ex, 1)
                    if n >= 1:
                        m = n - 1
                        keys = (m // MT + 1) * P
                        act.wait_ge(a_t, m + 1)
                        if m >= 2:
                            act.wait_ge(a_pv, m - 1)
                        act.activation(PT_[:, m % 2, 0:keys], PX[:, 2, 0:keys], ACT.Copy).then_inc(a_pt, 1)
                    if n in (1, 3):
                        split_high(act, U0["wo"] + n // 2, first=True)
                    if n in (5, 6):
                        four_high(act, HT_r, YT, n - 3)

            attention()
            for q in (0, 1):
                act.wait_ge(a_y, MT + 4 * q + 4)
                four_high(act, HT_r, YT, q)
            for t in range(KT + 1):
                if t < KT - 1:
                    split_high(act, U0["wo"] + t + 2)
                if t:
                    wait_taken(act, B0["wo"] + t - 1)
                    square(1, t - 1)
            act.dma_start(ROUTE, A["route"].rearrange("p (k n) -> p k n", k=KT)).then_inc(s_route_in, 16)
            root(1)
            split_high(act, U0["moe"] + 1)
            for q in range(4):
                act.wait_ge(s_h, KT + 4 * q + 4)
                four_high(act, H_HI, HT, q)
            def router_exps():
                act.wait_ge(s_router, 4)
                act.activation(G2, G1, ACT.Exp).then_inc(s_rexp, 1)
                act.wait_ge(s_router, 13)
                act.activation(E2, E1, ACT.Exp).then_inc(s_rexp, 1)

            def weights_of_experts():
                act.wait_ge(s_cbt, 1)
                act.activation(CT[0:32, :], PX[0:32, 2, 0:T], ACT.Copy).then_inc(s_cbb, 1)
                for e in range(NE):
                    act.wait_ge(s_cbt, e + 2)
                    act.activation(COMB[:, e, :], PX[:, e % 4, 0:T], ACT.Copy).then_inc(s_comb, 1)

            def hidden_high(i, e, j):
                act.wait_ge(s_he, i * 8 + (4 * e + j + 3))
                act.activation(HE_HI[:, e, j, :], HE[:, e, j, :], ACT.Copy).then_inc(he_hi, 1)

            def last_squares(d):
                for k in range(4 * d, 4 * d + 4):
                    wait_taken(act, B0["p2"] - 8 + k // 2)
                    square(2, k)
                act.dma_start(spill[:, 4 * d:4 * d + 4, :], XT[:, 4 * d:4 * d + 4, :]).then_inc(s_spill, 16)

            def two_experts(i, first=False, last=False):
                for e in range(2):
                    u = U0["moe"] + e * MOE_UNITS
                    use = B0["moe"] + e * MOE_USES
                    for n in range(MOE_UNITS):
                        if last and e == 1 and n + 2 >= MOE_UNITS:
                            if n + 2 == MOE_UNITS:
                                split_high(act, U0["p2"])
                        else:
                            split_high(act, u + n + 2, more=i * 24)
                        if last and e == 1 and n >= 9:
                            last_squares(n - 9)
                        j = n // 2
                        if n < 8 and n % 2 == 0:
                            act.wait_ge(unit_done, i * 24 + (u + n + 1))
                            act.wait_ge(s_he, i * 8 + (4 * e + j + 1))
                            act.activation(SG[:, j % 2, :], PG[:, (use + n) % BANKS, 0:T], ACT.Silu) \
                               .then_inc(free_bank(use + n), 1)
                        if first and e == 0 and n < 4:
                            if n == 1:
                                router_exps()
                            if n == 3:
                                weights_of_experts()
                                hidden_high(i, 0, 0)
                                hidden_high(i, 0, 1)
                        elif n < 8 and n % 2 == 1:
                            hidden_high(i, e, j)

            two_experts(0, first=True)
            with act.Fori(1, NE // 2 - 1) as i:
                two_experts(i)
            two_experts(NE // 2 - 1, last=True)
            last_squares(3)

            act.wait_ge(free_bank(0), B0["p2"] // BANKS)
            act.wait_ge(s_he, 2 + 4 * NE)
            act.dma_start(S5B, A["s5_b"].rearrange("p (c i n) -> p c i n", c=2, i=S5_TILES)).then_inc(c_par, 16)
            act.dma_start(S5C, A["s5_c"].rearrange("p (c i n) -> p c i n", c=2, i=S5_TILES)).then_inc(c_par, 16)
            root(2)
            split_high(act, U0["p2"] + 1)
            act.wait_ge(s_spill, 64)
            for q in range(4):
                act.wait_ge(s_h, 2 * KT + 4 * q + 4)
                four_high(act, XT_r, HT, q)
            v = lambda name: V[:, VEC[name][0]:VEC[name][1]]
            act.activation(S_DT, v("log_dt"), ACT.Exp).then_inc(c_act, 1)
            for n in range(48):
                u, use = U0["p2"] + n, B0["p2"] + n
                if n + 2 < S5_FIRST or n >= S5_END:
                    split_high(act, u + 2)
                act.wait_ge(unit_done, u + 1)
                dst = S5IN[:, n, :] if n < 8 else UV[:, n - 8, :] if n < 24 else QKV[:, n - 24, :]
                act.activation(dst, PG[:, use % BANKS, 0:T], ACT.Gelu_apprx_tanh if 8 <= n < 24 else ACT.Copy) \
                   .then_inc(free_bank(use), 1)
                if n == 3:
                    act.wait_ge(c_dve, 1)
                    act.activation(S_MAG, S_LR, ACT.Exp)
                    act.activation(S_SIN, S_R, ACT.Sin)
                    act.activation(S_COS, S_R, ACT.Sin, scale=0.5).then_inc(c_act, 1)
                if n == 8:
                    act.wait_ge(c_par, 32)
                    act.wait_ge(c_zero, 1)
                    for c in range(2):
                        for h in range(2):
                            act.activation(CD[64 * h:64 * h + 64, c, :, 16 * h:16 * h + 16],
                                           S5C[64 * h:64 * h + 64, c, :, :], ACT.Copy,
                                           scale=(1.0, -1.0)[c]).then_inc(c_cd, 1)
                if n == S5_FIRST - 2:
                    act.wait_ge(c_turn, 1)
                    for q in range(4):
                        act.activation(LB[:, q // 2, 4 * (q % 2):4 * (q % 2) + 4, :],
                                       PX[:, q, :].rearrange("p (m n) -> p m n", m=4), ACT.Copy).then_inc(c_lb, 1)
                if S5_FIRST <= n < S5_END and (n - S5_FIRST) % 3 == 2:
                    b = (n - S5_FIRST) // 3
                    act.wait_ge(c_yd, b + 1)
                    act.activation(S5IN[:, b, :], S5IN[:, b, :], ACT.Gelu_apprx_tanh).then_inc(c_g, 1)
                if n == S5_END - 2:
                    for m in (0, 1):
                        split_high(act, U0["p2"] + S5_END + m, first=True)

            def gate_event(g):
                if g == 0:
                    for k in range(MT):
                        if k >= 4:
                            act.wait_ge(g_sum, k - 3)
                        act.activation(SQ[:, k % 4, :], UV[:, MT + k, :], ACT.Square).then_inc(g_sq, 1)
                elif g == 1:
                    act.wait_ge(g_ms, 1)
                    act.activation(RS[:, :], RS[:, :], ACT.Sqrt).then_inc(g_rt, 1)
                elif g in (3, 4):
                    for q in range(4):
                        act.wait_ge(g_t, 4 * (g - 3) + q + 1)
                        dst = (GVT, AVT)[g - 3]
                        act.activation(dst[:, q // 2, 4 * P * (q % 2):4 * P * (q % 2) + 4 * P], PX[:, q, :],
                                       ACT.Copy).then_inc(g_tt, 1)
                for h in range(MT):
                    if g == HEAD_AT[h]:
                        z, l = ZS[:, h % 2, :], LN_[:, h % 2, :]
                        act.wait_ge(b_z, h + 1)
                        if h >= 2:
                            act.wait_ge(b_w, h - 1)
                        link(act.activation(z, PX[:, 0, 0:384], ACT.Copy, scale=P ** -0.5))
                        link(act.activation(l, z, ACT.Abs))
                        link(act.activation(l, l, ACT.Exp, scale=-1.0))
                        act.activation(l, l, ACT.Ln, bias=1.0).then_inc(b_l, 1)
                    if g == HEAD_AT[h] + 3:
                        act.wait_ge(b_w, h + 1)
                        act.activation(WW[:, h % 2, :], WW[:, h % 2, :], ACT.Exp).then_inc(b_e, 1)

            for g in range(48):
                use = B0["p2"] + 48 + g
                if g == 0:
                    act.wait_ge(c_yd, MT)
                    act.dma_start(SPAT, A["spatial"].rearrange("p (m n) -> p m n", m=MT)).then_inc(g_in, 16)
                    act.dma_start(SPAT_B[0:1, :], A["spatial_b"]).then_inc(g_in, 16)
                split_high(act, U0["p2"] + 48 + g + 2)
                act.wait_ge(unit_done, U0["p2"] + 48 + g + 1)
                if g == 36:
                    act.wait_ge(b_y, MT)
                act.activation(GT[:, g, :], PG[:, use % BANKS, 0:T], ACT.Sigmoid, bias=vec("b_gate", g)) \
                   .then_inc(free_bank(use), 1)
                gate_event(g)
                if g in (40, 41):
                    four_high(act, S5_HI, S5IN, g - 40)
                if g in (42, 43):
                    four_high(act, YA_HI, UV, g - 42)
            act.wait_ge(unit_done, U0["glu"])
            act.dma_start(XT[:, :, :], spill).then_inc(s_back, 16)
            for j in range(4):
                use = B0["glu"] + j
                split_high(act, U0["glu"] + j + 2)
                act.wait_ge(unit_done, U0["glu"] + j + 1)
                if j >= 2:
                    act.wait_ge(s_yb, j - 1)
                act.activation(SQ[:, 2 * (j % 2), :], PG[:, use % BANKS, 0:T], ACT.Sigmoid, bias=vec("b_glu", 2 * j))
                act.activation(SQ[:, 2 * (j % 2) + 1, :], PG[:, use % BANKS, T:2 * T], ACT.Sigmoid,
                               bias=vec("b_glu", 2 * j + 1)).then_inc(free_bank(use), 1)
            for n in range(24):
                split_high(act, U0["br"] + n + 2)
                if n in (0, 1):
                    if n == 0:
                        act.wait_ge(s_yb, 4)
                    four_high(act, YT_r[:, MT:KT, :], YT, n)
                if n in (3, 4):
                    four_high(act, YC_HI, QKV, n - 3)
                if n >= 18 and n % 2 == 0:
                    wait_taken(act, B0["br"] + n - 1)
                    four_high(act, M_HI, HT, (n - 18) // 2)
            wait_taken(act, B0["br"] + 23)
            four_high(act, M_HI, HT, 3)
            for t in range(KT + 1):
                if t < KT - 1:
                    split_high(act, U0["wo2"] + t + 2)
                if t:
                    wait_taken(act, B0["wo2"] + t - 1)
                    square(3, t - 1)
            root(3)
            split_high(act, U0["mlp"] + 1)
            for q in range(4):
                act.wait_ge(s_h, 3 * KT + 4 * q + 4)
                four_high(act, M_HI, HT, q)

            def hidden_high(i, t):
                wait_taken(act, B0["mlp"] + t, i * 8)
                act.activation(HID_HI[:, t, :], HID[:, t, :], ACT.Copy).then_inc(hid_hi, 1)

            def block_of_hidden(i, last=False):
                for n in range(2 * KT):
                    if n == KT:
                        hidden_high(i, n - 1)
                    if not (last and n + 2 >= 2 * KT):
                        split_high(act, U0["mlp"] + n + 2, more=i * 32)
                    if n < KT:
                        use = B0["mlp"] + n
                        act.wait_ge(unit_done, i * 32 + (U0["mlp"] + n + 1))
                        if n >= 2:
                            wait_taken(act, use - 2, i * 8)
                        act.activation(SQ[:, n % 2, :], PG[:, use % BANKS, 0:T], ACT.Relu).then_inc(s_relu, 1)
                    if 1 <= n < KT:
                        hidden_high(i, n - 1)
                    if last and n > KT:
                        wait_taken(act, B0["mlp"] + 96 + n - 1)
                        square(4, n - KT - 1)

            with act.Fori(0, 3) as i:
                block_of_hidden(i)
            block_of_hidden(3, last=True)
            wait_taken(act, B0["mlp"] + 127)
            square(4, KT - 1)
            root(4)

        @block.vector
        def _(dve):
            n_chain = [0]

            def link(ins):
                n_chain[0] += 1
                ins.then_inc(dve_chain, 1)
                dve.wait_ge(dve_chain, n_chain[0])

            dve.memset(MBF[:, :, 0:1], 0.0)
            dve.memset(W_, 0.0)
            dve.memset(U_, 0.0).then_inc(s_zero, 1)
            dve.wait_ge(s_vec, 16)
            a, b = VEC["w0"][0], VEC["mu"][0]
            dve.tensor_scalar(NEGS[:, 0:8], V[:, a:a + 8], -1.0, None, ALU.mult).then_inc(s_vprep, 1)
            a = VEC["a0"][0]
            dve.tensor_scalar(NEGS[:, 8:16], V[:, a:a + 8], -1.0, None, ALU.mult).then_inc(s_vprep, 1)
            dve.tensor_scalar(ONEMU[:, :], V[:, b:b + 27], -1.0, 1.0, ALU.mult, ALU.add).then_inc(s_vprep, 1)
            a = VEC["k_a"][0]
            dve.tensor_scalar(ONEKA[:, :], V[:, a:a + 8], -1.0, 1.0, ALU.mult, ALU.add).then_inc(s_vprep, 1)
            dve.wait_ge(s_vprep, 4)

            def norm(n, gain, dst=HT, low=None, second=None):
                if n == 0:
                    dve.wait_ge(s_squsd, KT)
                else:
                    dve.wait_ge(s_sqsum, n)
                dve.tensor_scalar(RS[:, :], PX[:, 0, 0:T], 1.0 / D, 1e-6, ALU.mult, ALU.add).then_inc(s_ms, 1)
                dve.wait_ge(s_rt, n + 1)
                link(dve.reciprocal(RS[:, :], RS[:, :]))
                for k in range(KT):
                    dve.scalar_tensor_tensor(dst[:, k, :], XT[:, k, :], vec(gain, k), RS[:, :], ALU.mult,
                                             ALU.mult).then_inc(s_h, 1)
                    if low and k % 4 == 3 and k > 3:
                        low(k // 4 - 1)
                if low:
                    low(3)
                    split_low(dve, second)

            norm(0, "g_mix")

            def mix(what, dst):
                m, u = MIX_ORDER.index(what), P1_AT[what]
                c = MU_COL[what]
                dve.wait_ge(s_mixed, m + 1)
                dve.scalar_tensor_tensor(dst, PG[:, u % BANKS, 0:T], ONEMU[:, c:c + 1], MBF[:, m % 3, 0:T],
                                         ALU.mult, ALU.add).then_inc(free_bank(u), 1)

            for m in range(3):
                mix(("misc", m), LO[:, m, :])
            dve.wait_ge(s_lo_act, 3)
            dve.tensor_scalar(LO[:, 1, :], LO[:, 1, :], 0.5, 0.5, ALU.mult, ALU.add).then_inc(s_lo_dve, 1)
            dve.tensor_scalar(LO[0:32, 2, :], LO[0:32, 2, :], 0.5, 0.5, ALU.mult, ALU.add).then_inc(s_lo_dve, 1)

            def pair(p):
                pe = lambda name: dve.wait_ge(PR.sem, PR.at(p, name))
                act = lambda name: dve.wait_ge(AR_.sem, AR_.at(p, name))

                def done(ins, name):
                    ins.then_inc(DR.sem, DR.step(p, name))

                def me(name):
                    dve.wait_ge(DR.sem, DR.at(p, name))

                mix(("r", p), R_)
                mix(("k", p), K_)
                mix(("v", p), V_)
                v = P1_AT[("v", p)]
                dve.wait_ge(free_bank(v), v // BANKS + 1)
                done(dve.memset(ZB[:, 0, :], 0.0), "k")
                act("lora")
                dve.tensor_scalar(EW, EW, 1.0, None, ALU.add)
                link(dve.tensor_scalar(EA, EA, 1.0, None, ALU.add))
                dve.reciprocal(EW, EW)
                link(dve.reciprocal(EA, EA))
                link(dve.tensor_tensor_scan(CS, con("reset"), EW, 0.0, ALU.mult, ALU.add))
                done(dve.tensor_tensor(CP, CS, EW, ALU.subtract), "cum")
                pe("kks")
                done(dve.tensor_scalar(RN, PX[:, 3, 0:T], 1e-24, None, ALU.max), "kmax")
                link(dve.tensor_scalar(AM, EA, vec("k_a", p), ONEKA[:, p:p + 1], ALU.mult, ALU.add))
                link(dve.tensor_tensor(KM, K_, AM, ALU.mult))
                done(dve.scalar_tensor_tensor(AM, R_, vec("r_k", p), KM, ALU.mult, ALU.mult), "rk")
                act("rn")
                link(dve.scalar_tensor_tensor(RN, K_, vec("k_k", p), RN, ALU.mult, ALU.mult))
                link(dve.tensor_tensor(EA, RN, EA, ALU.mult))
                act("exps")
                a3 = lambda a: a.rearrange("p (tt n) -> p tt n", tt=TT)
                dve.scalar_tensor_tensor(AR[:, :, 0, :], a3(RN), -1.0, a3(PPREV), ALU.mult, ALU.mult)
                dve.tensor_tensor(AR[:, :, 1, :], a3(R_), a3(PIN), ALU.mult)
                dve.tensor_tensor(BT_, EA, PINV, ALU.mult)
                done(dve.tensor_tensor(KT_, KM, PINV, ALU.mult), "tilde")
                pe("tok")
                done(dve.tensor_tensor(BON, PX[:, 3, T:2 * T], V_, ALU.mult), "bon")
                pe("sco")
                c0 = CON["up_strict64"][0]
                m4 = C[:, c0:c0 + 2 * P].rearrange("p (o n) -> p o n", o=1).to_broadcast([P, TT, 2 * P])
                for h in range(2):
                    ins = dve.tensor_tensor(MBK[:, h, :, :, :].rearrange("p tt a n -> p tt (a n)"),
                                            PX[:, 2 + h, :].rearrange("p (tt n) -> p tt n", tt=TT), m4, ALU.mult)
                done(ins, "mb")
                me("mb")
                bc = lambda name: con(name).rearrange("p (o n) -> p o n", o=1).to_broadcast([P, 4, P])
                mbt = MBK[:, :, :, 0, :].rearrange("p h tt n -> p (h tt) n")
                link(dve.tensor_tensor(DT, mbt, bc("up_diag16"), ALU.mult))
                dve.tensor_tensor(Q_, DT, bc("ident"), ALU.add)
                act("mab")
                dve.tensor_tensor(EE, MAB, bc("lo_in32"), ALU.mult)
                dve.tensor_tensor(FF, MAB, bc("lo_in64"), ALU.mult)
                done(dve.tensor_tensor(DA, MAB, bc("lo_diag16"), ALU.mult), "dq")
                pe("ksco")
                for h in range(2):
                    ins = dve.tensor_tensor(MKK[:, h, :, :, :].rearrange("p tt a n -> p tt (a n)"),
                                            PX[:, 2 + h, :].rearrange("p (tt n) -> p tt n", tt=TT), m4, ALU.mult)
                done(ins, "mk")
                bank = lambda b: PX[:, b, :].rearrange("p (n a) -> p n a", n=4)
                pe("sq2")
                done(dve.tensor_copy(D2T, bank(1)), "d2t")
                pe("sq4")
                done(dve.tensor_tensor(Q_, Q_, bank(2), ALU.add), "q1")
                pe("sq8")
                me("q1")
                done(dve.tensor_tensor(Q_, Q_, bank(3), ALU.add), "q2")
                pe("inv16")
                me("q2")
                done(dve.tensor_tensor(Q_, Q_, bank(2), ALU.add), "q16")
                for t, b in (("16", 3), ("32", 2)):
                    pe("t" + t)
                    done(dve.tensor_copy(GM, bank(1)), "g" + t)
                    nxt = "32" if t == "16" else "64"
                    pe("inv" + nxt)
                    done(dve.tensor_tensor(Q_, Q_, bank(b), ALU.add), "q" + nxt)
                for c in range(NCH):
                    end = c * CH + CH - 1
                    pc = PIN[:, end:end + 1]
                    if c:
                        me(f"z{c - 1}")
                    dve.tensor_scalar(ZP, ZB[:, c % 2, :], pc, None, ALU.mult)
                    pe(f"Z{c}")
                    link(dve.scalar_tensor_tensor(ZT, PX[:, 2, 0:P], pc, con("head64"), ALU.mult, ALU.mult))
                    done(dve.tensor_tensor(ZB[:, (c + 1) % 2, :], ZT, ZP, ALU.add), f"z{c}")
                pe("gn1")
                done(dve.scalar_tensor_tensor(YC, PX[:, 0, 0:T], -1.0 / 64, Y_, ALU.mult, ALU.add), "yc")
                pe("gn2")
                done(dve.tensor_scalar(GRS, PX[:, 1, 0:T], 1.0 / 64, 64e-5, ALU.mult, ALU.add), "var")
                act("grs")
                link(dve.scalar_tensor_tensor(YC, YC, vec("ln_w", p), GRS, ALU.mult, ALU.mult))
                link(dve.scalar_tensor_tensor(YC, YC, vec("ln_b", p), BON, ALU.add, ALU.add))
                done(dve.tensor_tensor(YT[:, MT + p, :], YC, G_, ALU.mult), "out")

            for p in range(MT):
                pair(p)

            def attention():
                for n in range(16):
                    dve.wait_ge(a_sum, n + 1)
                    dve.tensor_scalar(MSB[:, n, :], PX[:, n % 2, 0:T], 1.0 / P, 1e-6, ALU.mult,
                                      ALU.add).then_inc(a_ms, 1)

                def normed(r):
                    n = r - 9
                    if n % 4 == 0:
                        dve.wait_ge(a_rs, n // 4 + 1)
                    dve.scalar_tensor_tensor(DQ[:, r, :], DQ[:, r, :], vec("q_gain" if n < 8 else "k_gain"),
                                             MSB[:, n, :], ALU.mult, ALU.mult).then_inc(a_nrm, 1)

                for r in range(25):
                    if 9 <= r + 1 < 25:
                        normed(r + 1)
                    dve.wait_ge(a_rot, r + 1)
                    link(dve.tensor_tensor(ROPE_S[:, r % 2, :], PX[:, 2 + r % 2, 0:T],
                                           con("sin64" if r < 9 else "sin128"), ALU.mult))
                    dve.wait_ge(a_cos, r + 1)
                    dve.tensor_tensor(DQ[:, r, :], ROPE_S[:, r % 2, :], ROPE_C[:, r % 4, :], ALU.add) \
                       .then_inc(a_rope, 1)
                dve.wait_ge(a_v, 1)
                for tt in range(TT):
                    keys = (tt + 1) * P
                    sc = ISC[:, tt, 0:keys]
                    for h in range(IDX_HEADS):
                        n = tt * IDX_HEADS + h
                        dve.wait_ge(a_relu, n + 1)
                        w = WX[:, tt, h:h + 1]
                        if h == 0:
                            dve.tensor_scalar(sc, RL[:, n % 4, 0:keys], w, None, ALU.mult).then_inc(a_acc, 1)
                        else:
                            dve.scalar_tensor_tensor(sc, RL[:, n % 4, 0:keys], w, sc, ALU.mult, ALU.add) \
                               .then_inc(a_acc, 1)
                        dve.wait_ge(a_acc, n + 1)
                    link(dve.memset(ISC[0:CH, tt, keys - CH:keys], NEG))
                    for n in range(TOP_K // 8):
                        link(dve.max(TOP8, sc))
                        link(dve.match_replace(out=sc, in_to_replace=TOP8, in_values=sc, imm_value=-3.0e38))
                    dve.tensor_scalar(BIAS[:, tt, 0:keys], sc, -2.0e38, NEG, ALU.is_gt, ALU.mult).then_inc(a_bias, 1)
                dve.wait_ge(a_bias, 2)
                for n in range(18):
                    if n < 16:
                        tt = n // MT
                        keys = (tt + 1) * P
                        dve.wait_ge(a_lg, n + 1)
                        if n >= 2:
                            dve.wait_ge(a_ex, n - 1)
                        link(dve.tensor_tensor_reduce(LG[:, n % 2, 0:keys], PX[:, n % 2, 0:keys], BIAS[:, tt, 0:keys],
                                                      P ** -0.5, -3.0e38, ALU.add, ALU.max, MX[:, n:n + 1]))
                        dve.tensor_scalar(NMX[:, n:n + 1], MX[:, n:n + 1], -1.0, None, ALU.mult).then_inc(a_l, 1)
                    if 1 <= n < 17:
                        m = n - 1
                        keys = (m // MT + 1) * P
                        dve.wait_ge(a_ex, m + 1)
                        link(dve.reciprocal(RSUM[:, m:m + 1], SUM[:, m:m + 1]))
                        dve.tensor_scalar(PR_[:, m % 2, 0:keys], PR_[:, m % 2, 0:keys], RSUM[:, m:m + 1], None,
                                          ALU.mult).then_inc(a_p, 1)
                    if n >= 2:
                        m = n - 2
                        dve.wait_ge(a_pv, m + 1)
                        dve.tensor_copy(YT[:, m % MT, (m // MT) * P:(m // MT) * P + P], PX[:, 3, 0:P]).then_inc(a_y, 1)
                    if n in (2, 4):
                        split_low(dve, U0["wo"] + n // 2 - 1)
                    if n in (6, 7):
                        four_low(dve, YT_r, YT, HT_r, n - 4, X0["y"] + n - 6)

            attention()

            def add_tile(u, use, t):
                dve.wait_ge(unit_done, u + 1)
                dve.tensor_tensor(XT[:, t, :], XT[:, t, :], PG[:, use % BANKS, 0:T], ALU.add) \
                   .then_inc(free_bank(use), 1)

            for q in (0, 1):
                four_low(dve, YT_r, YT, HT_r, q, X0["y"] + q + 2)
            for t in range(KT):
                add_tile(U0["wo"] + t, B0["wo"] + t, t)
                if t < KT - 1:
                    split_low(dve, U0["wo"] + t + 2)

            def router():
                n_done = [0]

                def do(ins):
                    n_done[0] += 1
                    ins.then_inc(s_router, 1)
                    dve.wait_ge(s_router, n_done[0])

                b = lambda a, n: a.rearrange("p (t o) -> p t o", o=1).to_broadcast([P, TT, n])
                br = V[:, VEC["b_route"][0]:VEC["b_route"][1]].rearrange("p (o n) -> p o n", o=1) \
                    .to_broadcast([P, TT, 20])
                rank = lambda n: con("rank")[:, 0:n].rearrange("p (o n) -> p o n", o=1).to_broadcast([P, TT, n])
                do(dve.memset(CB, 0.0))
                dve.wait_ge(s_lgt, 1)
                do(dve.tensor_tensor(LGT, PX[:, 1, 0:64].rearrange("p (t n) -> p t n", t=TT)[:, :, 0:20], br, ALU.add))
                grp = LGT[:, :, 0:NG]
                do(dve.tensor_reduce(m1, grp, AX_X, ALU.max))
                do(dve.tensor_tensor(G1, grp, b(m1, NG), ALU.subtract))
                do(dve.tensor_tensor(G3, grp, b(m1, NG), ALU.is_equal))
                do(dve.tensor_tensor(G3, G3, rank(NG), ALU.mult))
                do(dve.tensor_reduce(m2, G3, AX_X, ALU.max))
                do(dve.tensor_tensor(GO, G3, b(m2, NG), ALU.is_equal))
                do(dve.tensor_scalar(GO, GO, -NEG, NEG, ALU.mult, ALU.add))
                for t in range(TT):
                    ins = dve.tensor_tensor(E1[:, t, :].rearrange("p (g e) -> p g e", g=NG),
                                            LGT[:, t, NG:20].rearrange("p (g e) -> p g e", g=NG),
                                            GO[:, t, :].rearrange("p (g o) -> p g o", o=1)
                                            .to_broadcast([P, NG, EPG]), ALU.add)
                    do(ins)
                do(dve.tensor_reduce(m3, E1, AX_X, ALU.max))
                do(dve.tensor_tensor(E1, E1, b(m3, NE), ALU.subtract))
                assert n_done[0] == 13
                dve.wait_ge(s_rexp, 2)
                do(dve.tensor_reduce(pg, G2, AX_X, ALU.add))
                for v, o in ((v0, O0), (v1, O1)):
                    do(dve.tensor_reduce(v, E2, AX_X, ALU.max))
                    do(dve.tensor_tensor(E3, E2, b(v, NE), ALU.is_equal))
                    do(dve.tensor_tensor(E3, E3, rank(NE), ALU.mult))
                    do(dve.tensor_reduce(m2, E3, AX_X, ALU.max))
                    do(dve.tensor_tensor(o, E3, b(m2, NE), ALU.is_equal))
                    do(dve.scalar_tensor_tensor(E2, o, -4.0, E2, ALU.mult, ALU.add))
                    do(dve.tensor_tensor(o, o, b(v, NE), ALU.mult))
                do(dve.tensor_tensor(vs, v0, v1, ALU.add))
                do(dve.tensor_tensor(vs, vs, pg, ALU.mult))
                do(dve.reciprocal(vs, vs))
                do(dve.tensor_tensor(O0, O0, O1, ALU.add))
                do(dve.tensor_tensor(CB[:, :, 0:NE], O0, b(vs, NE), ALU.mult))
                assert n_done[0] == R_DONE, n_done[0]

            norm(1, "g_ffn", low=lambda q: four_low(dve, YT_r, HT, H_HI, q, X0["h"] + q),
                 second=U0["moe"] + 1)
            dve.memset(UP[:, 0, :], 0.0).then_inc(s_he, 1)
            dve.memset(UP[:, 1, :], 0.0).then_inc(s_he, 1)
            dve.wait_ge(s_he, 2)

            def hidden_low(i, e, j):
                dve.wait_ge(he_hi, i * 8 + (4 * e + j + 1))
                dve.tensor_tensor(HE_LO[:, e, j, :], HE[:, e, j, :], HE_HI[:, e, j, :].bitcast(F32),
                                  ALU.subtract).then_inc(he_lo, 1)

            def hidden(i, e, j):
                use = B0["moe"] + e * MOE_USES + 2 * j
                dve.wait_ge(unit_done, i * 24 + (U0["moe"] + e * MOE_UNITS + 2 * j + 2))
                dve.tensor_tensor(UP[:, j % 2, :], PG[:, (use + 1) % BANKS, 0:T],
                                  COMB[:, bass.ds(i * 2 + e, 1), :].rearrange("p o t -> p (o t)"),
                                  ALU.mult).then_inc(free_bank(use + 1), 1)
                wait_taken(dve, use + 1, i * 8)
                wait_taken(dve, use, i * 8)
                dve.tensor_tensor(HE[:, e, j, :], UP[:, j % 2, :], SG[:, j % 2, :], ALU.mult).then_inc(s_he, 1)

            def two_experts(i, first=False, last=False):
                for e in range(2):
                    u, use = U0["moe"] + e * MOE_UNITS, B0["moe"] + e * MOE_USES
                    for n in range(MOE_UNITS):
                        j, d = n // 2, n - 8
                        early = first and e == 0 and n < 4
                        if n < 8 and n % 2 == 1 and not early:
                            hidden(i, e, j)
                        if last and e == 1 and n + 2 >= MOE_UNITS:
                            if n + 2 == MOE_UNITS:
                                split_low(dve, U0["p2"])
                        else:
                            split_low(dve, u + n + 2, more=i * 24)
                        if n < 8 and n % 2 == 1 and not early:
                            hidden_low(i, e, j)
                        if early and n == 1:
                            router()
                        if early and n == 3:
                            dve.wait_ge(s_comb, NE)
                            for j in range(2):
                                hidden(i, 0, j)
                                hidden_low(i, 0, j)
                        if n >= 8:
                            dve.wait_ge(unit_done, i * 24 + (u + n + 1))
                            for half in range(2):
                                x = XT[:, 4 * d + 2 * half:4 * d + 2 * half + 2, :].rearrange("p a t -> p (a t)")
                                b = use + 8 + 2 * d + half
                                dve.tensor_tensor(x, x, PG[:, b % BANKS, :], ALU.add).then_inc(free_bank(b), 1)

            two_experts(0, first=True)
            with dve.Fori(1, NE // 2 - 1) as i:
                two_experts(i)
            two_experts(NE // 2 - 1, last=True)

            def s5_angles():
                v = lambda name: V[:, VEC[name][0]:VEC[name][1]]
                tt, ts = dve.tensor_tensor, dve.tensor_scalar
                dve.wait_ge(c_act, 1)
                tt(S_LR, v("lam_re"), S_DT, ALU.mult)
                link(tt(S_TH, v("lam_im"), S_DT, ALU.mult))
                link(ts(S_N, S_TH, float(np.float32(1 / (2 * np.pi))), 12582912.0, ALU.mult, ALU.add))
                link(ts(S_N, S_N, -12582912.0, None, ALU.add))
                src = S_TH
                for part in (6.28125, 0.0019350051879882812, 3.019915981956753e-07):
                    link(dve.scalar_tensor_tensor(S_R, S_N, -part, src, ALU.mult, ALU.add))
                    src = S_R
                ts(S_R, S_R, 3.1415925, -3.1415925, ALU.min, ALU.max).then_inc(c_dve, 1)
                dve.memset(CD, 0.0)
                dve.memset(BBD, 0.0).then_inc(c_zero, 1)

            def s5_factors():
                v = lambda name: V[:, VEC[name][0]:VEC[name][1]]
                tt, ts = dve.tensor_tensor, dve.tensor_scalar
                dve.wait_ge(c_act, 2)
                link(tt(S_COS, S_COS, S_COS, ALU.mult))
                link(ts(S_COS, S_COS, -2.0, 1.0, ALU.mult, ALU.add))
                tt(S_ABR, S_MAG, S_COS, ALU.mult)
                link(tt(S_ABI, S_MAG, S_SIN, ALU.mult))
                ts(S_ABR, S_ABR, -1.0, None, ALU.add)
                tt(S_A, v("lam_re"), v("lam_re"), ALU.mult)
                link(tt(S_B, v("lam_im"), v("lam_im"), ALU.mult))
                link(tt(S_DEN, S_A, S_B, ALU.add))
                dve.reciprocal(S_DEN, S_DEN)
                tt(S_A, S_ABR, v("lam_re"), ALU.mult)
                link(tt(S_B, S_ABI, v("lam_im"), ALU.mult))
                link(tt(S_KR, S_A, S_B, ALU.add))
                tt(S_A, S_ABI, v("lam_re"), ALU.mult)
                link(tt(S_B, S_ABR, v("lam_im"), ALU.mult))
                link(tt(S_KI, S_A, S_B, ALU.subtract))
                tt(S_KR, S_KR, S_DEN, ALU.mult)
                link(tt(S_KI, S_KI, S_DEN, ALU.mult))

            def s5_input_matrix():
                tt = dve.tensor_tensor
                dve.wait_ge(c_par, 32)
                dve.wait_ge(c_zero, 1)
                wide = lambda a: a.rearrange("p (i o) -> p i o", o=1).to_broadcast([P, S5_TILES, 16])
                a4 = lambda n: PB[:, n, :].rearrange("p (i n) -> p i n", i=S5_TILES)
                br, bi = S5B[:, 0, :, :], S5B[:, 1, :, :]
                tt(a4(0), br, wide(S_KR), ALU.mult)
                tt(a4(1), bi, wide(S_KI), ALU.mult)
                tt(a4(2), bi, wide(S_KR), ALU.mult)
                link(tt(a4(3), br, wide(S_KI), ALU.mult))
                for h in range(2):
                    hs, cs = slice(64 * h, 64 * h + 64), slice(16 * h, 16 * h + 16)
                    tt(BBD[hs, 0, :, cs], a4(0)[hs], a4(1)[hs], ALU.subtract)
                    ins = tt(BBD[hs, 1, :, cs], a4(2)[hs], a4(3)[hs], ALU.add)
                ins.then_inc(c_dve, 1)

            def s5_scan(b):
                tt = dve.tensor_tensor
                w = lambda a: a.rearrange("p (i t) -> p i t", i=4)
                bu = lambda c: PX[:, :, c * T:c * T + T]
                er, ei = w(ROT[:, b % 2, 0, :]), w(ROT[:, b % 2, 1, :])
                x0, x1, t0, t1 = w(XR[:, 0, :]), w(XR[:, 1, :]), w(TR[:, 0, :]), w(TR[:, 1, :])
                dve.wait_ge(c_bu, b + 1)
                dve.wait_ge(c_tab, b + 1)
                if b == 0:
                    dve.wait_ge(c_lb, 4)
                    dve.wait_ge(c_cd, 4)
                tt(x0, bu(0), er, ALU.mult)
                tt(t0, bu(1), ei, ALU.mult)
                tt(x1, bu(1), er, ALU.mult)
                link(tt(t1, bu(0), ei, ALU.mult))
                tt(x0, x0, t0, ALU.add)
                tt(x1, x1, t1, ALU.subtract).then_inc(c_x, 1)
                dve.wait_ge(c_x, b + 1)
                for i in range(4):
                    mag = S_MAG[:, 4 * b + i:4 * b + i + 1].to_broadcast([P, T])
                    for x in (x0, x1):
                        ins = dve.tensor_tensor_scan(x[:, i, :], mag, x[:, i, :], 0.0, ALU.mult, ALU.add)
                link(ins)
                tt(t0, x0, er, ALU.mult)
                link(tt(t1, x1, ei, ALU.mult))
                link(tt(t0, t0, t1, ALU.subtract))
                tt(t1, x0, ei, ALU.mult)
                link(tt(x1, x1, er, ALU.mult))
                tt(x1, x1, t1, ALU.add).then_inc(c_s, 1)
                if b == MT - 1:
                    for m in (0, 1):
                        split_low(dve, U0["p2"] + S5_END + m)
                dve.wait_ge(c_y, b + 1)
                dve.scalar_tensor_tensor(S5IN[:, b, :], S5IN[:, b, :], vec("s5_d", b), PX[:, 0, 0:T], ALU.mult,
                                         ALU.add).then_inc(c_yd, 1)

            norm(2, "norm1", low=lambda q: four_low(dve, P2_LO, HT, XT_r, q, X0["h1"] + q),
                 second=U0["p2"] + 1)
            for n in range(S5_FIRST - 2):
                split_low(dve, U0["p2"] + n + 2)
                if n == 1:
                    s5_angles()
                if n == 5:
                    s5_factors()
                if n == 9:
                    s5_input_matrix()
            for b in range(MT):
                s5_scan(b)

            dve.wait_ge(unit_done, U0["p2"] + S5_END)
            for q in range(4):
                c = slice(4 * q, 4 * q + 4)
                dve.tensor_tensor(HT_r[:, c, :], HT[:, c, :], XT_r[:, c, :].bitcast(F32),
                                  ALU.subtract).then_inc(late_lo, 1)
            for n in range(S5_END, 48):
                split_low(dve, U0["p2"] + n + 2)
            diag = lambda a: a.rearrange("p (b n) -> p b n", b=3)[:, 0:3:2, :]
            two = lambda a: a.rearrange("p (o n) -> p o n", o=1).to_broadcast([P, 2, P])

            def gate_event(g):
                if g == 1:
                    dve.wait_ge(g_sum, MT)
                    dve.tensor_scalar(RS[:, :], PX[:, 0, 0:T], 1.0 / MIX, 1e-6, ALU.mult,
                                      ALU.add).then_inc(g_ms, 1)
                    dve.wait_ge(g_rt, 1)
                    link(dve.reciprocal(RS[:, :], RS[:, :]))
                    for k in range(MT):
                        dve.scalar_tensor_tensor(UV[:, MT + k, :], UV[:, MT + k, :], vec("gm_norm", k), RS[:, :],
                                                 ALU.mult, ALU.mult).then_inc(g_vn, 1)
                if g == 2:
                    dve.wait_ge(g_in, 32)
                    dve.tensor_scalar(NEGM, con("up_strict"), -NEG, NEG, ALU.mult, ALU.add)
                    dve.tensor_tensor(SPAT, SPAT, con("up_incl").rearrange("p (o n) -> p o n", o=1)
                                      .to_broadcast([P, MT, P]), ALU.mult).then_inc(g_in, 1)
                    dve.wait_ge(g_in, 33)
                if g == 5:
                    dve.wait_ge(g_mix, 1)
                    for q in range(4):
                        u = UV[:, 2 * q:2 * q + 2, :].rearrange("p a t -> p (a t)")
                        dve.tensor_tensor(u, u, PX[:, q, :], ALU.mult).then_inc(g_y, 1)
                for h in range(MT):
                    z, l, sp, w = (a[:, h % 2, :] for a in (ZS, LN_, SP_, WW))
                    if g == HEAD_AT[h] + 1:
                        dve.wait_ge(b_l, h + 1)
                        link(dve.scalar_tensor_tensor(sp, z, 0.0, l, ALU.max, ALU.add))
                        dve.tensor_tensor(diag(sp), diag(sp), two(con("up_strict")), ALU.mult).then_inc(b_sp, 1)
                    if g == HEAD_AT[h] + 2:
                        dve.wait_ge(b_r, h + 1)
                        if h >= 2:
                            dve.wait_ge(b_pv, h - 1)
                        link(dve.tensor_tensor(w, z, PX[:, 1, 0:384], ALU.subtract))
                        dve.tensor_tensor(diag(w), diag(w), two(NEGM), ALU.add).then_inc(b_w, 1)
                    if g == HEAD_AT[h] + 4:
                        dve.wait_ge(b_pv, h + 1)
                        dve.tensor_copy(QKV[:, h, :], PX[:, 2, 0:T]).then_inc(b_y, 1)

            for g in range(48):
                split_low(dve, U0["p2"] + 48 + g + 2)
                gate_event(g)
                if g in (40, 41):
                    four_low(dve, YT_r[:, MT:KT, :], S5IN, S5_HI, g - 40, X0["s5"] + g - 40)
                if g in (42, 43):
                    four_low(dve, YA_LO, UV, YA_HI, g - 42, X0["ya"] + g - 42)
            for j in range(4):
                split_low(dve, U0["glu"] + j + 2)
                wait_taken(dve, B0["glu"] + j)
                dve.tensor_tensor(YB[:, 2 * j:2 * j + 2, :], S5IN[:, 2 * j:2 * j + 2, :],
                                  SQ[:, 2 * (j % 2):2 * (j % 2) + 2, :], ALU.mult).then_inc(s_yb, 1)
            dve.wait_ge(s_yb, 4)
            for n in range(3):
                for j in range(8):
                    use = B0["br"] + 8 * n + j
                    split_low(dve, U0["br"] + 8 * n + j + 2)
                    if n == 0 and j in (0, 1):
                        four_low(dve, YT_r, YT, YT_r[:, MT:KT, :], j, X0["yb"] + j)
                    if n == 0 and j in (3, 4):
                        four_low(dve, YC_LO, QKV, YC_HI, j - 3, X0["yc"] + j - 3)
                    m = HT[:, 2 * j:2 * j + 2, :].rearrange("p a t -> p (a t)")
                    gate = GT[:, n * KT + 2 * j:n * KT + 2 * j + 2, :].rearrange("p a t -> p (a t)")
                    dve.wait_ge(unit_done, U0["br"] + 8 * n + j + 1)
                    if n == 0:
                        dve.tensor_tensor(m, PG[:, use % BANKS, :], gate, ALU.mult).then_inc(free_bank(use), 1)
                    else:
                        link(dve.tensor_tensor(SQF[:, 0:2 * T], PG[:, use % BANKS, :], gate, ALU.mult))
                        dve.tensor_tensor(m, m, SQF[:, 0:2 * T], ALU.add).then_inc(free_bank(use), 1)
                        wait_taken(dve, use)
                    if n == 2 and j % 2 == 0 and j:
                        four_low(dve, HT_r, HT, M_HI, j // 2 - 1, X0["merged"] + j // 2 - 1)
            four_low(dve, HT_r, HT, M_HI, 3, X0["merged"] + 3)
            dve.wait_ge(s_back, 16)
            for t in range(KT):
                add_tile(U0["wo2"] + t, B0["wo2"] + t, t)
                if t < KT - 1:
                    split_low(dve, U0["wo2"] + t + 2)
            norm(3, "norm2", low=lambda q: four_low(dve, HT_r, HT, M_HI, q, X0["h2"] + q),
                 second=U0["mlp"] + 1)

            def hidden_low(i, t):
                dve.wait_ge(hid_hi, i * KT + (t + 1))
                dve.tensor_tensor(HID_LO[:, t, :], HID[:, t, :], HID_HI[:, t, :].bitcast(F32),
                                  ALU.subtract).then_inc(hid_lo, 1)

            def block_of_hidden(i, last=False):
                for n in range(2 * KT):
                    use = B0["mlp"] + n
                    if n < KT:
                        dve.wait_ge(s_relu, i * KT + (n + 1))
                        dve.scalar_tensor_tensor(HID[:, n, :], PG[:, use % BANKS, 0:T], 0.0, SQ[:, n % 2, :],
                                                 ALU.max, ALU.mult).then_inc(free_bank(use), 1)
                        wait_taken(dve, use, i * 8)
                    if n == KT:
                        hidden_low(i, n - 1)
                    if not (last and n + 2 >= 2 * KT):
                        split_low(dve, U0["mlp"] + n + 2, more=i * 32)
                    if 1 <= n < KT:
                        hidden_low(i, n - 1)
                    if n >= KT:
                        dve.wait_ge(unit_done, i * 32 + (U0["mlp"] + n + 1))
                        x = XT[:, n - KT, :]
                        dve.tensor_tensor(x, x, PG[:, use % BANKS, 0:T], ALU.add).then_inc(free_bank(use), 1)

            with dve.Fori(0, 3) as i:
                block_of_hidden(i)
            block_of_hidden(3, last=True)
            norm(4, "final", YT)

        @block.gpsimd
        def _(pool):
            def norm(n):
                for k in range(KT):
                    pool.wait_ge(s_sq, KT * n + k + 1)
                    if k == 0:
                        pool.tensor_copy(RS[:, :], SQ[:, 0, :]).then_inc(s_squsd, 1)
                    else:
                        pool.wait_ge(s_squsd, KT * n + k)
                        pool.tensor_tensor(RS[:, :], RS[:, :], SQ[:, k % 4, :], ALU.add).then_inc(s_squsd, 1)

            for r in range(25):
                pool.wait_ge(a_sq, 1) if r < 9 else pool.wait_ge(a_nrm, r - 8)
                if r >= 4:
                    pool.wait_ge(a_rope, r - 3)
                pool.tensor_tensor(ROPE_C[:, r % 4, :], DQ[:, r, :], con("cos64" if r < 9 else "cos128"),
                                   ALU.mult).then_inc(a_cos, 1)
            norm(1)
            norm(2)
            n_chain = [0]

            def link(ins):
                n_chain[0] += 1
                ins.then_inc(pool_chain, 1)
                pool.wait_ge(pool_chain, n_chain[0])

            tt = pool.tensor_tensor
            pool.wait_ge(c_dve, 2)
            ar, ai, sr, si, tmp = PW
            wide = lambda a, n: a.rearrange("p (i o) -> p i o", o=1).to_broadcast([P, S5_TILES, n])

            def square():
                tt(sr, ar, ar, ALU.mult)
                tt(si, ai, ai, ALU.mult)
                link(tt(tmp, ar, ai, ALU.mult))
                tt(ar, sr, si, ALU.subtract)
                link(tt(ai, tmp, tmp, ALU.add))

            link(pool.tensor_copy(ar, S_COS))
            link(pool.tensor_copy(ai, S_SIN))
            for f in range(2):
                re, im = POW[:, f, 0, :, :], POW[:, f, 1, :, :]
                pool.memset(re[:, :, 0:1], 1.0)
                link(pool.memset(im[:, :, 0:1], 0.0))
                pool.tensor_copy(re[:, :, 1:2], ar.rearrange("p (i o) -> p i o", o=1))
                link(pool.tensor_copy(im[:, :, 1:2], ai.rearrange("p (i o) -> p i o", o=1)))
                for m in (2, 4, 8):
                    square()
                    t0 = PT2[:, 0, 0:S5_TILES * m].rearrange("p (i n) -> p i n", i=S5_TILES)
                    t1 = PT2[:, 1, 0:S5_TILES * m].rearrange("p (i n) -> p i n", i=S5_TILES)
                    tt(t0, re[:, :, 0:m], wide(ar, m), ALU.mult)
                    link(tt(t1, im[:, :, 0:m], wide(ai, m), ALU.mult))
                    link(tt(re[:, :, m:2 * m], t0, t1, ALU.subtract))
                    tt(t0, re[:, :, 0:m], wide(ai, m), ALU.mult)
                    link(tt(t1, im[:, :, 0:m], wide(ar, m), ALU.mult))
                    link(tt(im[:, :, m:2 * m], t0, t1, ALU.add))
                square()
            for b in range(MT):
                if b:
                    pool.wait_ge(c_tab, b)
                for c in range(2):
                    for i in range(4):
                        i_ = 4 * b + i
                        J = lambda k: POW[:, 0, k, i_, :].rearrange("p (o n) -> p o n", o=1).to_broadcast([P, 16, 16])
                        F = lambda k: POW[:, 1, k, i_, :].rearrange("p (n o) -> p n o", o=1).to_broadcast([P, 16, 16])
                        o = lambda a: a[:, i * T:i * T + T].rearrange("p (c j) -> p c j", c=16)
                        if b >= 2 and c == 0 and i == 0:
                            pool.wait_ge(c_s, b - 1)
                        tt(o(ROT[:, b % 2, c, :]), J(0), F(c), ALU.mult)
                        ins = tt(o(PT2[:, 0, :]), J(1), F(1 - c), ALU.mult)
                    link(ins)
                    r = ROT[:, b % 2, c, :]
                    ins = tt(r, r, PT2[:, 0, :], ALU.subtract if c == 0 else ALU.add)
                    if c == 0:
                        link(ins)
                    else:
                        ins.then_inc(c_tab, 1)
            norm(3)
            norm(4)


DSA_COLS = (MIX, MIX, MIX, IDX_HEADS * 64, 64, IDX_HEADS)
RWKV_COLS = (MIX, 64, MIX, MIX, 64, 160)


def units(w, cols):
    k, n = w.shape
    return w.reshape(k // P, P, n // cols, cols).transpose(2, 1, 0, 3).reshape(n // cols, P, k // P * cols)


def by_feature(v):
    return v.reshape(-1, P).T


def lay_out(x):
    f = {k: np.asarray(v) for k, v in x.items()}
    w_in = f["w_in"][0]
    edges = np.cumsum((0,) + DSA_COLS + RWKV_COLS)
    q, k, v, qi, ki, wi, r, dw, kr, vr, da, dg = (w_in[:, a:b] for a, b in zip(edges[:-1], edges[1:]))
    pad = np.zeros((D, P - 48), np.float32)
    p1 = {"misc": np.concatenate([dw, da, dg[:, :P], dg[:, P:], wi, pad], 1), "r": r, "k": kr, "v": vr,
          "dsa": np.concatenate([ki, ki, qi, q, k, v], 1)}
    parts = [units(np.concatenate([p1[a][:, n * P:n * P + P] for a, n in P1_ORDER], 1), P), units(f["w_out"][0], P)]
    for e in range(NE):
        g, up, dn = f["w_e_gate"][0, e], f["w_e_up"][0, e], f["w_e_down"][0, e]
        parts.append(np.stack([units(g, P), units(up, P)], 1).reshape(8, P, UNIT))
        parts.append(units(dn, 4 * P))
    w2 = f["w_in_2"][0]
    parts.append(units(np.concatenate([w2[:, 2 * MIX:3 * MIX], w2[:, :2 * MIX], w2[:, 3 * MIX:]], 1), P))
    parts.append(units(f["s5_w_glu_2"][0], 2 * P))
    parts += [units(f["w_branch_2"][0, n], 2 * P) for n in range(3)]
    parts.append(units(f["w_out_2"][0], P))
    for b in range(4):
        parts.append(units(f["w_mlp_in_2"][0][:, b * D:(b + 1) * D], P))
        parts.append(units(f["w_mlp_out_2"][0][b * D:(b + 1) * D], P))
    weights = np.concatenate(parts, 0)
    assert weights.shape == (UNITS, P, UNIT), weights.shape

    mu = f["rwkv_shift_mix"][0]
    e2 = np.cumsum((0,) + RWKV_COLS)
    mr, mdw, mk, mv, mda, mdg = (mu[a:b] for a, b in zip(e2[:-1], e2[1:]))
    mu_cols = np.concatenate([mdw, mda, mdg, np.zeros(P - 32, np.float32), mr, mk, mv])
    states = lambda a: a.reshape(S5_TILES, P).T
    vectors = {"g_mix": f["g_mix"], "mu": mu_cols, "w0": f["w0"], "a0": f["a0"], "k_k": f["k_k"], "k_a": f["k_a"],
               "r_k": f["r_k"], "ln_w": f["ln_x_w"], "ln_b": f["ln_x_b"], "q_gain": f["q_gain"],
               "k_gain": f["k_gain"], "g_ffn": f["g_ffn"], "norm1": f["norm1_g_2"], "b_gate": f["b_gate_2"],
               "gm_norm": f["gm_norm_g_2"], "s5_d": f["s5_d_2"], "b_glu": f["s5_b_glu_2"], "norm2": f["norm2_g_2"],
               "final": f["final_g_2"], "lam_re": f["s5_lambda_re_2"], "lam_im": f["s5_lambda_im_2"],
               "log_dt": np.repeat(f["s5_log_dt_2"].reshape(-1), 64)}
    V = np.zeros((P, NV), np.float32)
    for name, a in vectors.items():
        V[:, VEC[name][0]:VEC[name][1]] = by_feature(a.reshape(-1))
    V[:, VEC["b_route"][0]:VEC["b_route"][1]] = np.concatenate([f["b_route_group"][0], f["b_route_expert"][0]])[None]

    gate_up = np.zeros((P, 2, MIX), np.float32)
    gate_up[:, 0] = f["w_gate_lora_up"][0, :P]
    gate_up[:32, 1] = f["w_gate_lora_up"][0, P:]
    state_rows = lambda a: a.reshape(S5_TILES, P, 16).transpose(1, 0, 2)
    route = np.concatenate([f["w_route_group"][0], f["w_route_expert"][0]], 1)
    return {
        "xT": f["x"][0].T.reshape(KT, P, T).transpose(1, 0, 2),
        "weights": weights, "vectors": V, "constants": constants(),
        "lora": np.concatenate([f["w_decay_up"][0], f["w_aicl_up"][0]], 0),
        "gate_up": gate_up.reshape(P, 2 * MIX),
        "route": route.reshape(KT, P, 20).transpose(1, 0, 2).reshape(P, KT * 20),
        "spatial": f["gm_w_s_2"][0].transpose(2, 0, 1).reshape(P, MT * P),
        "spatial_b": f["gm_b_s_2"][0].reshape(1, MT * P),
        "s5_b": np.stack([state_rows(f["s5_b_re_2"][0]), state_rows(f["s5_b_im_2"][0])], 1).reshape(P, -1),
        "s5_c": np.stack([state_rows(f["s5_c_re_2"][0].transpose(0, 2, 1)),
                          state_rows(f["s5_c_im_2"][0].transpose(0, 2, 1))], 1).reshape(P, -1),
    }


def kernel(**inputs):
    import concourse.bacc as bacc
    from concourse.bass_utils import run_bass_kernel_spmd as run

    nc = bacc.Bacc("TRN2", target_bir_lowering=False, num_devices=1)
    arrays = {k: np.ascontiguousarray(v) for k, v in lay_out(inputs).items()}
    A = {k: nc.dram_tensor(k, v.shape, F32, kind="ExternalInput").ap() for k, v in arrays.items()}
    out = nc.dram_tensor("result", (P, KT, T), F32, kind="ExternalOutput").ap()
    build(nc, A, out)
    r = run(nc, [arrays], core_ids=[0])
    return r.results[0]["result"].transpose(1, 0, 2).reshape(D, T).T.reshape(1, T, D)
```
